# Optimizing a Trainium2 kernel written in Bass

```python
import math
import jax
import jax.numpy as jnp
from jax import lax
import numpy as np

D_MODEL = 2048
BATCH = 1
SEQ = 256
DEPTH = 2

SB_WIDTH = D_MODEL // 2
SB_HEAD_DIM = 128
SB_HEADS = SB_WIDTH // SB_HEAD_DIM
QBLOCK = 128
RW_WIDTH = D_MODEL - SB_WIDTH
RW_HEAD_DIM = 64
RW_HEADS = RW_WIDTH // RW_HEAD_DIM
RW_DECAY_LORA = 64
RW_A_LORA = 64
RW_V_LORA = 32
RW_GATE_LORA = 160
RW_LNX_EPS = 64e-5
RW_KK_EPS = 1e-12
GDN_K_HEADS = 16
GDN_V_HEADS = 32
GDN_HEAD_DIM = 128
GDN_KEY_WIDTH = GDN_K_HEADS * GDN_HEAD_DIM
GDN_VAL_WIDTH = GDN_V_HEADS * GDN_HEAD_DIM
GDN_CONV_CH = 2 * GDN_KEY_WIDTH + GDN_VAL_WIDTH
GDN_CONV = 4
GDN_CHUNK = 64
GDN_NORM_EPS = 1e-6
GDN_QK_EPS = 1e-6
D_FF = 4 * D_MODEL
DN_ALPHA = (2 * DEPTH) ** 0.25
DN_BETA = (8 * DEPTH) ** -0.25
LN_EPS = 1e-5
N_EVEN = (DEPTH + 1) // 2
N_ODD = DEPTH // 2
EV_A_COLS = 3 * SB_WIDTH
EV_B_COLS = 3 * RW_WIDTH + RW_DECAY_LORA + RW_A_LORA + RW_GATE_LORA
EV_IN = EV_A_COLS + EV_B_COLS
OD_IN = GDN_CONV_CH + GDN_VAL_WIDTH + 2 * GDN_V_HEADS

kernel_name = 'hybrid_sb_rwkv7_gdn_deepnorm_trunk'

def split_cols(x, sizes):
    return jnp.split(x, [int(i) for i in np.cumsum(sizes)[:-1]], axis=-1)

def to_heads(t, head_dim):
    return t.reshape(t.shape[:-1] + (t.shape[-1] // head_dim, head_dim))

def layer_norm(x, g, b):
    xf = x.astype(jnp.float32)
    mu = jnp.mean(xf, axis=-1, keepdims=True)
    var = jnp.mean(jnp.square(xf - mu), axis=-1, keepdims=True)
    return ((xf - mu) * lax.rsqrt(var + LN_EPS) * g + b).astype(x.dtype)

def l2_normalize(x, eps):
    return x * lax.rsqrt(jnp.sum(x * x, axis=-1, keepdims=True) + eps)

def token_shift(p):
    return jnp.pad(p, ((0, 0), (1, 0), (0, 0)))[:, :-1]

def causal_dwconv(x, w):
    return lax.conv_general_dilated(
        x, w[:, None, :].astype(x.dtype), window_strides=(1,),
        padding=[(w.shape[0] - 1, 0)], dimension_numbers=('NWC', 'WIO', 'NWC'),
        feature_group_count=x.shape[-1])

def stick_breaking_attention(q, k, v):
    bsz, t_len, h, d = q.shape
    nb = t_len // QBLOCK
    qb = q.astype(jnp.float32).reshape(bsz, nb, QBLOCK, h, d).transpose(1, 0, 3, 2, 4)
    kf = k.astype(jnp.float32).transpose(0, 2, 1, 3)
    vf = v.astype(jnp.float32).transpose(0, 2, 1, 3)
    key_pos = jnp.arange(t_len)

    def one_block(args):
        q_blk, start = args
        z = jnp.einsum('bhqd,bhsd->bhqs', q_blk, kf) * (d ** -0.5)
        mask = key_pos[None, :] < (start + jnp.arange(QBLOCK))[:, None]
        log_keep = jnp.where(mask, jax.nn.log_sigmoid(-z), 0.0)
        log_a = z + lax.cumsum(log_keep, axis=3, reverse=True)
        a = jnp.exp(jnp.where(mask, log_a, -jnp.inf))
        return jnp.einsum('bhqs,bhsd->bhqd', a, vf)

    o = lax.map(one_block, (qb, jnp.arange(nb) * QBLOCK))
    return o.transpose(1, 0, 3, 2, 4).reshape(bsz, t_len, h * d)

def rwkv7_scan(r, decay, k, v, kk, a):
    bsz, _, h, n = r.shape

    def step(S, inp):
        r_t, w_t, k_t, v_t, kk_t, a_t = inp
        s_kk = jnp.einsum('bhij,bhj->bhi', S, kk_t)
        S = (S * w_t[:, :, None, :] - s_kk[..., None] * (kk_t * a_t)[:, :, None, :]
             + v_t[..., None] * k_t[:, :, None, :])
        return S, jnp.einsum('bhij,bhj->bhi', S, r_t)

    xs = tuple(jnp.moveaxis(t, 1, 0) for t in (r, decay, k, v, kk, a))
    _, y = lax.scan(step, jnp.zeros((bsz, h, n, n), jnp.float32), xs)
    return jnp.moveaxis(y, 0, 1)

def rwkv7_group(pb, mu, w0, w_up, a0, a_up, g_up, k_k, k_a, r_k, lnx_g, lnx_b,
                v_first, v0, v_up):
    pf = pb.astype(jnp.float32)
    xs = pf + (token_shift(pf) - pf) * mu
    sizes = [RW_WIDTH] * 3 + [RW_DECAY_LORA, RW_A_LORA, RW_GATE_LORA]
    if v_first is not None:
        sizes = sizes + [RW_V_LORA]
    parts = split_cols(xs, sizes)
    r, k, v, w_lo, a_lo, g_lo = parts[:6]
    if v_first is None:
        v_first = v
    else:
        v = v + (v_first - v) * jax.nn.sigmoid(v0 + parts[6] @ v_up)
    w_log = -jax.nn.softplus(-(w0 + jnp.tanh(w_lo) @ w_up)) - 0.5
    decay = jnp.exp(-jnp.exp(w_log))
    a = jax.nn.sigmoid(a0 + a_lo @ a_up)
    g = jax.nn.sigmoid(g_lo) @ g_up
    kk = l2_normalize(to_heads(k * k_k, RW_HEAD_DIM), RW_KK_EPS)
    k = k * (1.0 + (a - 1.0) * k_a)
    rh, kh, vh = (to_heads(t, RW_HEAD_DIM) for t in (r, k, v))
    y = rwkv7_scan(rh, to_heads(decay, RW_HEAD_DIM), kh, vh, kk, to_heads(a, RW_HEAD_DIM))
    mu_y = jnp.mean(y, axis=-1, keepdims=True)
    var_y = jnp.mean(jnp.square(y - mu_y), axis=-1, keepdims=True)
    y = ((y - mu_y) * lax.rsqrt(var_y + RW_LNX_EPS)).reshape(pb.shape[:2] + (RW_WIDTH,))
    y = y * lnx_g + lnx_b
    bonus = jnp.sum(rh * kh * r_k, axis=-1, keepdims=True) * vh
    return (y + bonus.reshape(y.shape)) * g, v_first

def gated_delta_rule_chunked(q, k, v, g, beta):
    bsz, t_len, h, dk = q.shape
    dv = v.shape[-1]
    n_chunks = t_len // GDN_CHUNK

    def to_chunks(t):
        t = t.reshape((bsz, n_chunks, GDN_CHUNK, h) + t.shape[3:])
        return jnp.moveaxis(t, 3, 1)

    q, k, v, g, beta = (to_chunks(t) for t in (q, k, v, g, beta))
    gc = jnp.cumsum(g, axis=-1)
    pos = jnp.arange(GDN_CHUNK)
    lower = pos[:, None] >= pos[None, :]
    strict = pos[:, None] > pos[None, :]
    decay = jnp.exp(jnp.where(lower, gc[..., :, None] - gc[..., None, :], -jnp.inf))
    k_beta = k * beta[..., None]
    kkt = jnp.einsum('bhncd,bhnsd->bhncs', k_beta, k) * decay
    tri = jnp.where(strict, kkt, 0.0) + jnp.eye(GDN_CHUNK, dtype=kkt.dtype)
    rhs = jnp.concatenate([v * beta[..., None], k_beta * jnp.exp(gc)[..., None]], axis=-1)
    sol = lax.linalg.triangular_solve(tri, rhs, left_side=True, lower=True, unit_diagonal=True)
    u, w = sol[..., :dv], sol[..., dv:]
    attn = jnp.where(lower, jnp.einsum('bhncd,bhnsd->bhncs', q, k) * decay, 0.0)

    def step(S, inp):
        q_c, k_c, u_c, w_c, gc_c, attn_c = inp
        v_new = u_c - jnp.einsum('bhcd,bhde->bhce', w_c, S)
        o_c = (jnp.einsum('bhcd,bhde->bhce', q_c * jnp.exp(gc_c)[..., None], S)
               + jnp.einsum('bhcs,bhse->bhce', attn_c, v_new))
        g_last = gc_c[..., -1:]
        S = S * jnp.exp(g_last)[..., None] + jnp.einsum(
            'bhcd,bhce->bhde', k_c * jnp.exp(g_last - gc_c)[..., None], v_new)
        return S, o_c

    xs = tuple(jnp.moveaxis(t, 2, 0) for t in (q, k, u, w, gc, attn))
    _, o = lax.scan(step, jnp.zeros((bsz, h, dk, dv), jnp.float32), xs)
    return o.transpose(1, 0, 3, 2, 4).reshape(bsz, t_len, h, dv)

def gated_deltanet(p, conv_w, a_log, dt_bias, norm_w):
    bsz, t_len, _ = p.shape
    qkv, z, b, a = split_cols(p, [GDN_CONV_CH, GDN_VAL_WIDTH, GDN_V_HEADS, GDN_V_HEADS])
    qkv = jax.nn.silu(causal_dwconv(qkv, conv_w)).astype(jnp.float32)
    q, k, v = split_cols(qkv, [GDN_KEY_WIDTH, GDN_KEY_WIDTH, GDN_VAL_WIDTH])
    rep = GDN_V_HEADS // GDN_K_HEADS
    q = jnp.repeat(l2_normalize(to_heads(q, GDN_HEAD_DIM), GDN_QK_EPS), rep, axis=2) * (GDN_HEAD_DIM ** -0.5)
    k = jnp.repeat(l2_normalize(to_heads(k, GDN_HEAD_DIM), GDN_QK_EPS), rep, axis=2)
    v = to_heads(v, GDN_HEAD_DIM)
    beta = jax.nn.sigmoid(b.astype(jnp.float32))
    g = -jnp.exp(a_log.astype(jnp.float32)) * jax.nn.softplus(a.astype(jnp.float32) + dt_bias)
    o = gated_delta_rule_chunked(q, k, v, g, beta)
    o = o * lax.rsqrt(jnp.mean(o * o, axis=-1, keepdims=True) + GDN_NORM_EPS) * norm_w
    o = o * jax.nn.silu(to_heads(z.astype(jnp.float32), GDN_HEAD_DIM))
    return o.reshape(bsz, t_len, GDN_VAL_WIDTH)

def sq_relu_mlp(x, w1, w2):
    return jnp.square(jax.nn.relu(x @ w1)) @ w2

def setup_inputs(seed: int = 0) -> dict:
    key = jax.random.key(seed)
    keys = iter(jax.random.split(key, 40))
    f32 = jnp.float32

    def normal(shape, scale):
        return jax.random.normal(next(keys), shape, f32) * scale

    def uniform(shape, lo, hi):
        return jax.random.uniform(next(keys), shape, f32, lo, hi)

    E, O, L = N_EVEN, N_ODD, DEPTH
    EV = max(N_EVEN - 1, 0)
    dt = jnp.exp(uniform((O, GDN_V_HEADS), math.log(1e-3), math.log(1e-1)))
    return {
        'x': normal((BATCH, SEQ, D_MODEL), 1.0),
        'ev_w_in': normal((E, D_MODEL, EV_IN), D_MODEL ** -0.5),
        'ev_shift': uniform((E, EV_B_COLS), 0.0, 1.0),
        'ev_w0': uniform((E, RW_WIDTH), -6.5, -1.5),
        'ev_w_up': normal((E, RW_DECAY_LORA, RW_WIDTH), RW_DECAY_LORA ** -0.5),
        'ev_a0': normal((E, RW_WIDTH), 0.1),
        'ev_a_up': normal((E, RW_A_LORA, RW_WIDTH), RW_A_LORA ** -0.5),
        'ev_g_up': normal((E, RW_GATE_LORA, RW_WIDTH), RW_GATE_LORA ** -0.5),
        'ev_k_k': 0.85 + normal((E, RW_WIDTH), 0.02),
        'ev_k_a': 1.0 + normal((E, RW_WIDTH), 0.02),
        'ev_r_k': normal((E, RW_HEADS, RW_HEAD_DIM), 0.1),
        'ev_lnx_g': 1.0 + normal((E, RW_WIDTH), 0.02),
        'ev_lnx_b': normal((E, RW_WIDTH), 0.02),
        'vres_w_down': normal((EV, D_MODEL, RW_V_LORA), D_MODEL ** -0.5),
        'vres_shift': uniform((EV, RW_V_LORA), 0.0, 1.0),
        'vres_v0': 1.0 + normal((EV, RW_WIDTH), 0.1),
        'vres_v_up': normal((EV, RW_V_LORA, RW_WIDTH), RW_V_LORA ** -0.5),
        'ev_w_out': normal((E, SB_WIDTH + RW_WIDTH, D_MODEL), (SB_WIDTH + RW_WIDTH) ** -0.5 * DN_BETA),
        'od_w_in': normal((O, D_MODEL, OD_IN), D_MODEL ** -0.5),
        'od_conv': normal((O, GDN_CONV, GDN_CONV_CH), GDN_CONV ** -0.5),
        'od_a_log': jnp.log(uniform((O, GDN_V_HEADS), 1.0, 16.0)),
        'od_dt_bias': dt + jnp.log(-jnp.expm1(-dt)),
        'od_norm_w': 1.0 + normal((O, GDN_HEAD_DIM), 0.02),
        'od_w_out': normal((O, GDN_VAL_WIDTH, D_MODEL), GDN_VAL_WIDTH ** -0.5 * DN_BETA),
        'ln1_g': 1.0 + normal((L, D_MODEL), 0.02),
        'ln1_b': normal((L, D_MODEL), 0.02),
        'mlp_w1': normal((L, D_MODEL, D_FF), D_MODEL ** -0.5),
        'mlp_w2': normal((L, D_FF, D_MODEL), D_FF ** -0.5 * DN_BETA),
        'ln2_g': 1.0 + normal((L, D_MODEL), 0.02),
        'ln2_b': normal((L, D_MODEL), 0.02),
    }

def reference(x, ev_w_in, ev_shift, ev_w0, ev_w_up, ev_a0, ev_a_up, ev_g_up, ev_k_k,
              ev_k_a, ev_r_k, ev_lnx_g, ev_lnx_b, vres_w_down, vres_shift, vres_v0,
              vres_v_up, ev_w_out, od_w_in, od_conv, od_a_log, od_dt_bias, od_norm_w,
              od_w_out, ln1_g, ln1_b, mlp_w1, mlp_w2, ln2_g, ln2_b):
    v_first = None
    for layer in range(DEPTH):
        if layer % 2 == 0:
            e = layer // 2
            if e == 0:
                w_in, mu, v0, v_up = ev_w_in[0], ev_shift[0], None, None
            else:
                w_in = jnp.concatenate([ev_w_in[e], vres_w_down[e - 1]], axis=1)
                mu = jnp.concatenate([ev_shift[e], vres_shift[e - 1]])
                v0, v_up = vres_v0[e - 1], vres_v_up[e - 1]
            p = x @ w_in
            sb_q, sb_k, sb_v = split_cols(p[..., :EV_A_COLS], [SB_WIDTH] * 3)
            o_sb = stick_breaking_attention(to_heads(sb_q, SB_HEAD_DIM),
                                            to_heads(sb_k, SB_HEAD_DIM),
                                            to_heads(sb_v, SB_HEAD_DIM))
            o_rw, v_first = rwkv7_group(p[..., EV_A_COLS:], mu, ev_w0[e], ev_w_up[e], ev_a0[e],
                                        ev_a_up[e], ev_g_up[e], ev_k_k[e], ev_k_a[e], ev_r_k[e],
                                        ev_lnx_g[e], ev_lnx_b[e], v_first, v0, v_up)
            h = jnp.concatenate([o_sb, o_rw], axis=-1).astype(x.dtype) @ ev_w_out[e]
        else:
            o = layer // 2
            h = gated_deltanet(x @ od_w_in[o], od_conv[o], od_a_log[o], od_dt_bias[o],
                               od_norm_w[o]).astype(x.dtype) @ od_w_out[o]
        x = layer_norm(DN_ALPHA * x + h.astype(x.dtype), ln1_g[layer], ln1_b[layer])
        x = layer_norm(DN_ALPHA * x + sq_relu_mlp(x, mlp_w1[layer], mlp_w2[layer]).astype(x.dtype),
                       ln2_g[layer], ln2_b[layer])
    return x


_drawn_inputs = setup_inputs


def setup_inputs(seed=0):
    import zlib

    import numpy as np

    out = dict(_drawn_inputs(seed))
    spreads = {}
    factors = {'ev_w_up': 8.0,
     'ev_a0': 8.0,
     'ev_k_k': 8.0,
     'ev_k_a': 8.0,
     'ev_lnx_g': 8.0,
     'ev_lnx_b': 8.0,
     'od_norm_w': 8.0}
    for name, (base, spread) in spreads.items():
        noise = np.random.default_rng([zlib.crc32(name.encode()), seed]).standard_normal(out[name].shape)
        drawn = base * np.exp(spread * noise) if base else spread * noise
        out[name] = jnp.asarray(drawn.astype(out[name].dtype))
    for name, factor in factors.items():
        out[name] = (out[name] * factor).astype(out[name].dtype)
    return out
```

```python
from contextlib import ExitStack

import concourse.bass as bass
from concourse import mybir

F32 = mybir.dt.float32
F32R = mybir.dt.float32r
ALU = mybir.AluOpType
ACT = mybir.ActivationFunctionType

P = 128
D = 2048
T = 256
KT = D // P
TT = T // P
UK = 2
UNITS = KT // UK
RING = 4
WIDE = 512
NARROW = 384
GROUPS = 8
FF = 4 * D
FG = FF // D
ALPHA = 4.0 ** 0.25
LN_EPS = 1e-5
LNX_EPS = 64e-5
KK_EPS = 1e-12
SB_SCALE = 128.0 ** -0.5
LEAD = 2

P_GROUPS0 = 1
P_OUT0 = P_GROUPS0 + 2 * GROUPS
P_MLP0 = P_OUT0 + 4
P_L1 = P_MLP0 + 8 * FG
HALF1 = 4 * 3 + 4
P_MLP1 = P_L1 + 2 * HALF1
PANELS = P_MLP1 + 8 * FG

C_ID, C_ONES, C_LV, C_M0 = 0, 128, 256, 640
C_SHARED = 768
C0_SB, C0_BIG, C0_TRI, C0_BO, C0_BO64, C0_RW, C0_RST = 0, 384, 768, 896, 1024, 1152, 1408
C0_N = 1664
C1_GM, C1_SL = 0, 256
C1_N = 384
WS = 53215 - 36864 - C_SHARED - 32


class Steps:

    def __init__(self, eng, sem):
        self.eng, self.sem, self.total, self.n, self.base, self.per = eng, sem, 0, 0, 0, None

    def enter(self, i, per):
        self.base, self.per, self.n = i * per + self.total, per, 0

    def __call__(self, ins):
        self.n += 1
        return ins.then_inc(self.sem, 1)

    def settle(self):
        self.eng.wait_ge(self.sem, self.base + self.n)

    def leave(self, times):
        assert self.n == self.per, f"the body has {self.n} steps, {self.per} declared"
        self.total += times * self.per
        self.base, self.n, self.per = self.total, 0, None

    def leave_straight(self):
        self.total += self.n
        self.base, self.n = self.total, 0


class Lay:

    def __init__(self, ws, at=0):
        self.ws, self.at = ws, at

    def __call__(self, n):
        self.at += n
        assert self.at <= WS, self.at
        return self.ws[:, self.at - n:self.at]


def trunk(nc, stop, x, w384, w512, wba, consts, c0, c1, prm0, lora, conv, rows1, normw, ln, out):
    ctx = ExitStack()
    with ctx:
        def sb(name, shape, dt=F32):
            return ctx.enter_context(nc.sbuf_tensor(name, shape, dt))

        sems = {}

        def S(name):
            if name not in sems:
                sems[name] = ctx.enter_context(nc.semaphore(name))
            return sems[name]

        raw = sb("raw", [P, UNITS, UK, WIDE])
        wh = sb("wh", [P, RING, UK, WIDE], F32R)
        wl = sb("wl", [P, RING, UK, WIDE], F32R)
        xres = sb("xres", [P, TT, D])
        aTh = sb("aTh", [P, KT, T], F32R)
        aTl = sb("aTl", [P, KT, T], F32R)
        hTh = sb("hTh", [P, KT, T], F32R)
        hTl = sb("hTl", [P, KT, T], F32R)
        cc = sb("cc", [P, C_SHARED])
        ws = sb("ws", [P, WS])
        small = sb("small", [P, 16])
        pp = [ctx.enter_context(nc.psum_tensor(f"pp{b}", [P, 2 * WIDE], F32)) for b in range(2)]
        mb = [ctx.enter_context(nc.psum_tensor(f"mb{b}", [P, WIDE], F32)) for b in range(4)]

        ident = cc[:, C_ID:C_ID + P]
        ones = cc[:, C_ONES:C_ONES + P]
        eps_ln, eps_lnx, eps_kk, eps_l2, ln_qs = (small[:, j:j + 1] for j in range(5))
        mv = small[:, 8:12].rearrange("p (t s) -> p t s", t=TT)
        rstd = small[:, 12:14]

        def r2(ap, **kw):
            return ap.rearrange("p (a b) -> p a b", **kw)

        lay = Lay(ws)
        lng = lay(D)
        lnb = lay(D)
        stats = lay(TT * 4 * 6).rearrange("p (t c s) -> p t c s", t=TT, c=4)
        hid = lay(2 * WIDE)
        wba_sb = r2(Lay(ws, 2 * D + 64 + 1024)(KT * 64), a=KT)

        lay = Lay(ws)
        k0 = lay(C0_N)
        sbneg, sbbig = k0[:, C0_SB:C0_SB + 384], k0[:, C0_BIG:C0_BIG + 384]
        tri, bo, bo64 = (k0[:, c:c + P] for c in (C0_TRI, C0_BO, C0_BO64))
        rwmask, rst = k0[:, C0_RW:C0_RW + 256], k0[:, C0_RST:C0_RST + 256]
        pb = r2(lay(3 * (T + 1)), a=3)
        sbq = r2(lay(3 * T), a=3)
        rkv = r2(lay(3 * T), a=3)
        loT = r2(lay(3 * T), a=3)
        lw = r2(lay(3 * P), a=3)
        prmf = lay(GROUPS * 10 + 3)
        prm = r2(prmf[:, 0:GROUPS * 10], a=GROUPS)
        mulo = prmf[:, GROUPS * 10:GROUPS * 10 + 3]
        nprm = r2(lay(GROUPS * 2), a=GROUPS)
        ew = lay(2 * T)
        sigw, av = ew[:, 0:T], ew[:, T:2 * T]
        Lg, cum = lay(T), lay(T)
        p3 = lay(3 * T)
        pinc, pinv, pexc = (p3[:, j * T:(j + 1) * T] for j in range(3))
        yT, yc, yn = pinv, pexc, Lg
        kk0, k2 = lay(T), lay(T)
        KR = lay(2 * T).rearrange("p (t w c) -> p t w c", t=TT, w=2)
        bt, kt_, gg, rk = lay(T), lay(T), lay(T), lay(T)
        tok = lay(3 * T).rearrange("p (w t c) -> p w t c", w=3, t=TT)
        GMf = lay(2048)
        GM = GMf.rearrange("p (t h w r c) -> p t h w r c", t=TT, h=2, w=2, r=2)
        dsh = r2(GMf[:, 0:3 * T], a=3)
        lobuf = r2(GMf[:, 3 * T:3 * T + 3 * (T + 1)], a=3)
        ksq = GMf[:, 3 * T:4 * T]
        kkt = GMf[:, 4 * T:5 * T]
        X0 = r2(lay(4 * P), a=4)
        XT0 = r2(lay(4 * P), a=4)
        Yn0 = r2(lay(4 * 64), a=4)
        S0, dS0, Rn, U = (lay(P) for _ in range(4))
        vtk = r2(lay(T), a=TT)
        sba, sbb, sbc = (lay(384) for _ in range(3))

        lay = Lay(ws)
        k1 = lay(C1_N)
        gmask, SL = k1[:, C1_GM:C1_GM + 256], k1[:, C1_SL:C1_SL + P]
        UT = gmask[:, 0:P]
        cbuf = r2(lay(8 * (T + 3)), a=8)
        zs = r2(lay(4 * T), a=4)
        qkv = r2(lay(8 * T), a=8)
        Ef = lay(2048)
        E1 = r2(Ef, a=8)
        AT = Ef[:, 0:1024].rearrange("p (c h t) -> p c h t", c=TT, h=4)
        At = Ef[:, 1024:2048].rearrange("p (c h t) -> p c h t", c=TT, h=4)
        Df = lay(1024)
        SQ = r2(Df, a=4)
        Dm = Df.rearrange("p (c h t) -> p c h t", c=TT, h=4)
        KQf = lay(1024)
        KQ = KQf.rearrange("p (c j w t) -> p c j w t", c=TT, j=2, w=2)
        Xf = lay(1024)
        X1 = r2(Xf, a=8)
        UTg = Xf.rearrange("p (c h t) -> p c h t", c=TT, h=4)
        XT1 = r2(lay(1024), a=8)
        ktok = lay(512).rearrange("p (c j t) -> p c j t", c=TT, j=2)
        vs = lay(1024).rearrange("p (c h t) -> p c h t", c=TT, h=4)
        Yn1 = r2(lay(512), a=8)
        oT1 = r2(Yn1.rearrange("p a b -> p (a b)"), a=4)
        S1 = r2(lay(512), a=4)
        yp = r2(Df[:, 0:512], a=4)
        vk = r2(Df[:, 512:1024], a=4)
        vke = r2(KQf[:, 0:512], a=4)
        t2 = r2(KQf[:, 512:1024], a=4)
        gates = lay(7 * 64).rearrange("p (s c h) -> p s c h", s=7, c=TT)
        beta, gv, negc, egc, kend, egl, gtmp = (gates[:, s] for s in range(7))
        colk = lay(48)
        ssc = colk[:, 0:8].rearrange("p (c j) -> p c j", c=TT)
        lnss = colk[:, 8:16].rearrange("p (c j) -> p c j", c=TT)
        qsc = colk[:, 16:20].rearrange("p (c j) -> p c j", c=TT)
        skc = colk[:, 20:24].rearrange("p (c j) -> p c j", c=TT)
        wkc = colk[:, 24:28].rearrange("p (c j) -> p c j", c=TT)
        wc = colk[:, 28:36].rearrange("p (c h) -> p c h", c=TT)
        wke = lay(8).rearrange("p (c h) -> p c h", c=TT)
        oss = colk[:, 36:40]
        osc = colk[:, 40:44]
        osq = lay(4)
        cw = r2(lay(GROUPS * 32), a=GROUPS)
        r1 = lay(64)
        nw = lay(1)
        sqj = lay(P)

        block = ctx.enter_context(nc.Block())

        @block.sync
        def _(sp):
            sp.dma_start(xres[:, :, :], x.rearrange("(t p) d -> p t d", p=P)).then_inc(S("x_in"), 16)
            sp.dma_start(cc[:, :], consts).then_inc(S("consts_in"), 16)
            sp.dma_start(k0, c0).then_inc(S("c0_in"), 16)
            sp.dma_start(prmf, prm0).then_inc(S("prm_in"), 16)

            def load(n, src, width):
                for q in range(UNITS):
                    sp.wait_ge(S("lo_ready"), n * UNITS + (q + 1))
                    sp.dma_start(raw[:, q, :, 0:width], src[:, q * UK:(q + 1) * UK, :]).then_inc(S(f"landed{q}"), 16)

            with sp.Fori(0, P_OUT0) as i:
                load(i, w384[bass.ds(i, 1)].rearrange("a p k c -> p (a k) c"), NARROW)
            if stop != 1:
                with sp.Fori(0, PANELS - P_OUT0) as i:
                    load(i + P_OUT0, w512[bass.ds(i, 1)].rearrange("a p k c -> p (a k) c"), WIDE)
            else:
                with sp.Fori(0, 4) as i:
                    load(i + P_OUT0, w512[bass.ds(i, 1)].rearrange("a p k c -> p (a k) c"), WIDE)
            sp.wait_ge(S("ln_done"), 1)
            sp.dma_start(out.rearrange("(t p) d -> p t d", p=P), xres[:, :, :]).then_inc(S("stored"), 16)
            sp.wait_ge(S("stored"), 16)

        @block.gpsimd
        def _(pool):
            def scale_residual(k):
                pool.wait_ge(S("x_transposed"), k)
                nc.gpsimd.tensor_scalar(xres[:, :, :], xres[:, :, :], ALPHA, None, ALU.mult).then_inc(S("x_scaled"), 1)

            def load_ln(k):
                pool.wait_ge(S("ws_free"), k + 1)
                pool.dma_start(lng, ln[2 * k:2 * k + 1, :].partition_broadcast(P)).then_inc(S("ln_in"), 16)
                pool.dma_start(lnb, ln[2 * k + 1:2 * k + 2, :].partition_broadcast(P)).then_inc(S("ln_in"), 16)

            scale_residual(1)
            with pool.Fori(0, GROUPS) as i:
                pool.wait_ge(S("lora_used"), i + 1)
                pool.dma_start(lw, lora[bass.ds(i, 1)].rearrange("a p (w c) -> p (a w) c", w=3)).then_inc(S("lora_in"), 16)
            load_ln(0)
            if stop == 1:
                return
            scale_residual(2)
            load_ln(1)
            pool.dma_start(wba_sb, wba).then_inc(S("wba_in"), 16)
            scale_residual(3)
            pool.wait_ge(S("ba_out"), 1)
            pool.dma_start(k1, c1).then_inc(S("c1_in"), 16)
            pool.dma_start(cw, conv).then_inc(S("c1_in"), 16)
            pool.dma_start(r1, rows1.partition_broadcast(P)).then_inc(S("c1_in"), 16)
            pool.dma_start(nw, normw).then_inc(S("c1_in"), 16)
            load_ln(2)
            scale_residual(4)
            load_ln(3)

        @block.tensor
        def _(pe):
            mm = nc.tensor.matmul

            def unit(n, q, mode, act, buf, width, lag=2, ready=None):
                ah, al = act
                if q == 0:
                    pe.wait_ge(S("evacuated"), n + (3 - lag))
                pe.wait_ge(S("lo_ready"), n * UNITS + (q + 1 + UNITS))
                if ready is not None:
                    pe.wait_ge(S("hid_ready"), ready)
                slot = q % RING
                for j in range(width // P if mode == "B" else TT):
                    for kk in range(UK):
                        k = q * UK + kk
                        if mode == "B":
                            o = pp[buf][:, j * T:(j + 1) * T]
                            c = slice(j * P, (j + 1) * P)
                            pairs = [(wh[:, slot, kk, c], ah[:, k, :]), (wh[:, slot, kk, c], al[:, k, :]),
                                     (wl[:, slot, kk, c], ah[:, k, :])]
                            first = q == 0 and kk == 0 and j % 2 == 0
                        else:
                            o = pp[buf][:, j * WIDE:(j + 1) * WIDE]
                            c = slice(j * P, (j + 1) * P)
                            pairs = [(ah[:, k, c], wh[:, slot, kk, :]), (ah[:, k, c], wl[:, slot, kk, :]),
                                     (al[:, k, c], wh[:, slot, kk, :])]
                            first = q == 0 and kk == 0
                        for m, (lhs, rhs) in enumerate(pairs):
                            last = mm(o, lhs, rhs, start=first and m == 0, stop=q == UNITS - 1 and kk == UK - 1 and m == 2,
                                      skip_group_check=True)
                last.then_inc(S("unit_used"), 1)

            def panel(n, *a, **k):
                for q in range(UNITS):
                    unit(n, q, *a, **k)

            A, H = (aTh, aTl), (hTh, hTl)

            def transposes(k):
                for t in range(TT):
                    if k:
                        pe.wait_ge(S("x_ready"), TT * (k - 1) + t + 1)
                    for c in range(4):
                        r = TT * 4 * k + 4 * t + c
                        if r >= 4:
                            pe.wait_ge(S("xlo"), r - 3)
                        for e in range(4):
                            last = nc.tensor.transpose(mb[c][:, e * P:(e + 1) * P],
                                                       xres[:, t, (4 * c + e) * P:(4 * c + e + 1) * P], ident)
                        if t == TT - 1 and c == 3:
                            last.then_inc(S("x_transposed"), 1)
                        else:
                            last.then_inc(S("xT"), 1)

            pe.sem_inc(S("unit_used"), RING)
            pe.sem_inc(S("evacuated"), 2)
            pe.sem_inc(S("lora_used"), 1)
            pe.sem_inc(S("rw_o"), 1)
            pe.sem_inc(S("hid_ready"), 1)
            pe.wait_ge(S("consts_in"), 16)
            pe.wait_ge(S("x_in"), 16)
            transposes(0)
            pe.wait_ge(S("xlo"), 8)
            panel(0, "B", A, 1, NARROW)

            def mix0(m):
                m1 = m + 1
                pe.wait_ge(S("lora_in"), 16 * m1)
                pe.wait_ge(S("rw_o"), m1)
                pe.wait_ge(S("lo_acts"), 1)
                mm(mb[0][:, 0:T], lw[0:64, 0, :], loT[0:64, 0, :], start=True, stop=True)
                mm(mb[1][:, 0:T], lw[64:P, 0, :], loT[64:P, 0, :], start=True, stop=True)
                mm(mb[0][:, T:2 * T], lw[:, 1, :], loT[:, 1, :], start=True, stop=False, skip_group_check=True)
                mm(mb[0][:, T:2 * T], lw[0:32, 2, :], loT[0:32, 2, :], start=False, stop=True,
                   skip_group_check=True).then_inc(S("lora_used"), 1)
                pe.wait_ge(S("evacuated"), 2 * m + (2 + P_GROUPS0 + 2))
                nc.tensor.transpose(mb[1][:, T:T + P], sbq[:, 2, 0:P], ident)
                nc.tensor.transpose(mb[1][:, T + P:2 * T], sbq[:, 2, P:T], ident)
                mm(mb[3][:, 0:T], sbq[:, 1, 0:P], sbq[:, 0, :], start=True, stop=True, skip_group_check=True)
                mm(mb[3][:, T:T + P], sbq[:, 1, P:T], sbq[:, 0, P:T], start=True, stop=True,
                   skip_group_check=True).then_inc(S("scores"), 1)
                yield
                pe.wait_ge(S("ksq"), m1)
                pe.wait_ge(S("vtk"), m1)
                mm(mb[1][:, 0:T], bo, ksq, start=True, stop=True, skip_group_check=True).then_inc(S("kss"), 1)
                yield
                pe.wait_ge(S("lkeep"), m1)
                mm(mb[2][:, 0:384], tri, sbb, start=True, stop=False, skip_group_check=True)
                mm(mb[2][:, P:T], ones, sbb[:, T:384], start=False, stop=True, skip_group_check=True).then_inc(S("lcum"), 1)
                yield
                pe.wait_ge(S("attn"), m1)
                mm(mb[3][:, 0:T], vtk[:, 0, :], sba[:, 0:T], start=True, stop=False, skip_group_check=True)
                mm(mb[3][:, P:T], vtk[:, 1, :], sba[:, T:384], start=False, stop=True,
                   skip_group_check=True).then_inc(S("sb_o"), 1)
                yield
                pe.wait_ge(S("operands"), m1)
                for t in range(TT):
                    for h in range(2):
                        hr = slice(64 * h, 64 * h + 64)
                        for w, src in enumerate((bt, kt_)):
                            if t == 1 and h == 0 and w == 0:
                                pe.wait_ge(S("sb_lo"), m1)
                            last = mm(mb[2 * t + h][:, w * T:(w + 1) * T], src[hr, t * P:(t + 1) * P],
                                      KR[hr, t, :, :], start=w == 0, stop=True, skip_group_check=True)
                    last.then_inc(S("gram"), 1)
                yield
                pe.wait_ge(S("masked"), 2 * m + 1)
                for w, src in enumerate((bt, kt_, rkv[:, 2, :])):
                    for t in range(TT):
                        e = 2 * w + t
                        last = nc.tensor.transpose(mb[e // 4][:, (e % 4) * P:(e % 4 + 1) * P], src[:, t * P:(t + 1) * P], ident)
                last.then_inc(S("tokT"), 1)
                yield
                for lv in range(6):
                    if lv == 0:
                        pe.wait_ge(S("XT_first"), m1)
                        for p in range(4):
                            last = nc.tensor.transpose(mb[2][:, p * P:(p + 1) * P], XT0[:, p, :], ident)
                        last.then_inc(S("Xnew"), 1)
                        yield
                        continue
                    s = 1 << lv
                    pe.wait_ge(S("X_ready"), 6 * m + lv)
                    if lv > 1:
                        pe.wait_ge(S("XT_ready"), 5 * m + lv - 1)
                    for p in range(4):
                        Xp = X0[:, p, :].rearrange("p (b w s) -> p b w s", w=2, s=s)
                        last = mm(mb[3][:, p * 64:(p + 1) * 64], GM[:, p // 2, p % 2, 0, 0, :], Xp[:, :, 0, :],
                                  start=p == 0, stop=True, skip_group_check=True)
                    last.then_inc(S("AX"), 1)
                    yield
                    pe.wait_ge(S("Yn"), 5 * m + lv)
                    for p in range(4):
                        last = mm(mb[2][:, p * 64:(p + 1) * 64], XT0[:, p, :], Yn0[:, p, :], start=p == 0, stop=True,
                                  skip_group_check=True)
                    last.then_inc(S("dX"), 1)
                    yield
                    pe.wait_ge(S("X_ready"), 6 * m + lv + 1)
                    for p in range(4):
                        last = nc.tensor.transpose(mb[3][:, p * P:(p + 1) * P], X0[:, p, :], ident)
                    last.then_inc(S("Xnew"), 1)
                    yield
                for c in range(4):
                    t, hf = divmod(c, 2)
                    R = slice(64 * hf, 64 * hf + 64)
                    if c == 0:
                        pe.wait_ge(S("XT_ready"), 5 * m1)
                        pe.wait_ge(S("tok_ready"), m1)
                    pe.wait_ge(S("state0"), 5 * m + c + 1)
                    mm(mb[0][R, 0:P], KR[:, t, 0, R], S0, start=True, stop=False, skip_group_check=True)
                    for h in range(2):
                        last = mm(mb[0][R, 64 * h:64 * h + 64], GM[R, t, h, 1, 0, R], tok[R, 2, t, 64 * h:64 * h + 64],
                                  start=False, stop=True, skip_group_check=True)
                    last.then_inc(S("rhs"), 1)
                    yield
                    pe.wait_ge(S("Rn"), 4 * m + c + 1)
                    for h in range(2):
                        last = mm(mb[1][:, 64 * h:64 * h + 64], XT0[R, 2 * t + h, :], Rn[R, 64 * h:64 * h + 64],
                                  start=h == 0, stop=True, skip_group_check=True)
                    last.then_inc(S("u_psum"), 1)
                    yield
                    pe.wait_ge(S("U"), 4 * m + c + 1)
                    mm(mb[3][:, 0:P], tok[R, 0, t, :], U[R, :], start=True, stop=False, skip_group_check=True)
                    mm(mb[3][:, 0:P], tok[R, 1, t, :], tok[R, 2, t, :], start=False, stop=True,
                       skip_group_check=True).then_inc(S("dS"), 1)
                    yc_ = slice(64 * c, 64 * c + 64)
                    mm(mb[2][:, yc_], S0, KR[:, t, 1, R], start=True, stop=False, skip_group_check=True)
                    for h in range(2):
                        hs = slice(64 * h, 64 * h + 64)
                        mm(mb[2][hs, yc_], U[R, hs], GM[R, t, h, 0, 1, R], start=False, stop=False, skip_group_check=True)
                        last = mm(mb[2][hs, yc_], tok[R, 2, t, hs], GM[R, t, h, 1, 1, R], start=False, stop=True,
                                  skip_group_check=True)
                    last.then_inc(S("y_psum"), 1)
                    yield
                pe.wait_ge(S("yT"), m1)
                mm(mb[0][:, 0:T], bo64, yT, start=True, stop=True, skip_group_check=True)
                mm(mb[1][:, 0:T], bo, rk, start=True, stop=True, skip_group_check=True).then_inc(S("ymean"), 1)
                yield
                pe.wait_ge(S("ysq"), m1)
                mm(mb[0][:, T:2 * T], bo64, ksq, start=True, stop=True, skip_group_check=True).then_inc(S("yvar"), 1)
                yield

            def group0(i):
                n = 2 * i + P_GROUPS0
                return lambda u: unit(n + u // UNITS, u % UNITS, "B", A, u // UNITS, NARROW)

            def drive(mixer, one, units):
                k = 0
                for _ in mixer:
                    if k < units:
                        one(k)
                    k += 1
                for u in range(k, units):
                    one(u)

            pe.wait_ge(S("c0_in"), 16)
            drive([], group0(0), 2 * UNITS)
            with pe.Fori(1, GROUPS) as i:
                drive(mix0(i - 1), group0(i), 2 * UNITS)
            drive(mix0(GROUPS - 1), None, 0)
            pe.wait_ge(S("mix0_out"), GROUPS)
            for j in range(4):
                panel(P_OUT0 + j, "A", H, j % 2, WIDE)
            transposes(1)
            if stop == 1:
                return

            def mlp(n0, k, b0):
                pe.wait_ge(S("xlo"), 8 * k + 8)
                with pe.Fori(0, FG) as f:
                    for j in range(4):
                        panel(f * 8 + (n0 + j), "B", A, (b0 + j) % 2, WIDE)
                    for j in range(4):
                        for q in range(UNITS):
                            unit(f * 8 + (n0 + 4 + j), q, "A", H, (b0 + j) % 2, WIDE,
                                 ready=f * 4 + (4 * FG * (k - 1) // 2 + (UK * q + 1) // 4 + 2) if j == 0 and q % 2 == 0 else None)

            mlp(P_MLP0, 1, 0)
            transposes(2)
            pe.wait_ge(S("xlo"), 24)
            pe.wait_ge(S("wba_in"), 16)
            for t in range(TT):
                for k in range(KT):
                    for a in (aTh, aTl):
                        last = mm(mb[0][:, t * 64:(t + 1) * 64], a[:, k, t * P:(t + 1) * P].bitcast(F32), wba_sb[:, k, :],
                                  start=k == 0 and a is aTh and t == 0, stop=k == KT - 1 and a is aTl, skip_group_check=True)
            last.then_inc(S("ba_out"), 1)
            pe.wait_ge(S("g_ready"), 1)
            gvf = gv.rearrange("p c h -> p (c h)")
            mm(mb[1][:, 0:64], UT, gvf, start=True, stop=True, skip_group_check=True)
            mm(mb[1][:, 64:128], ones, gvf, start=True, stop=True, skip_group_check=True).then_inc(S("gsum"), 1)

            def mix1(g):
                g1 = g + 1
                for _ in range(7):
                    yield
                pe.wait_ge(S("sq"), g1)
                for c in range(TT):
                    for j in range(4):
                        last = mm(mb[0][:, 4 * c + j:4 * c + j + 1], SQ[:, j, c * P:(c + 1) * P], ones[:, 0:1],
                                  start=c + j == 0, stop=True, skip_group_check=True)
                last.then_inc(S("ssq"), 1)
                yield
                pe.wait_ge(S("cols"), g1)
                for c in range(TT):
                    for j in range(2):
                        last = nc.tensor.transpose(mb[1][:, (2 * c + j) * P:(2 * c + j + 1) * P],
                                                   qkv[:, 2 + j, c * P:(c + 1) * P], ident)
                last.then_inc(S("kT"), 1)
                for c in range(TT):
                    for h in range(4):
                        last = nc.tensor.transpose(mb[2 + c][:, h * P:(h + 1) * P], qkv[:, 4 + h, c * P:(c + 1) * P], ident)
                last.then_inc(S("vT"), 1)
                yield
                pe.wait_ge(S("tok1"), g1)
                for c in range(TT):
                    for j in range(2):
                        last = mm(mb[c][:, j * T:(j + 1) * T], qkv[:, 2 + j, c * P:(c + 1) * P],
                                  qkv[:, :, c * P:(c + 1) * P].rearrange("p (w j) t -> p j w t", j=2)[:, j, 0:2, :],
                                  start=j == 0, stop=True, skip_group_check=True)
                last.then_inc(S("kq"), 1)
                yield
                pe.wait_ge(S("utg"), g1)
                for c in range(TT):
                    last = mm(mb[2 + c][:, :], SL, UTg[:, c, :, :], start=True, stop=True, skip_group_check=True)
                last.then_inc(S("dlog"), 1)
                yield
                for lv in range(7):
                    if lv == 0:
                        pe.wait_ge(S("XT1_first"), g1)
                        for p in range(8):
                            last = nc.tensor.transpose(mb[2 + p // 4][:, (p % 4) * P:(p % 4 + 1) * P], XT1[:, p, :], ident)
                        last.then_inc(S("X1new"), 1)
                        yield
                        continue
                    s = 1 << lv
                    pe.wait_ge(S("X1_ready"), 7 * g + lv)
                    for p in range(8):
                        Xp = X1[:, p, :].rearrange("p (b w s) -> p b w s", w=2, s=s)
                        last = mm(mb[0][:, p * 64:(p + 1) * 64], At[:, p // 4, p % 4, :], Xp[:, :, 0, :],
                                  start=p == 0, stop=True, skip_group_check=True)
                    last.then_inc(S("AX1"), 1)
                    yield
                    pe.wait_ge(S("Yn1"), 6 * g + lv)
                    if lv > 1:
                        pe.wait_ge(S("XT1_ready"), 6 * g + lv - 1)
                    for p in range(8):
                        last = mm(mb[1][:, p * 64:(p + 1) * 64], XT1[:, p, :], Yn1[:, p, :], start=p == 0, stop=True,
                                  skip_group_check=True)
                    last.then_inc(S("dX1"), 1)
                    yield
                    pe.wait_ge(S("X1_ready"), 7 * g + lv + 1)
                    for p in range(8):
                        last = nc.tensor.transpose(mb[2 + p // 4][:, (p % 4) * P:(p % 4 + 1) * P], X1[:, p, :], ident)
                    last.then_inc(S("X1new"), 1)
                    yield
                pe.wait_ge(S("XT1_ready"), 6 * g1)
                for c in range(TT):
                    cs = slice(c * P, (c + 1) * P)
                    n = 2 * g + c
                    pe.wait_ge(S("state1"), 3 * g + c + 1)
                    for j in range(2):
                        last = mm(mb[0][:, j * T:(j + 1) * T], qkv[:, 2 + j, cs], S1[:, 2 * j:2 * j + 2, :], start=j == 0,
                                  stop=True, skip_group_check=True)
                    last.then_inc(S("kS"), 1)
                    for j in range(2):
                        last = mm(mb[1][:, j * T:(j + 1) * T], qkv[:, j, cs], S1[:, 2 * j:2 * j + 2, :], start=j == 0,
                                  stop=True, skip_group_check=True)
                    last.then_inc(S("qS"), 1)
                    yield
                    pe.wait_ge(S("yp"), n + 1)
                    for h in range(4):
                        last = mm(mb[2][:, h * P:(h + 1) * P], XT1[:, 4 * c + h, :], yp[:, h, :], start=h == 0, stop=True,
                                  skip_group_check=True)
                    last.then_inc(S("z_psum"), 1)
                    yield
                    pe.wait_ge(S("vke"), n + 1)
                    for j in range(2):
                        last = mm(mb[3][:, j * T:(j + 1) * T], ktok[:, c, j, :], vke[:, 2 * j:2 * j + 2, :], start=j == 0,
                                  stop=True, skip_group_check=True)
                    last.then_inc(S("dS1"), 1)
                    pe.wait_ge(S("vk"), n + 1)
                    for h in range(4):
                        last = mm(mb[0][:, h * P:(h + 1) * P], AT[:, c, h, :], vk[:, h, :], start=h == 0, stop=True,
                                  skip_group_check=True)
                    last.then_inc(S("o_psum"), 1)
                    yield
                    pe.wait_ge(S("on"), n + 1)
                    for h in range(4):
                        last = nc.tensor.transpose(mb[2][:, h * P:(h + 1) * P], yp[:, h, :], ident)
                    last.then_inc(S("oT"), 1)
                    yield

            def group1(n):
                return lambda u: unit(n + u // UNITS, u % UNITS, "B", A, (0, 1, 0)[u // UNITS], WIDE,
                                      lag=(1, 2, 2)[u // UNITS])

            with pe.Fori(0, 2) as half:
                n0 = half * HALF1 + P_L1
                drive([], group1(n0), 3 * UNITS)
                with pe.Fori(1, 4) as i:
                    drive(mix1(half * 4 + i - 1), group1(n0 + i * 3), 3 * UNITS)
                drive(mix1(half * 4 + 3), None, 0)
                pe.wait_ge(S("mix1_out"), half * 8 + 8)
                for j in range(4):
                    panel(n0 + (12 + j), "A", H, (1, 0)[j % 2], WIDE)
            transposes(3)
            mlp(P_MLP1, 3, 1)

        @block.scalar
        def _(act):
            go = nc.scalar.activation
            st = Steps(act, S("act_steps"))

            def split(n, q, width):
                act.wait_ge(S(f"landed{q}"), n * 16 + 16)
                act.wait_ge(S("unit_used"), n * UNITS + (q + 1))
                nc.scalar.copy(wh[:, q % RING, :, 0:width], raw[:, q, :, 0:width]).then_inc(S("hi_ready"), 1)

            def x_high(k):
                for t in range(TT):
                    for c in range(4):
                        r = TT * 4 * k + 4 * t + c
                        if t == TT - 1 and c == 3:
                            act.wait_ge(S("x_transposed"), k + 1)
                        else:
                            act.wait_ge(S("xT"), 7 * k + 4 * t + c + 1)
                        nc.scalar.copy(aTh[:, 4 * c:4 * c + 4, t * P:(t + 1) * P],
                                       r2(mb[c][:, :], a=4)).then_inc(S("xhi"), 1)

            def panel_done(n):
                act.wait_ge(S("unit_used"), n * UNITS + UNITS + RING)

            def between(k, units, one, hook, ahead):
                if k < units and (ahead or k + LEAD < units):
                    one(k + LEAD)
                if k > UNITS and (k - 1) // UNITS <= units // UNITS and (k - 1) % UNITS in (0, 1):
                    hook((k - 1) // UNITS - 1, (k - 1) % UNITS)

            def drive(mixer, units, one, hook, ahead, late=None, begun=False):
                if not ahead and not begun:
                    for u in range(LEAD):
                        one(u)
                k = 0
                for _ in mixer:
                    between(k, units, one, hook, ahead)
                    k += 1
                for k in range(k, units + 3):
                    between(k, units, one, hook, ahead)
                if late:
                    late()

            def ln_rstd(k):
                for t in range(TT):
                    act.wait_ge(S("ln_var"), TT * k + t + 1)
                    st(go(rstd[:, t:t + 1], mv[:, t, 1:2], ACT.Ln, bias=eps_ln))
                    st.settle()
                    go(rstd[:, t:t + 1], rstd[:, t:t + 1], ACT.Exp, scale=-0.5).then_inc(S("ln_rstd"), 1)

            nc.scalar.preload_act_table_set("natural_log_exp_and_others")
            act.wait_ge(S("eps_ready"), 1)
            x_high(0)
            for q in range(UNITS):
                split(0, q, NARROW)
            panel_done(0)
            act.wait_ge(S("zeroed"), 1)
            nc.scalar.copy(lobuf[:, :, 1:T + 1], r2(pp[1][:, 0:3 * T], a=3)).then_inc(S("evacuated"), 1)
            act.wait_ge(S("lo_shifted"), 1)
            st(go(loT[0:64, 0, :], loT[0:64, 0, :], ACT.Exp, scale=2.0))
            go(loT[:, 1:3, :], loT[:, 1:3, :], ACT.Exp, scale=-1.0).then_inc(S("lo_exp"), 1)

            def mix0(m):
                m1 = m + 1
                act.wait_ge(S("kk0"), m1)
                go(ksq, kk0, ACT.Square).then_inc(S("ksq"), 1)
                act.wait_ge(S("scores"), m1)
                st(go(ew[:, 0:T], mb[0][:, 0:T], ACT.Exp, scale=-1.0, bias=nprm[:, bass.ds(m, 1), 0]))
                go(ew[:, T:2 * T], mb[1][:, 0:T], ACT.Exp, scale=-1.0,
                   bias=nprm[:, bass.ds(m, 1), 1]).then_inc(S("gates_exp"), 1)
                st(go(sbb, mb[3][:, 0:384], ACT.Abs))
                st.settle()
                st(go(sbb, sbb, ACT.Exp, scale=-1.0))
                st.settle()
                go(sbb, sbb, ACT.Ln, bias=1.0).then_inc(S("softplus"), 1)
                st(nc.scalar.copy(gg, mb[0][:, T:2 * T]))
                nc.scalar.copy(vtk, r2(mb[1][:, T:2 * T], a=TT)).then_inc(S("vtk"), 1)
                yield
                act.wait_ge(S("kss"), m1)
                st(go(ksq, mb[1][:, 0:T], ACT.Ln, bias=eps_kk))
                st.settle()
                go(ksq, ksq, ACT.Exp, scale=-0.5).then_inc(S("rkk"), 1)
                act.wait_ge(S("cum"), m1)
                st(go(pinc, cum, ACT.Exp))
                st(go(pinv, cum, ACT.Exp, scale=-1.0))
                go(pexc, pexc, ACT.Exp).then_inc(S("powers"), 1)
                yield
                act.wait_ge(S("loga"), m1)
                go(sba, sba, ACT.Exp).then_inc(S("attn"), 1)
                yield
                act.wait_ge(S("sb_o"), m1)
                nc.scalar.copy(hTh[:, bass.ds(m, 1), :], mb[3][:, 0:T].unsqueeze(1)).then_inc(S("sb_hi"), 1)
                yield
                yield
                act.wait_ge(S("tokT"), m1)
                st(nc.scalar.copy(tok[:, 0:2, :, :], mb[0][:, :].rearrange("p (w t c) -> p w t c", w=2, t=TT)))
                nc.scalar.copy(tok[:, 2, :, :], r2(mb[1][:, 0:T], a=TT)).then_inc(S("tok_ready"), 1)
                yield
                for lv in range(6):
                    if lv:
                        yield
                        yield
                    act.wait_ge(S("Xnew"), 6 * m + lv + 1)
                    if lv == 0:
                        nc.scalar.copy(X0, r2(mb[2][:, :], a=4)).then_inc(S("X_ready"), 1)
                    else:
                        nc.scalar.copy(XT0, r2(mb[3][:, :], a=4)).then_inc(S("XT_ready"), 1)
                    yield
                for c in range(4):
                    R = slice(64 * (c % 2), 64 * (c % 2) + 64)
                    yield
                    act.wait_ge(S("u_psum"), 4 * m + c + 1)
                    nc.scalar.copy(U[R, :], mb[1][R, 0:P]).then_inc(S("U"), 1)
                    yield
                    if c == 3:
                        act.wait_ge(S("y_psum"), 4 * m1)
                        nc.scalar.copy(yT, mb[2][:, 0:T]).then_inc(S("yT"), 1)
                    yield
                act.wait_ge(S("yc"), m1)
                go(ksq, yc, ACT.Square).then_inc(S("ysq"), 1)
                yield
                act.wait_ge(S("yvar"), m1)
                st(go(ksq, mb[0][:, T:2 * T], ACT.Ln, bias=eps_lnx))
                st.settle()
                go(ksq, ksq, ACT.Exp, scale=-0.5).then_inc(S("yrstd"), 1)
                act.wait_ge(S("rw_o"), m1 + 1)
                nc.scalar.copy(hTh[:, bass.ds(m + 8, 1), :], yn.unsqueeze(1)).then_inc(S("rw_hi"), 1)
                yield

            def group0(i, first=False):
                n = i * 2 + P_GROUPS0

                def hook(j, late):
                    if late:
                        return
                    panel_done(n + j)
                    if j == 0:
                        if not first:
                            act.wait_ge(S("shifted"), i)
                        nc.scalar.copy(pb[:, :, 1:T + 1], r2(pp[0][:, 0:3 * T], a=3)).then_inc(S("evacuated"), 1)
                    else:
                        if not first:
                            act.wait_ge(S("scores"), i)
                        st(go(sbq[:, 0, :], pp[1][:, 0:T], ACT.Copy, scale=SB_SCALE))
                        nc.scalar.copy(sbq[:, 1:3, :], r2(pp[1][:, T:3 * T], a=2)).then_inc(S("evacuated"), 1)
                return 2 * UNITS, (lambda u: split(n + u // UNITS, u % UNITS, NARROW)), hook, False

            st.leave_straight()
            st.enter(0, 1)
            drive([], *group0(0, True))
            st.leave(1)
            PER = 9
            with act.Fori(1, GROUPS) as i:
                st.enter(i - 1, PER + 1)
                drive(mix0(i - 1), *group0(i))
            st.leave(GROUPS - 1)
            for u in range(LEAD):
                split(P_OUT0, u, WIDE)
            for _ in mix0(GROUPS - 1):
                pass

            def wide(n, units):
                return units, (lambda u: split(n + u // UNITS, u % UNITS, WIDE))

            def nothing(j, late):
                pass

            drive([], *wide(P_OUT0, 4 * UNITS), nothing, stop != 1, begun=True)
            ln_rstd(0)
            x_high(1)
            if stop == 1:
                return

            def mlp(n0, k, b0):
                def body(f, ahead):
                    n = f * 8 + n0

                    def hook(j, late):
                        if j < 4 and not late:
                            panel_done(n + j)
                            act.wait_ge(S("hid_ready"), f * 4 + (4 * FG * k + j + 1))
                            go(hid, pp[(b0 + j) % 2][:, :], ACT.Relu).then_inc(S("evacuated"), 1)
                            act.wait_ge(S("evacuated"), n + (j + 3))
                            go(hTh[:, 4 * j:4 * j + 4, :], r2(hid, a=4), ACT.Square).then_inc(S("hid_hi"), 1)
                    units, one = wide(n, 8 * UNITS)
                    for u in range(units + 3):
                        between(u, units, one, hook, ahead)
                with act.Fori(0, FG - 1) as f:
                    body(f, True)
                body(FG - 1, k == 0)

            mlp(P_MLP0, 0, 0)
            ln_rstd(1)
            x_high(2)
            st.leave_straight()
            act.wait_ge(S("ba_out"), 1)
            act.wait_ge(S("c1_in"), 64)
            ba = mb[0][:, 0:128].rearrange("p (c h) -> p c h", c=TT)
            st(go(beta, ba[:, :, 0:32], ACT.Exp, scale=-1.0))
            go(r1[:, 0:32], r1[:, 0:32], ACT.Exp).then_inc(S("beta_exp"), 1)
            act.wait_ge(S("a_dt"), 1)
            st(go(gtmp, gv, ACT.Abs))
            st.settle()
            st(go(gtmp, gtmp, ACT.Exp, scale=-1.0))
            st.settle()
            go(gtmp, gtmp, ACT.Ln, bias=1.0).then_inc(S("g_ln"), 1)
            act.wait_ge(S("gsum"), 1)
            gc_ps = mb[1][:, 0:64].rearrange("p (c h) -> p c h", c=TT)
            gl_ps = mb[1][:, 64:128].rearrange("p (c h) -> p c h", c=TT)
            st(go(egc, gc_ps, ACT.Exp))
            go(egl, gl_ps, ACT.Exp).then_inc(S("gsum_read"), 1)
            act.wait_ge(S("kend_log"), 1)
            go(kend, kend, ACT.Exp).then_inc(S("gates1"), 1)

            def mix1(g, n, gl):
                g1 = g + 1
                head = lambda a, c, h: a[:, c, bass.ds(g * 4 + h, 1)]
                for j in range(8):
                    last = go(qkv[:, j, :], cbuf[:, j, 3:T + 3], ACT.Copy, scale=cw[:, bass.ds(g, 1), 4 * j + 3])
                    if j < 7:
                        st(last)
                last.then_inc(S("conv_first"), 1)
                for _ in range(3):
                    yield
                act.wait_ge(S("conv"), g1)
                go(E1, qkv, ACT.Exp, scale=-1.0).then_inc(S("e_qkv"), 1)
                go(SQ, zs, ACT.Exp, scale=-1.0).then_inc(S("e_z"), 1)
                yield
                yield
                yield
                act.wait_ge(S("zs_ready"), g1)
                go(SQ, qkv[:, 0:4, :], ACT.Square).then_inc(S("sq"), 1)
                yield
                act.wait_ge(S("ssq"), g1)
                st(go(lnss, r2(mb[0][:, 0:8], a=TT), ACT.Ln, bias=eps_l2))
                st.settle()
                st(go(qsc, lnss[:, :, 0:2], ACT.Exp, scale=-0.5, bias=ln_qs))
                st(go(skc, lnss[:, :, 2:4], ACT.Exp, scale=0.5))
                go(wkc, lnss[:, :, 2:4], ACT.Exp, scale=-1.0).then_inc(S("cols"), 1)
                yield
                act.wait_ge(S("kT"), g1)
                st(nc.scalar.copy(ktok, mb[1][:, :].rearrange("p (c j t) -> p c j t", c=TT, j=2)))
                act.wait_ge(S("vT"), g1)
                for c in range(TT):
                    for j in range(2):
                        last = go(vs[:, c, 2 * j:2 * j + 2, :], r2(mb[2 + c][:, j * T:(j + 1) * T], a=2), ACT.Copy,
                                  scale=skc[:, c, j:j + 1])
                        if c + j < 2:
                            st(last)
                last.then_inc(S("tok1"), 1)
                yield
                yield
                act.wait_ge(S("dlog"), g1)
                for c in range(TT):
                    last = go(Dm[:, c, :, :], r2(mb[2 + c][:, :], a=4), ACT.Exp)
                    if c == 0:
                        st(last)
                last.then_inc(S("D"), 1)
                yield
                for lv in range(7):
                    if lv:
                        yield
                        yield
                    act.wait_ge(S("X1new"), 7 * g + lv + 1)
                    dst = XT1 if lv else X1
                    st(nc.scalar.copy(dst[:, 0:4, :], r2(mb[2][:, :], a=4)))
                    nc.scalar.copy(dst[:, 4:8, :], r2(mb[3][:, :], a=4)).then_inc(S("XT1_ready" if lv else "X1_ready"), 1)
                    yield
                for c in range(TT):
                    nn = 2 * g + c
                    act.wait_ge(S("qS"), nn + 1)
                    for h in range(4):
                        last = go(t2[:, h, :], mb[1][:, h * P:(h + 1) * P], ACT.Copy, scale=head(egc, c, h))
                        if h < 3:
                            st(last)
                    last.then_inc(S("t1"), 1)
                    yield
                    act.wait_ge(S("z_psum"), nn + 1)
                    for h in range(4):
                        last = go(vk[:, h, :], mb[2][:, h * P:(h + 1) * P], ACT.Copy, scale=wc[:, c, h:h + 1])
                        if h < 3:
                            st(last)
                    last.then_inc(S("vk"), 1)
                    yield
                    act.wait_ge(S("t2"), nn + 1)
                    for h in range(4):
                        go(sqj, t2[:, h, :], ACT.Square, accum_out=oss[:, h:h + 1]).then_inc(S("oss"), 1)
                        act.wait_ge(S("oss"), 4 * nn + h + 1)
                    act.wait_ge(S("o_ms"), nn + 1)
                    st(go(osq, osc, ACT.Ln, bias=eps_l2))
                    st.settle()
                    go(osq, osq, ACT.Exp, scale=-0.5).then_inc(S("o_rstd"), 1)
                    yield
                    act.wait_ge(S("oTf"), nn + 1)
                    nc.scalar.copy(hTh[:, bass.ds(gl * 4, 4), c * P:(c + 1) * P], oT1).then_inc(S("mix1_hi"), 1)
                    yield

            def group1(n, before=None):
                units, one = wide(n, 3 * UNITS)

                def hook(j, late):
                    if late or j == 2:
                        return
                    panel_done(n + j)
                    if before is not None:
                        act.wait_ge(S("conv"), before)
                    nc.scalar.copy(cbuf[:, 4 * j:4 * j + 4, 3:T + 3], r2(pp[j][:, :], a=4)).then_inc(S("evacuated"), 1)

                def z_out():
                    panel_done(n + 2)
                    nc.scalar.copy(zs, r2(pp[0][:, :], a=4)).then_inc(S("evacuated"), 1)
                return units, one, hook, True, z_out

            PER1 = 36
            st.leave_straight()
            act.wait_ge(S("zeroed"), 2)
            base = st.total
            with act.Fori(0, 2) as half:
                n0 = half * HALF1 + P_L1
                drive([], *group1(n0))
                with act.Fori(1, 4) as i:
                    st.enter((half * 4) + (i - 1), PER1)
                    drive(mix1(half * 4 + i - 1, None, i - 1), *group1(n0 + i * 3, half * 4 + i))
                st.enter(half * 4 + 3, PER1)
                for _ in mix1(half * 4 + 3, None, 3):
                    pass
                units, one = wide(n0 + 12, 4 * UNITS)
                for u in range(units):
                    one(u + LEAD)
            st.leave(8)
            ln_rstd(2)
            x_high(3)
            mlp(P_MLP1, 1, 1)
            ln_rstd(3)

        @block.vector
        def _(dve):
            tt, ts, stt = nc.vector.tensor_tensor, nc.vector.tensor_scalar, nc.vector.scalar_tensor_tensor
            st = Steps(dve, S("dve_steps"))

            def f(ap):
                return ap.bitcast(F32)

            def rep(ap, n):
                return ap.unsqueeze(1).to_broadcast([P, n, ap.shape[-1]])

            def split(n, q, width):
                dve.wait_ge(S("hi_ready"), n * UNITS + (q + 1))
                tt(wl[:, q % RING, :, 0:width], raw[:, q, :, 0:width], f(wh[:, q % RING, :, 0:width]),
                   ALU.subtract).then_inc(S("lo_ready"), 1)

            def x_low(k):
                for t in range(TT):
                    for c in range(4):
                        dve.wait_ge(S("xhi"), 8 * k + 4 * t + c + 1)
                        ks, ts_ = slice(4 * c, 4 * c + 4), slice(t * P, (t + 1) * P)
                        tt(aTl[:, ks, ts_], r2(mb[c][:, :], a=4), f(aTh[:, ks, ts_]), ALU.subtract).then_inc(S("xlo"), 1)

            def panel_done(n):
                dve.wait_ge(S("unit_used"), n * UNITS + UNITS + RING)

            def between(k, units, one, hook, ahead):
                if k < units and (ahead or k + LEAD < units):
                    one(k + LEAD)
                if k > UNITS and (k - 1) // UNITS <= units // UNITS and (k - 1) % UNITS in (0, 1):
                    hook((k - 1) // UNITS - 1, (k - 1) % UNITS)

            def drive(mixer, units, one, hook, ahead, begun=False):
                if not ahead and not begun:
                    for u in range(LEAD):
                        one(u)
                k = 0
                for _ in mixer:
                    between(k, units, one, hook, ahead)
                    k += 1
                for k in range(k, units + 3):
                    between(k, units, one, hook, ahead)

            def add_residual(n, j, b):
                panel_done(n)
                dve.wait_ge(S("evacuated"), n + 2)
                o = xres[:, :, j * WIDE:(j + 1) * WIDE]
                tt(o, o, r2(pp[b][:, :], a=TT), ALU.add).then_inc(S("evacuated"), 1)

            def sigmoid_tail(ap):
                st(ts(ap, ap, 1e30, 1.0, ALU.min, ALU.add))
                st.settle()
                st(nc.vector.reciprocal(ap, ap))
                st.settle()

            def layer_norm(k, n_last):
                st.leave_straight()
                dve.wait_ge(S("evacuated"), n_last + 3)
                for t in range(TT):
                    for c in range(4):
                        st(nc.vector.bn_stats(stats[:, t, c, :], xres[:, t, c * WIDE:(c + 1) * WIDE]))
                    st.settle()
                    nc.vector.bn_aggr(mv[:, t, :], stats[:, t, :, :].rearrange("p c s -> p (c s)")).then_inc(S("ln_var"), 1)
                dve.wait_ge(S("ln_in"), 32 * (k + 1))
                for t in range(TT):
                    dve.wait_ge(S("ln_rstd"), TT * k + t + 1)
                    o = xres[:, t, :]
                    st(ts(o, o, mv[:, t, 0:1], rstd[:, t:t + 1], ALU.subtract, ALU.mult))
                    st.settle()
                    st(tt(o, o, lng, ALU.mult))
                    st.settle()
                    if k < 3:
                        tt(o, o, lnb, ALU.add).then_inc(S("x_ready"), 1)
                    else:
                        st(tt(o, o, lnb, ALU.add))
                if k in (0, 2):
                    dve.wait_ge(S("x_ready"), TT * (k + 1))
                    dve.sem_inc(S("ws_free"), 1)

            dve.sem_inc(S("lo_ready"), UNITS)
            for ap, v in ((eps_ln, LN_EPS), (eps_lnx, LNX_EPS), (eps_kk, KK_EPS), (eps_l2, 1e-6)):
                st(nc.vector.memset(ap, v))
            nc.vector.memset(ln_qs, -3.5 * 0.6931471805599453).then_inc(S("eps_ready"), 1)
            st(nc.vector.memset(pb[:, :, 0:1], 0.0))
            nc.vector.memset(lobuf[:, :, 0:1], 0.0).then_inc(S("zeroed"), 1)
            dve.wait_ge(S("prm_in"), 16)
            st(ts(nprm, prm[:, :, 3:5], -1.0, None, ALU.mult))
            x_low(0)
            for q in range(UNITS):
                split(0, q, NARROW)
            dve.wait_ge(S("evacuated"), 3)
            st(tt(dsh, lobuf[:, :, 0:T], lobuf[:, :, 1:T + 1], ALU.subtract))
            st.settle()
            for j in range(3):
                last = stt(loT[:, j, :], dsh[:, j, :], mulo[:, j:j + 1], lobuf[:, j, 1:T + 1], ALU.mult, ALU.add)
                if j < 2:
                    st(last)
            last.then_inc(S("lo_shifted"), 1)
            dve.wait_ge(S("lo_exp"), 1)
            sigmoid_tail(loT[:, 1:3, :])
            sigmoid_tail(loT[0:64, 0, :])
            ts(loT[0:64, 0, :], loT[0:64, 0, :], -2.0, 1.0, ALU.mult, ALU.add).then_inc(S("lo_acts"), 1)
            dve.wait_ge(S("c0_in"), 16)

            def mix0(m):
                m1 = m + 1
                par = lambda j: prm[:, bass.ds(m, 1), j]
                st(nc.vector.memset(S0, 0.0))
                dve.wait_ge(S("evacuated"), 2 * m + (P_GROUPS0 + 3))
                st(tt(dsh, pb[:, :, 0:T], pb[:, :, 1:T + 1], ALU.subtract))
                st.settle()
                for j in range(3):
                    last = stt(rkv[:, j, :], dsh[:, j, :], par(j), pb[:, j, 1:T + 1], ALU.mult, ALU.add)
                    if j < 2:
                        st(last)
                last.then_inc(S("shifted"), 1)
                dve.wait_ge(S("shifted"), m1)
                ts(kk0, rkv[:, 1, :], par(5), None, ALU.mult).then_inc(S("kk0"), 1)
                dve.wait_ge(S("gates_exp"), m1)
                sigmoid_tail(ew)
                st(ts(Lg, sigw, -0.6065306597126334, None, ALU.mult))
                st.settle()
                st(nc.vector.tensor_tensor_scan(cum, rst, Lg, 0.0, ALU.mult, ALU.add))
                st.settle()
                tt(pexc, cum, Lg, ALU.subtract).then_inc(S("cum"), 1)
                dve.wait_ge(S("softplus"), m1)
                st(stt(sbb, mb[3][:, 0:384], 0.0, sbb, ALU.max, ALU.add))
                st(tt(sbc, mb[3][:, 0:384], sbbig, ALU.add))
                st.settle()
                tt(sbb, sbb, sbneg, ALU.mult).then_inc(S("lkeep"), 1)
                yield
                st(ts(k2, av, 1.0, par(6), ALU.subtract, ALU.mult))
                st.settle()
                st(stt(k2, k2, 1.0, rkv[:, 1, :], ALU.add, ALU.mult))
                dve.wait_ge(S("rkk"), m1)
                st(tt(kkt, kk0, ksq, ALU.mult))
                st.settle()
                st(stt(rk, rkv[:, 0, :], par(7), k2, ALU.mult, ALU.mult))
                st(tt(bt, kkt, av, ALU.mult))
                dve.wait_ge(S("powers"), m1)
                st(tt(KR[:, :, 1, :], r2(rkv[:, 0, :], a=TT), r2(pinc, a=TT), ALU.mult))
                st(tt(KR[:, :, 0, :], r2(kkt, a=TT), r2(pexc, a=TT), ALU.mult))
                st(tt(kt_, k2, pinv, ALU.mult))
                st.settle()
                tt(bt, bt, pinv, ALU.mult).then_inc(S("operands"), 1)
                yield
                dve.wait_ge(S("lcum"), m1)
                tt(sba, sbc, mb[2][:, 0:384], ALU.add).then_inc(S("loga"), 1)
                yield
                dve.wait_ge(S("sb_hi"), m1)
                tt(hTl[:, bass.ds(m, 1), :], mb[3][:, 0:T].unsqueeze(1), f(hTh[:, bass.ds(m, 1), :]),
                   ALU.subtract).then_inc(S("sb_lo"), 1)
                yield
                for t in range(TT):
                    dve.wait_ge(S("gram"), 2 * m + t + 1)
                    for h in range(2):
                        last = tt(GM[:, t, h, :, :, :].rearrange("p w r c -> p w (r c)"), r2(mb[2 * t + h][:, :], a=2),
                                  rep(rwmask, 2), ALU.mult)
                        if h == 0:
                            st(last)
                    last.then_inc(S("masked"), 1)
                dve.wait_ge(S("masked"), 2 * m1)
                st(tt(XT0, GM.rearrange("p t h w r c -> p (t h) w r c")[:, :, 0, 0, :], rep(cc[:, C_M0:C_M0 + P], 4), ALU.mult))
                st.settle()
                tt(XT0, XT0, rep(ident, 4), ALU.add).then_inc(S("XT_first"), 1)
                yield
                yield
                yield
                for lv in range(1, 6):
                    s_ = 1 << lv
                    nb = 64 // s_
                    dve.wait_ge(S("AX"), 5 * m + lv)
                    tt(Yn0, r2(mb[3][:, 0:256], a=4), rep(cc[:, C_LV + 64 * (lv - 1):C_LV + 64 * lv], 4),
                       ALU.mult).then_inc(S("Yn"), 1)
                    yield
                    dve.wait_ge(S("dX"), 5 * m + lv)
                    left = X0.rearrange("p a (b w s) -> p a b w s", w=2, s=s_)[:, :, :, 0, :]
                    tt(left, left, mb[2][:, 0:256].rearrange("p (a b s) -> p a b s", a=4, s=s_), ALU.add).then_inc(S("X_ready"), 1)
                    yield
                    yield
                st.settle()
                nc.vector.tensor_copy(dS0, S0).then_inc(S("state0"), 1)
                for c in range(4):
                    R = slice(64 * (c % 2), 64 * (c % 2) + 64)
                    dve.wait_ge(S("rhs"), 4 * m + c + 1)
                    ts(Rn[R, :], mb[0][R, 0:P], -1.0, None, ALU.mult).then_inc(S("Rn"), 1)
                    yield
                    yield
                    dve.wait_ge(S("dS"), 4 * m + c + 1)
                    st(tt(dS0, mb[3][:, 0:P], bo, ALU.mult))
                    st.settle()
                    st(tt(dS0, dS0, S0, ALU.add))
                    st.settle()
                    dve.wait_ge(S("y_psum"), 4 * m + c + 1)
                    ts(S0, dS0, pinc[:, 64 * c + 63:64 * c + 64], None, ALU.mult).then_inc(S("state0"), 1)
                    dve.wait_ge(S("state0"), 5 * m + c + 2)
                    yield
                dve.wait_ge(S("ymean"), m1)
                tt(yc, yT, mb[0][:, 0:T], ALU.subtract).then_inc(S("yc"), 1)
                yield
                dve.wait_ge(S("yrstd"), m1)
                st(tt(yn, yc, ksq, ALU.mult))
                st.settle()
                st(ts(yn, yn, par(8), par(9), ALU.mult, ALU.add))
                st(tt(yc, mb[1][:, 0:T], rkv[:, 2, :], ALU.mult))
                st.settle()
                st(tt(yn, yn, yc, ALU.add))
                st.settle()
                tt(yn, yn, gg, ALU.mult).then_inc(S("rw_o"), 1)
                dve.wait_ge(S("rw_hi"), m1)
                tt(hTl[:, bass.ds(m + 8, 1), :], yn.unsqueeze(1), f(hTh[:, bass.ds(m + 8, 1), :]),
                   ALU.subtract).then_inc(S("mix0_out"), 1)
                dve.wait_ge(S("mix0_out"), m1)
                yield

            def nothing(j, late):
                pass

            def group0(i):
                n = i * 2 + P_GROUPS0
                return 2 * UNITS, (lambda u: split(n + u // UNITS, u % UNITS, NARROW)), nothing, False

            st.leave_straight()
            drive([], *group0(0))
            PER = 33
            with dve.Fori(1, GROUPS) as i:
                st.enter(i - 1, PER)
                drive(mix0(i - 1), *group0(i))
            st.leave(GROUPS - 1)
            for u in range(LEAD):
                split(P_OUT0, u, WIDE)
            for _ in mix0(GROUPS - 1):
                pass
            dve.sem_inc(S("ws_free"), 1)

            def wide(n, units):
                return units, (lambda u: split(n + u // UNITS, u % UNITS, WIDE))

            def out_hook(n, b0):
                def hook(j, late):
                    if not late:
                        add_residual(n + j, j, (b0 + j) % 2)
                return hook

            dve.wait_ge(S("x_scaled"), 1)
            drive([], *wide(P_OUT0, 4 * UNITS), out_hook(P_OUT0, 0), stop != 1, begun=True)
            layer_norm(0, P_OUT0 + 3)
            x_low(1)
            if stop == 1:
                dve.wait_ge(S("xlo"), 16)
                dve.sem_inc(S("ln_done"), 1)
                return

            def mlp(n0, k, b0):
                def body(f_, ahead):
                    n = f_ * 8 + n0

                    def hook(j, late):
                        if j < 4 and late:
                            seen = f_ * 4 + (4 * FG * k + j + 1)
                            dve.wait_ge(S("hid_hi"), seen)
                            tt(hid, hid, hid, ALU.mult).then_inc(S("hid_sq"), 1)
                            dve.wait_ge(S("hid_sq"), seen)
                            tt(hTl[:, 4 * j:4 * j + 4, :], r2(hid, a=4), f(hTh[:, 4 * j:4 * j + 4, :]),
                               ALU.subtract).then_inc(S("hid_ready"), 1)
                        elif j >= 4 and not late:
                            add_residual(n + j, j - 4, (b0 + j) % 2)
                    units, one = wide(n, 8 * UNITS)
                    for u in range(units + 3):
                        between(u, units, one, hook, ahead)
                with dve.Fori(0, FG - 1) as f_:
                    body(f_, True)
                body(FG - 1, k == 0)

            dve.wait_ge(S("x_scaled"), 2)
            mlp(P_MLP0, 0, 0)
            layer_norm(1, P_MLP0 + 8 * FG - 1)
            x_low(2)
            st.leave_straight()
            dve.wait_ge(S("beta_exp"), 1)
            tt(gv, mb[0][:, 0:128].rearrange("p (c h) -> p c h", c=TT)[:, :, 32:64], rep(r1[:, 32:64], TT),
               ALU.add).then_inc(S("a_dt"), 1)
            sigmoid_tail(beta)
            dve.wait_ge(S("g_ln"), 1)
            st(stt(gv, gv, 0.0, gtmp, ALU.max, ALU.add))
            st.settle()
            stt(gv, gv, -1.0, rep(r1[:, 0:32], TT), ALU.mult, ALU.mult).then_inc(S("g_ready"), 1)
            nc.vector.memset(cbuf[:, :, 0:3], 0.0).then_inc(S("zeroed"), 1)
            dve.wait_ge(S("gsum_read"), 1)
            st(nc.vector.tensor_copy(gtmp, mb[1][:, 0:64].rearrange("p (c h) -> p c h", c=TT)))
            st.settle()
            tt(kend, mb[1][:, 64:128].rearrange("p (c h) -> p c h", c=TT), gtmp, ALU.subtract).then_inc(S("kend_log"), 1)
            dve.wait_ge(S("gates1"), 1)
            st(ts(negc, egc, -1.0, None, ALU.mult))

            def mix1(g, n, gl):
                g1 = g + 1
                head = lambda a, c, h: a[:, c, bass.ds(g * 4 + h, 1)]
                heads = lambda a: a[:, :, bass.ds(g * 4, 4)].rearrange("p c (j r) -> p c j r", r=2)
                two = lambda a: a.unsqueeze(3).to_broadcast([P, TT, 2, 2])
                dve.wait_ge(S("evacuated"), n + 5)
                dve.wait_ge(S("conv_first"), g1)
                for tap in range(3):
                    for j in range(8):
                        last = stt(qkv[:, j, :], cbuf[:, j, tap:T + tap], cw[:, bass.ds(g, 1), 4 * j + tap], qkv[:, j, :],
                                   ALU.mult, ALU.add)
                        if j < 7 or tap < 2:
                            st(last)
                    if tap == 2:
                        last.then_inc(S("conv"), 1)
                    else:
                        st.settle()
                    yield
                dve.wait_ge(S("e_qkv"), g1)
                st(ts(E1, E1, 1e30, 1.0, ALU.min, ALU.add))
                st.settle()
                yield
                st(nc.vector.reciprocal(E1, E1))
                st.settle()
                yield
                tt(qkv, qkv, E1, ALU.mult).then_inc(S("qkv_act"), 1)
                dve.wait_ge(S("e_z"), g1)
                st(ts(SQ, SQ, 1e30, 1.0, ALU.min, ALU.add))
                st.settle()
                yield
                st(nc.vector.reciprocal(SQ, SQ))
                st.settle()
                st(nc.vector.memset(S1, 0.0))
                dve.wait_ge(S("qkv_act"), g1)
                tt(zs, zs, SQ, ALU.mult).then_inc(S("zs_ready"), 1)
                yield
                for c in range(TT):
                    for h in range(4):
                        last = ts(UTg[:, c, h, :], UT, head(gv, c, h), None, ALU.mult)
                        if c * 4 + h < 7:
                            st(last)
                last.then_inc(S("utg"), 1)
                dve.wait_ge(S("cols"), g1)
                w4 = wc.rearrange("p c (j r) -> p c j r", r=2)
                st(tt(w4, heads(beta), two(wkc), ALU.mult))
                st.settle()
                st(tt(wke.rearrange("p c (j r) -> p c j r", r=2), w4, heads(kend), ALU.mult))
                yield
                yield
                dve.wait_ge(S("kq"), g1)
                for c in range(TT):
                    st(tt(KQ[:, c, :, :, :].rearrange("p j w t -> p j (w t)"), r2(mb[c][:, :], a=2), rep(gmask, 2), ALU.mult))
                yield
                dve.wait_ge(S("D"), g1)
                st.settle()
                for c in range(TT):
                    st(tt(AT[:, c, :, :].rearrange("p (j r) t -> p j r t", r=2), Dm[:, c, :, :].rearrange("p (j r) t -> p j r t", r=2),
                          KQ[:, c, :, 0:1, :].to_broadcast([P, 2, 2, P]), ALU.mult))
                    for h in range(4):
                        st(stt(At[:, c, h, :], Dm[:, c, h, :], wc[:, c, h:h + 1], KQ[:, c, h // 2, 1, :], ALU.mult, ALU.mult))
                st.settle()
                st(tt(XT1, At.rearrange("p c h t -> p (c h) t"), rep(cc[:, C_M0:C_M0 + P], 8), ALU.mult))
                st.settle()
                tt(XT1, XT1, rep(ident, 8), ALU.add).then_inc(S("XT1_first"), 1)
                yield
                yield
                for lv in range(1, 7):
                    s_ = 1 << lv
                    dve.wait_ge(S("AX1"), 6 * g + lv)
                    tt(Yn1, r2(mb[0][:, :], a=8), rep(cc[:, C_LV + 64 * (lv - 1):C_LV + 64 * lv], 8),
                       ALU.mult).then_inc(S("Yn1"), 1)
                    yield
                    dve.wait_ge(S("dX1"), 6 * g + lv)
                    left = X1.rearrange("p a (b w s) -> p a b w s", w=2, s=s_)[:, :, :, 0, :]
                    tt(left, left, mb[1][:, :].rearrange("p (a b s) -> p a b s", a=8, s=s_), ALU.add).then_inc(S("X1_ready"), 1)
                    yield
                    yield
                for c in range(TT):
                    nn = 2 * g + c
                    if c == 0:
                        st(nc.vector.memset(sqj, 0.0))
                        nc.vector.memset(oss, 0.0).then_inc(S("state1"), 1)
                    dve.wait_ge(S("kS"), nn + 1)
                    for h in range(4):
                        last = stt(yp[:, h, :], mb[0][:, h * P:(h + 1) * P], head(negc, c, h), vs[:, c, h, :], ALU.mult, ALU.add)
                        if h < 3:
                            st(last)
                    last.then_inc(S("yp"), 1)
                    yield
                    dve.wait_ge(S("vk"), nn + 1)
                    for h in range(4):
                        last = ts(vke[:, h, :], mb[2][:, h * P:(h + 1) * P], wke[:, c, h:h + 1], None, ALU.mult)
                        if h < 3:
                            st(last)
                    last.then_inc(S("vke"), 1)
                    yield
                    dve.wait_ge(S("dS1"), nn + 1)
                    for h in range(4):
                        last = stt(S1[:, h, :], S1[:, h, :], head(egl, c, h), mb[3][:, h * P:(h + 1) * P], ALU.mult, ALU.add)
                        if h < 3:
                            st(last)
                    last.then_inc(S("state1"), 1)
                    dve.wait_ge(S("o_psum"), nn + 1)
                    dve.wait_ge(S("t1"), nn + 1)
                    tt(t2, r2(mb[0][:, :], a=4), t2, ALU.add).then_inc(S("t2"), 1)
                    dve.wait_ge(S("oss"), 4 * nn + 4)
                    q2 = qsc[:, c, :].unsqueeze(2).to_broadcast([P, 2, 2])
                    o4 = lambda a: a.rearrange("p (j r) -> p j r", r=2)
                    st(stt(o4(osc), o4(oss), 1.0 / P, q2, ALU.mult, ALU.mult))
                    st.settle()
                    tt(o4(osc), o4(osc), q2, ALU.mult).then_inc(S("o_ms"), 1)
                    dve.wait_ge(S("o_rstd"), nn + 1)
                    st(tt(o4(osq), o4(osq), q2, ALU.mult))
                    st.settle()
                    for h in range(4):
                        last = ts(yp[:, h, :], t2[:, h, :], osq[:, h:h + 1], None, ALU.mult)
                        if h < 3:
                            st(last)
                    last.then_inc(S("on"), 1)
                    yield
                    dve.wait_ge(S("oT"), nn + 1)
                    stt(oT1, r2(mb[2][:, :], a=4), nw, zs[:, :, c * P:(c + 1) * P], ALU.mult, ALU.mult).then_inc(S("oTf"), 1)
                    dve.wait_ge(S("mix1_hi"), nn + 1)
                    hs = (slice(None), bass.ds(gl * 4, 4), slice(c * P, (c + 1) * P))
                    tt(hTl[hs], oT1, f(hTh[hs]), ALU.subtract).then_inc(S("mix1_out"), 1)
                    dve.wait_ge(S("mix1_out"), nn + 1)
                    yield

            PER1 = 79
            st.leave_straight()
            with dve.Fori(0, 2) as half:
                n0 = half * HALF1 + P_L1
                drive([], *wide(n0, 3 * UNITS), nothing, True)
                with dve.Fori(1, 4) as i:
                    st.enter((half * 4) + (i - 1), PER1)
                    drive(mix1(half * 4 + i - 1, n0 + (i - 1) * 3, i - 1), *wide(n0 + i * 3, 3 * UNITS), nothing, True)
                st.enter(half * 4 + 3, PER1)
                for _ in mix1(half * 4 + 3, n0 + 9, 3):
                    pass
                units, one = wide(n0 + 12, 4 * UNITS)
                dve.wait_ge(S("x_scaled"), 3)
                for u in range(units + 3):
                    between(u, units, one, out_hook(n0 + 12, 1), True)
            st.leave(8)
            dve.sem_inc(S("ws_free"), 1)
            layer_norm(2, P_MLP1 - 1)
            x_low(3)
            dve.wait_ge(S("x_scaled"), 4)
            mlp(P_MLP1, 1, 1)
            layer_norm(3, PANELS - 1)
            st.settle()
            dve.sem_inc(S("ln_done"), 1)


def constants():
    import numpy as np

    a = np.arange(P)
    s, t = a[:, None], a[None, :]
    cc = np.zeros((P, C_SHARED), np.float32)
    cc[:, C_ID:C_ID + P] = s == t
    cc[:, C_ONES:C_ONES + P] = 1
    for lv in range(1, 7):
        w = 1 << lv
        cols = a.reshape(-1, 2, w)[:, 0, :].reshape(-1)[None, :]
        same = (s // (2 * w) == cols // (2 * w)) & (s // w % 2 == 1)
        cc[:, C_LV + 64 * (lv - 1):C_LV + 64 * lv] = -1.0 * same
    cc[:, C_M0:C_M0 + P] = -1.0 * ((s // 2 == t // 2) & (s < t))
    c0 = np.zeros((P, C0_N), np.float32)
    q = np.arange(T)[None, :]
    keep = np.concatenate([s < q, s < t], axis=1)
    c0[:, C0_SB:C0_SB + 384] = -1.0 * keep
    c0[:, C0_BIG:C0_BIG + 384] = np.where(keep, 0.0, -1e30)
    c0[:, C0_TRI:C0_TRI + P] = s >= t
    block = s // 64 == t // 64
    c0[:, C0_BO:C0_BO + P] = block
    c0[:, C0_BO64:C0_BO64 + P] = block / 64.0
    c0[:, C0_RW:C0_RW + P] = block & (s < t)
    c0[:, C0_RW + P:C0_RW + 2 * P] = block & (s <= t)
    c0[:, C0_RST:C0_RST + T] = q % 64 != 0
    c1 = np.zeros((P, C1_N), np.float32)
    c1[:, C1_GM:C1_GM + P] = s <= t
    c1[:, C1_GM + P:C1_GM + 2 * P] = s < t
    c1[:, C1_SL:C1_SL + P] = s > t
    return cc, c0, c1


def layout(x, ev_w_in, ev_shift, ev_w0, ev_w_up, ev_a0, ev_a_up, ev_g_up, ev_k_k, ev_k_a, ev_r_k, ev_lnx_g, ev_lnx_b,
           vres_w_down, vres_shift, vres_v0, vres_v_up, ev_w_out, od_w_in, od_conv, od_a_log, od_dt_bias, od_norm_w,
           od_w_out, ln1_g, ln1_b, mlp_w1, mlp_w2, ln2_g, ln2_b):
    import numpy as np

    def fill(dst, w):
        dst[:, :, :w.shape[1]] = w.reshape(KT, P, w.shape[1]).transpose(1, 0, 2)

    w384 = np.zeros((P_OUT0, P, KT, NARROW), np.float32)
    w = ev_w_in[0]
    fill(w384[0], w[:, 6144:])
    for i in range(GROUPS):
        for b in range(3):
            for n, base in ((1 + 2 * i, 3072), (2 + 2 * i, 0)):
                c = base + 1024 * b + P * i
                fill(w384[n][:, :, b * P:(b + 1) * P], w[:, c:c + P])
    w512 = np.empty((PANELS - P_OUT0, P, KT, WIDE), np.float32)
    at = 0

    def put(w):
        nonlocal at
        fill(w512[at], w)
        at += 1

    def put_mlp(k):
        for f in range(FG):
            for j in range(4):
                put(mlp_w1[k][:, f * D + j * WIDE:f * D + (j + 1) * WIDE])
            for j in range(4):
                put(mlp_w2[k][f * D:(f + 1) * D, j * WIDE:(j + 1) * WIDE])

    for j in range(4):
        put(ev_w_out[0][:, j * WIDE:(j + 1) * WIDE])
    put_mlp(0)
    w = od_w_in[0]
    for half in range(2):
        for g in range(4 * half, 4 * half + 4):
            fill(w512[at][:, :, 0:256], w[:, 256 * g:256 * g + 256])
            fill(w512[at][:, :, 256:512], w[:, 2048 + 256 * g:2048 + 256 * g + 256])
            at += 1
            put(w[:, 4096 + 512 * g:4096 + 512 * g + 512])
            put(w[:, 8192 + 512 * g:8192 + 512 * g + 512])
        for j in range(4):
            put(od_w_out[0][half * D:(half + 1) * D, j * WIDE:(j + 1) * WIDE])
    put_mlp(1)
    assert at == PANELS - P_OUT0
    wba = np.ascontiguousarray(w[:, 12288:].reshape(KT, P, 64).transpose(1, 0, 2))

    prm0 = np.zeros((P, GROUPS * 10 + 3), np.float32)
    vecs = [ev_shift[0][0:1024], ev_shift[0][1024:2048], ev_shift[0][2048:3072], ev_w0[0], ev_a0[0], ev_k_k[0], ev_k_a[0],
            ev_r_k[0].reshape(-1), ev_lnx_g[0], ev_lnx_b[0]]
    for j, v in enumerate(vecs):
        prm0[:, j:GROUPS * 10:10] = v.reshape(GROUPS, P).T
    lo = np.zeros(384, np.float32)
    lo[:288] = ev_shift[0][3072:]
    prm0[:, GROUPS * 10:] = lo.reshape(3, P).T
    lora = np.zeros((GROUPS, P, 3, P), np.float32)
    for m in range(GROUPS):
        c = slice(m * P, (m + 1) * P)
        lora[m, 0:64, 0], lora[m, 64:, 0] = ev_w_up[0][:, c], ev_a_up[0][:, c]
        lora[m, :, 1], lora[m, 0:32, 2] = ev_g_up[0][0:P, c], ev_g_up[0][P:, c]
    conv = np.zeros((P, GROUPS, 8, 4), np.float32)
    for g in range(GROUPS):
        for j in range(8):
            c = (256 * g + P * j, 2048 + 256 * g + P * (j - 2), 4096 + 512 * g + P * (j - 4))[(j >= 2) + (j >= 4)]
            conv[:, g, j] = od_conv[0][:, c:c + P].T
    rows1 = np.concatenate([od_a_log, od_dt_bias], axis=1)
    ln = np.stack([ln1_g[0], ln1_b[0], ln2_g[0], ln2_b[0], ln1_g[1], ln1_b[1], ln2_g[1], ln2_b[1]])
    cc, c0, c1 = constants()
    return {"x": x[0], "w384": w384, "w512": w512, "wba": wba, "consts": cc, "c0": c0, "c1": c1, "prm0": prm0,
            "lora": lora.reshape(GROUPS, P, 3 * P), "conv": conv.reshape(P, GROUPS * 32), "rows1": rows1,
            "normw": np.ascontiguousarray(od_norm_w[0].reshape(P, 1)), "ln": ln}


STOP = 0


def kernel(**inputs):
    import numpy as _np
    import concourse.bacc as _bacc
    from concourse import mybir as _mybir
    from concourse.bass_utils import run_bass_kernel_spmd as _run

    nc = _bacc.Bacc("TRN2", target_bir_lowering=False, num_devices=1)
    laid = layout(**{k: _np.asarray(v) for k, v in inputs.items()})
    arrays, args = {}, {}
    for name, a in laid.items():
        a = _np.ascontiguousarray(a)
        arrays[f"in_{name}_dram"] = a
        args[name] = nc.dram_tensor(f"in_{name}_dram", a.shape, _mybir.dt.from_np(a.dtype), kind="ExternalInput").ap()
    args["out"] = nc.dram_tensor("out_0_dram", (T, D), _mybir.dt.float32, kind="ExternalOutput").ap()
    trunk(nc, STOP, **args)
    r = _run(nc, [arrays], core_ids=[0])
    return r.results[0]["out_0_dram"].reshape(1, T, D)
```

```python
from contextlib import ExitStack

import concourse.bass as bass
from concourse import mybir

F32 = mybir.dt.float32
F32R = mybir.dt.float32r
ALU = mybir.AluOpType
ACT = mybir.ActivationFunctionType

P = 128
D = 2048
T = 256
KT = D // P
TT = T // P
UK = 2
UNITS = KT // UK
RING = 4
WIDE = 512
NARROW = 384
GROUPS = 8
FF = 4 * D
FG = FF // D
ALPHA = 4.0 ** 0.25
LN_EPS = 1e-5
LNX_EPS = 64e-5
KK_EPS = 1e-12
SB_SCALE = 128.0 ** -0.5
LEAD = 2

P_GROUPS0 = 1
P_OUT0 = P_GROUPS0 + 2 * GROUPS
P_MLP0 = P_OUT0 + 4
P_L1 = P_MLP0 + 8 * FG
P_OUT1A = P_L1 + 3 * 5
P_L1B = P_OUT1A + 4
P_OUT1B = P_L1B + 3 * 3
P_MLP1 = P_OUT1B + 4
PANELS = P_MLP1 + 8 * FG
B_OUT0 = P_OUT0
B_MLP0 = B_OUT0 + 8
B_L1 = B_MLP0 + 8 * FG
B_OUT1A = B_L1 + 3 * 5
B_L1B = B_OUT1A + 4
B_OUT1B = B_L1B + 3 * 3
B_MLP1 = B_OUT1B + 8
Y0, Y1 = 28, 31

C_ID, C_ONES, C_LV, C_M0 = 0, 128, 256, 640
C_SHARED = 768
C0_SB, C0_BIG, C0_TRI, C0_BO, C0_BO64, C0_RW, C0_RST = 0, 384, 768, 896, 1024, 1152, 1408
C0_N = 1664
C1_GM, C1_SL = 0, 256
C1_N = 384
WS = 53215 - 36864 - C_SHARED - 32


class Steps:

    def __init__(self, eng, sem):
        self.eng, self.sem, self.total, self.n, self.base, self.per = eng, sem, 0, 0, 0, None

    def enter(self, i, per):
        self.base, self.per, self.n = i * per + self.total, per, 0

    def __call__(self, ins):
        self.n += 1
        return ins.then_inc(self.sem, 1)

    def settle(self):
        self.eng.wait_ge(self.sem, self.base + self.n)

    def leave(self, times):
        assert self.n == self.per, f"the body has {self.n} steps, {self.per} declared"
        self.total += times * self.per
        self.base, self.n, self.per = self.total, 0, None

    def leave_straight(self):
        self.total += self.n
        self.base, self.n = self.total, 0


def interleave(mixer, hops, units, one, ends, hook, ahead, begun=False, late=None, u0=0):
    if not begun:
        for u in range(LEAD):
            one(u0 + u)
    wait = 1 if mixer else 2
    hops = hops if mixer else units
    for y in range(hops + wait + 1):
        if mixer and y < hops:
            next(mixer)
        for u in range(units):
            if 2 * u * hops // (2 * units) == y and (ahead or u + LEAD < units):
                one(u0 + u + LEAD)
        for j, e in enumerate(ends):
            after = y - (2 * e + 1) * hops // (2 * units) - wait
            if after in (0, 1):
                hook(j, after)
    if mixer:
        assert next(mixer, "over") == "over"
    if late:
        late()


class Lay:

    def __init__(self, ws, at=0):
        self.ws, self.at = ws, at

    def __call__(self, n):
        self.at += n
        assert self.at <= WS, self.at
        return self.ws[:, self.at - n:self.at]


def trunk(nc, stop, x, w384, w512, wba, consts, c0, c1, prm0, lora, conv, rows1, normw, ln, out):
    ctx = ExitStack()
    with ctx:
        def sb(name, shape, dt=F32):
            return ctx.enter_context(nc.sbuf_tensor(name, shape, dt))

        sems = {}

        def S(name):
            if name not in sems:
                sems[name] = ctx.enter_context(nc.semaphore(name))
            return sems[name]

        raw = sb("raw", [P, UNITS, UK, WIDE])
        wh = sb("wh", [P, RING, UK, WIDE], F32R)
        wl = sb("wl", [P, RING, UK, WIDE], F32R)
        xres = sb("xres", [P, TT, D])
        aTh = sb("aTh", [P, KT, T], F32R)
        aTl = sb("aTl", [P, KT, T], F32R)
        hTh = sb("hTh", [P, KT, T], F32R)
        hTl = sb("hTl", [P, KT, T], F32R)
        cc = sb("cc", [P, C_SHARED])
        ws = sb("ws", [P, WS])
        small = sb("small", [P, 16])
        pp = [ctx.enter_context(nc.psum_tensor(f"pp{b}", [P, 2 * WIDE], F32)) for b in range(2)]
        mb = [ctx.enter_context(nc.psum_tensor(f"mb{b}", [P, WIDE], F32)) for b in range(4)]

        ident = cc[:, C_ID:C_ID + P]
        ones = cc[:, C_ONES:C_ONES + P]
        eps_ln, eps_lnx, eps_kk, eps_l2, ln_qs = (small[:, j:j + 1] for j in range(5))
        mv = small[:, 8:12].rearrange("p (t s) -> p t s", t=TT)
        rstd = small[:, 12:14]
        nmean = small[:, 5:7]

        def r2(ap, **kw):
            return ap.rearrange("p (a b) -> p a b", **kw)

        lay = Lay(ws)
        lng = lay(D)
        lnb = lay(D)
        stats = lay(TT * 4 * 6).rearrange("p (t c s) -> p t c s", t=TT, c=4)
        hid = lay(2 * WIDE)
        wba_sb = r2(Lay(ws, 2 * D + 64 + 1024)(KT * 64), a=KT)

        lay = Lay(ws)
        k0 = lay(C0_N)
        sbneg, sbbig = k0[:, C0_SB:C0_SB + 384], k0[:, C0_BIG:C0_BIG + 384]
        tri, bo, bo64 = (k0[:, c:c + P] for c in (C0_TRI, C0_BO, C0_BO64))
        rwmask, rst = k0[:, C0_RW:C0_RW + 256], k0[:, C0_RST:C0_RST + 256]
        pb = r2(lay(3 * (T + 1)), a=3)
        sbq = r2(lay(3 * T), a=3)
        rkv = r2(lay(3 * T), a=3)
        loT = r2(lay(3 * T), a=3)
        lw = r2(lay(3 * P), a=3)
        prmf = lay(GROUPS * 10 + 3)
        prm = r2(prmf[:, 0:GROUPS * 10], a=GROUPS)
        mulo = prmf[:, GROUPS * 10:GROUPS * 10 + 3]
        nprm = r2(lay(GROUPS * 2), a=GROUPS)
        ew = lay(2 * T)
        sigw, av = ew[:, 0:T], ew[:, T:2 * T]
        Lg, cum = lay(T), lay(T)
        p3 = lay(3 * T)
        pinc, pinv, pexc = (p3[:, j * T:(j + 1) * T] for j in range(3))
        yT, yc, yn = pinv, pexc, Lg
        kk0, k2 = lay(T), lay(T)
        KR = lay(2 * T).rearrange("p (t w c) -> p t w c", t=TT, w=2)
        bt, kt_, gg, rk = lay(T), lay(T), lay(T), lay(T)
        tok = lay(4 * T).rearrange("p (w t c) -> p w t c", w=4, t=TT)
        GMf = lay(2048)
        GM = GMf.rearrange("p (t h w r c) -> p t h w r c", t=TT, h=2, w=2, r=2)
        dsh = r2(GMf[:, 0:3 * T], a=3)
        lobuf = r2(GMf[:, 3 * T:3 * T + 3 * (T + 1)], a=3)
        ksq = GMf[:, 3 * T:4 * T]
        kkt = GMf[:, 4 * T:5 * T]
        X0 = r2(lay(4 * P), a=4)
        XT0 = r2(lay(4 * P), a=4)
        Yn0 = r2(lay(4 * 64), a=4)
        Sa, Sb, U = (lay(P) for _ in range(3))
        vtk = r2(lay(T), a=TT)
        sba, sbb, sbc = (lay(384) for _ in range(3))
        AVs, Un = sba[:, 0:T], sbb[:, 0:T]
        dS0, pcS = sbc[:, 0:P], sbc[:, P:2 * P]

        lay = Lay(ws)
        k1 = lay(C1_N)
        gmask, SL = k1[:, C1_GM:C1_GM + 256], k1[:, C1_SL:C1_SL + P]
        UT = gmask[:, 0:P]
        cbuf = r2(lay(8 * (T + 3)), a=8)
        zs = r2(lay(4 * T), a=4)
        qkv = r2(lay(8 * T), a=8)
        Ef = lay(2048)
        E1 = r2(Ef, a=8)
        AT = Ef[:, 0:1024].rearrange("p (c h t) -> p c h t", c=TT, h=4)
        At = Ef[:, 1024:2048].rearrange("p (c h t) -> p c h t", c=TT, h=4)
        Df = lay(1024)
        SQ = r2(Df, a=4)
        Dm = Df.rearrange("p (c h t) -> p c h t", c=TT, h=4)
        KQf = lay(1024)
        KQ = KQf.rearrange("p (c j w t) -> p c j w t", c=TT, j=2, w=2)
        Xf = lay(1024)
        X1 = r2(Xf, a=8)
        UTg = Xf.rearrange("p (c h t) -> p c h t", c=TT, h=4)
        XT1 = r2(lay(1024), a=8)
        ktok = lay(512).rearrange("p (c j t) -> p c j t", c=TT, j=2)
        vs = lay(1024).rearrange("p (c h t) -> p c h t", c=TT, h=4)
        Yn1 = r2(lay(512), a=8)
        oT1 = r2(Yn1.rearrange("p a b -> p (a b)"), a=4)
        S1 = r2(lay(512), a=4)
        yp = r2(Df[:, 0:512], a=4)
        vk = r2(Df[:, 512:1024], a=4)
        vke = r2(KQf[:, 0:512], a=4)
        os = (r2(KQf[:, 512:1024], a=4), r2(Ef[:, 1024:1536], a=4))
        on = r2(Ef[:, 1536:2048], a=4)
        gates = lay(7 * 64).rearrange("p (s c h) -> p s c h", s=7, c=TT)
        beta, gv, negc, egc, kend, egl, gtmp = (gates[:, s] for s in range(7))
        colk = lay(48)
        ssc = colk[:, 0:8].rearrange("p (c j) -> p c j", c=TT)
        lnss = colk[:, 8:16].rearrange("p (c j) -> p c j", c=TT)
        qsc = colk[:, 16:20].rearrange("p (c j) -> p c j", c=TT)
        skc = colk[:, 20:24].rearrange("p (c j) -> p c j", c=TT)
        wkc = colk[:, 24:28].rearrange("p (c j) -> p c j", c=TT)
        wc = colk[:, 28:36].rearrange("p (c h) -> p c h", c=TT)
        wke = lay(8).rearrange("p (c h) -> p c h", c=TT)
        oss = colk[:, 36:40]
        osc = colk[:, 40:44]
        osq = lay(4)
        cw = r2(lay(GROUPS * 32), a=GROUPS)
        r1 = lay(64)
        nw = lay(1)
        sqj = lay(P)

        block = ctx.enter_context(nc.Block())

        @block.sync
        def _(sp):
            sp.dma_start(xres[:, :, :], x.rearrange("(t p) d -> p t d", p=P)).then_inc(S("x_in"), 16)
            sp.dma_start(cc[:, :], consts).then_inc(S("consts_in"), 16)
            sp.dma_start(k0, c0).then_inc(S("c0_in"), 16)
            sp.dma_start(prmf, prm0).then_inc(S("prm_in"), 16)

            def load(n, src, width):
                for q in range(UNITS):
                    sp.wait_ge(S("lo_ready"), n * UNITS + (q + 1))
                    sp.dma_start(raw[:, q, :, 0:width], src[:, q, :, :]).then_inc(S(f"landed{q}"), 16)

            with sp.Fori(0, P_OUT0) as i:
                load(i, w384[bass.ds(i * UNITS, UNITS)].rearrange("q p k c -> p q k c"), NARROW)
            with sp.Fori(0, 4 if stop == 1 else PANELS - P_OUT0) as i:
                load(i + P_OUT0, w512[bass.ds(i * UNITS, UNITS)].rearrange("q p k c -> p q k c"), WIDE)
            o = out.rearrange("(t p) d -> p t d", p=P)
            for t in range(TT):
                sp.wait_ge(S("x_ready"), (2 if stop == 1 else 14) + 2 * t)
                sp.dma_start(o[:, t, :], xres[:, t, :]).then_inc(S("stored"), 16)
            sp.wait_ge(S("stored"), 16 * TT)

        @block.gpsimd
        def _(pool):
            def scale_residual(k):
                pool.wait_ge(S("x_transposed"), k)
                nc.gpsimd.tensor_scalar(xres[:, :, :], xres[:, :, :], ALPHA, None, ALU.mult).then_inc(S("x_scaled"), 1)

            def load_ln(k):
                pool.wait_ge(S("ws_free"), k + 1)
                pool.dma_start(lng, ln[2 * k:2 * k + 1, :].partition_broadcast(P)).then_inc(S("ln_in"), 16)
                pool.dma_start(lnb, ln[2 * k + 1:2 * k + 2, :].partition_broadcast(P)).then_inc(S("ln_in"), 16)

            scale_residual(1)
            with pool.Fori(0, GROUPS) as i:
                pool.wait_ge(S("lora_used"), i + 1)
                pool.dma_start(lw, lora[bass.ds(i, 1)].rearrange("a p (w c) -> p (a w) c", w=3)).then_inc(S("lora_in"), 16)
            load_ln(0)
            if stop == 1:
                return
            scale_residual(2)
            load_ln(1)
            pool.dma_start(wba_sb, wba).then_inc(S("wba_in"), 16)
            scale_residual(3)
            pool.wait_ge(S("ba_out"), 1)
            pool.dma_start(k1, c1).then_inc(S("c1_in"), 16)
            pool.dma_start(cw, conv).then_inc(S("c1_in"), 16)
            pool.dma_start(r1, rows1.partition_broadcast(P)).then_inc(S("c1_in"), 16)
            pool.dma_start(nw, normw).then_inc(S("c1_in"), 16)
            load_ln(2)
            scale_residual(4)
            load_ln(3)

        @block.tensor
        def _(pe):
            mm = nc.tensor.matmul

            def unit(n, u, mode, act, buf, width, ks, first=None, end=False, half=None, ready=None):
                ah, al = act
                if first is not None and half != 1:
                    pe.wait_ge(S("evacuated"), first)
                if half != 1:
                    pe.wait_ge(S("lo_ready"), n * UNITS + (u + 1 + UNITS))
                if ready is not None and half != 1:
                    pe.wait_ge(S("hid_ready"), ready)
                slot = u % RING
                halves = (0, 1) if half is None else (half,)
                for j in range(width // P if mode == "B" else TT):
                    for kk in halves:
                        k = ks[kk]
                        c = slice(j * P, (j + 1) * P)
                        if mode == "B":
                            o = pp[buf][:, j * T:(j + 1) * T]
                            pairs = [(wh[:, slot, kk, c], ah[:, k, :]), (wh[:, slot, kk, c], al[:, k, :]),
                                     (wl[:, slot, kk, c], ah[:, k, :])]
                            opens = first is not None and kk == 0 and j % 2 == 0
                        else:
                            o = pp[buf][:, j * WIDE:(j + 1) * WIDE]
                            pairs = [(ah[:, k, c], wh[:, slot, kk, :]), (ah[:, k, c], wl[:, slot, kk, :]),
                                     (al[:, k, c], wh[:, slot, kk, :])]
                            opens = first is not None and kk == 0
                        for m, (lhs, rhs) in enumerate(pairs):
                            last = mm(o, lhs, rhs, start=opens and m == 0, stop=end and kk == 1 and m == 2,
                                      skip_group_check=True)
                if half != 0:
                    last.then_inc(S("unit_used"), 1)

            def blocks(n, b, mode, act, bufs, width, per=UNITS, u0=0, k0=0, lag=2):
                def one(u, half=None):
                    j, q = divmod(u - u0, per)
                    unit(n, u, mode, act, bufs[j], width, (k0 + 2 * q, k0 + 2 * q + 1),
                         first=b + (j + 3 - (lag if j == 0 else 2)) if q == 0 else None, end=q == per - 1, half=half)
                return one

            def drive(one, units, u0=0, mixer=None, hops=0):
                if mixer is None:
                    for u in range(units):
                        one(u0 + u)
                    return
                for y in range(hops):
                    next(mixer)
                    for h in range(2 * units):
                        if h * hops // (2 * units) == y:
                            one(u0 + h // 2, h % 2)
                assert next(mixer, "over") == "over"

            A, H = (aTh, aTl), (hTh, hTl)

            def transposes(k):
                for t in range(TT):
                    for c in range(4):
                        if k and c % 2 == 0:
                            pe.wait_ge(S("x_ready"), 4 * (k - 1) + 2 * t + c // 2 + 1)
                        r = TT * 4 * k + 4 * t + c
                        if r >= 4:
                            pe.wait_ge(S("xlo"), r - 3)
                        for e in range(4):
                            last = nc.tensor.transpose(mb[c][:, e * P:(e + 1) * P],
                                                       xres[:, t, (4 * c + e) * P:(4 * c + e + 1) * P], ident)
                        if t == TT - 1 and c == 3:
                            last.then_inc(S("x_transposed"), 1)
                        else:
                            last.then_inc(S("xT"), 1)

            pe.sem_inc(S("unit_used"), RING)
            pe.sem_inc(S("evacuated"), 2)
            pe.sem_inc(S("lora_used"), 1)
            pe.sem_inc(S("rw_o"), 1)
            pe.sem_inc(S("hid_ready"), 1)
            pe.wait_ge(S("consts_in"), 16)
            pe.wait_ge(S("x_in"), 16)
            transposes(0)
            pe.wait_ge(S("xlo"), 8)
            drive(blocks(0, 0, "B", A, (1,), NARROW), UNITS)

            def mix0(m):
                m1 = m + 1
                pe.wait_ge(S("lora_in"), 16 * m1)
                pe.wait_ge(S("rw_o"), m1)
                pe.wait_ge(S("lo_acts"), 1)
                mm(mb[0][:, 0:T], lw[0:64, 0, :], loT[0:64, 0, :], start=True, stop=True)
                mm(mb[1][:, 0:T], lw[64:P, 0, :], loT[64:P, 0, :], start=True, stop=True)
                mm(mb[0][:, T:2 * T], lw[:, 1, :], loT[:, 1, :], start=True, stop=False, skip_group_check=True)
                mm(mb[0][:, T:2 * T], lw[0:32, 2, :], loT[0:32, 2, :], start=False, stop=True,
                   skip_group_check=True).then_inc(S("lora_used"), 1)
                pe.wait_ge(S("evacuated"), 2 * m + (2 + P_GROUPS0 + 2))
                nc.tensor.transpose(mb[1][:, T:T + P], sbq[:, 2, 0:P], ident)
                nc.tensor.transpose(mb[1][:, T + P:2 * T], sbq[:, 2, P:T], ident)
                mm(mb[3][:, 0:T], sbq[:, 1, 0:P], sbq[:, 0, :], start=True, stop=True, skip_group_check=True)
                mm(mb[3][:, T:T + P], sbq[:, 1, P:T], sbq[:, 0, P:T], start=True, stop=True,
                   skip_group_check=True).then_inc(S("scores"), 1)
                yield
                pe.wait_ge(S("ksq"), m1)
                pe.wait_ge(S("vtk"), m1)
                mm(mb[1][:, 0:T], bo, ksq, start=True, stop=True, skip_group_check=True).then_inc(S("kss"), 1)
                yield
                pe.wait_ge(S("lkeep"), m1)
                mm(mb[2][:, 0:384], tri, sbb, start=True, stop=False, skip_group_check=True)
                mm(mb[2][:, P:T], ones, sbb[:, T:384], start=False, stop=True, skip_group_check=True).then_inc(S("lcum"), 1)
                yield
                pe.wait_ge(S("attn"), m1)
                mm(mb[3][:, 0:T], vtk[:, 0, :], sba[:, 0:T], start=True, stop=False, skip_group_check=True)
                mm(mb[3][:, P:T], vtk[:, 1, :], sba[:, T:384], start=False, stop=True,
                   skip_group_check=True).then_inc(S("sb_o"), 1)
                yield
                pe.wait_ge(S("operands"), m1)
                for t in range(TT):
                    for h in range(2):
                        hr = slice(64 * h, 64 * h + 64)
                        for w, src in enumerate((bt, kt_)):
                            if t == 1 and h == 0 and w == 0:
                                pe.wait_ge(S("sb_lo"), m1)
                            last = mm(mb[2 * t + h][:, w * T:(w + 1) * T], src[hr, t * P:(t + 1) * P],
                                      KR[hr, t, :, :], start=w == 0, stop=True, skip_group_check=True)
                    last.then_inc(S("gram"), 1)
                yield
                pe.wait_ge(S("masked"), 2 * m + 1)
                for w, src in enumerate((bt, kt_, rkv[:, 2, :], None)):
                    for t in range(TT):
                        e = 2 * w + t
                        src_t = KR[:, t, 0, :] if src is None else src[:, t * P:(t + 1) * P]
                        last = nc.tensor.transpose(mb[e // 4][:, (e % 4) * P:(e % 4 + 1) * P], src_t, ident)
                last.then_inc(S("tokT"), 1)
                yield
                pe.wait_ge(S("XT_first"), m1)
                for p in range(4):
                    last = nc.tensor.transpose(mb[2][:, p * P:(p + 1) * P], XT0[:, p, :], ident)
                last.then_inc(S("Xnew"), 1)
                pe.wait_ge(S("tok_ready"), m1)
                for p in range(4):
                    last = mm(mb[1][:, p * 64:(p + 1) * 64], GM[:, p // 2, p % 2, 1, 0, :],
                              tok[:, 2, p // 2, 64 * (p % 2):64 * (p % 2) + 64], start=p == 0, stop=True,
                              skip_group_check=True)
                last.then_inc(S("AV"), 1)
                yield

                def a_times_x(lv):
                    s = 1 << lv
                    for p in range(4):
                        Xp = X0[:, p, :].rearrange("p (b w s) -> p b w s", w=2, s=s)
                        last = mm(mb[3][:, p * 64:(p + 1) * 64], GM[:, p // 2, p % 2, 0, 0, :], Xp[:, :, 0, :],
                                  start=p == 0, stop=True, skip_group_check=True)
                    last.then_inc(S("AX"), 1)

                pe.wait_ge(S("X_ready"), 6 * m + 1)
                a_times_x(1)
                yield
                for lv in range(1, 6):
                    pe.wait_ge(S("Yn"), 5 * m + lv)
                    if lv > 1:
                        pe.wait_ge(S("XT_ready"), 5 * m + lv - 1)
                    for p in range(4):
                        last = mm(mb[2][:, p * 64:(p + 1) * 64], XT0[:, p, :], Yn0[:, p, :], start=p == 0, stop=True,
                                  skip_group_check=True)
                    last.then_inc(S("dX"), 1)
                    yield
                    pe.wait_ge(S("X_ready"), 6 * m + lv + 1)
                    for p in range(4):
                        last = nc.tensor.transpose(mb[0][:, p * P:(p + 1) * P], X0[:, p, :], ident)
                    last.then_inc(S("Xnew"), 1)
                    if lv < 5:
                        a_times_x(lv + 1)
                    yield
                pe.wait_ge(S("XT_ready"), 5 * m1)
                pe.wait_ge(S("AVs"), m1)
                for p in range(4):
                    last = mm(mb[1][:, p * 64:(p + 1) * 64], XT0[:, p, :], AVs[:, p * 64:(p + 1) * 64], start=p == 0,
                              stop=True, skip_group_check=True)
                last.then_inc(S("XAV"), 1)
                for p in range(4):
                    t, h = divmod(p, 2)
                    last = mm(mb[2][64 * h:64 * h + 64, t * P:(t + 1) * P], tok[:, 3, t, 64 * h:64 * h + 64], XT0[:, p, :],
                              start=t == 0, stop=True, skip_group_check=True)
                last.then_inc(S("WT"), 1)
                yield
                for c in range(4):
                    t, hf = divmod(c, 2)
                    R = slice(64 * hf, 64 * hf + 64)
                    st_in, yc_ = (Sb, Sa)[c % 2], slice(64 * c, 64 * c + 64)
                    if c:
                        pe.wait_ge(S("state0"), 3 * m + c)
                        mm(mb[0][R, 0:P], KR[:, t, 0, R], st_in, start=True, stop=True,
                           skip_group_check=True).then_inc(S("u_psum"), 1)
                        yield
                    if c == 0:
                        pe.wait_ge(S("WT_ready"), m1)
                    pe.wait_ge(S("U"), 4 * m + c + 1)
                    if c < 3:
                        mm(mb[3][:, 0:P], tok[R, 0, t, :], U[R, :], start=True, stop=False, skip_group_check=True)
                        mm(mb[3][:, 0:P], tok[R, 1, t, :], tok[R, 2, t, :], start=False, stop=True,
                           skip_group_check=True).then_inc(S("dS"), 1)
                    if c:
                        mm(mb[2][:, yc_], st_in, KR[:, t, 1, R], start=True, stop=False, skip_group_check=True)
                    for h in range(2):
                        hs = slice(64 * h, 64 * h + 64)
                        mm(mb[2][hs, yc_], U[R, hs], GM[R, t, h, 0, 1, R], start=c == 0, stop=False, skip_group_check=True)
                        last = mm(mb[2][hs, yc_], tok[R, 2, t, hs], GM[R, t, h, 1, 1, R], start=False, stop=True,
                                  skip_group_check=True)
                    last.then_inc(S("y_psum"), 1)
                    yield
                pe.wait_ge(S("yT"), m1)
                mm(mb[0][:, 0:T], bo64, yT, start=True, stop=True, skip_group_check=True)
                mm(mb[1][:, 0:T], bo, rk, start=True, stop=True, skip_group_check=True).then_inc(S("ymean"), 1)
                yield
                pe.wait_ge(S("ysq"), m1)
                mm(mb[0][:, T:2 * T], bo64, ksq, start=True, stop=True, skip_group_check=True).then_inc(S("yvar"), 1)
                yield

            def group0(i):
                return blocks(i * 2 + P_GROUPS0, i * 2 + P_GROUPS0, "B", A, (0, 1), NARROW)

            pe.wait_ge(S("c0_in"), 16)
            drive(group0(0), 2 * UNITS)
            with pe.Fori(1, GROUPS) as i:
                drive(group0(i), 2 * UNITS, 0, mix0(i - 1), Y0)
            pe.wait_ge(S("mix0_out"), GROUPS - 1)
            drive(blocks(P_OUT0, B_OUT0, "A", H, (0, 1, 0, 1), WIDE, per=7), 28, 0, mix0(GROUPS - 1), Y0)
            pe.wait_ge(S("mix0_out"), GROUPS)
            drive(blocks(P_OUT0, B_OUT0 + 4, "A", H, (0, 1, 0, 1), WIDE, per=1, u0=28, k0=14), 4, 28)
            transposes(1)
            if stop == 1:
                return

            def mlp(n0, b0, k, par):
                pe.wait_ge(S("xlo"), 8 * k + 8)
                with pe.Fori(0, FG) as f:
                    n, b = f * 8 + n0, f * 8 + b0
                    bufs = tuple((par + j) % 2 for j in range(4))
                    drive(blocks(n, b, "B", A, bufs, WIDE), 4 * UNITS)
                    for u in range(4 * UNITS):
                        j, q = divmod(u, UNITS)
                        ready = f * 4 + (4 * FG * (k - 1) // 2 + (UK * q + 1) // 4 + 2) if j == 0 and q % 2 == 0 else None
                        unit(n, u + 4 * UNITS, "A", H, bufs[j], WIDE, (2 * q, 2 * q + 1),
                             first=b + (4 + j + 1) if q == 0 else None, end=q == UNITS - 1, ready=ready)

            mlp(P_MLP0, B_MLP0, 1, 0)
            transposes(2)
            pe.wait_ge(S("xlo"), 24)
            pe.wait_ge(S("wba_in"), 16)
            for t in range(TT):
                for k in range(KT):
                    for a in (aTh, aTl):
                        last = mm(mb[0][:, t * 64:(t + 1) * 64], a[:, k, t * P:(t + 1) * P].bitcast(F32), wba_sb[:, k, :],
                                  start=k == 0 and a is aTh and t == 0, stop=k == KT - 1 and a is aTl, skip_group_check=True)
            last.then_inc(S("ba_out"), 1)
            pe.wait_ge(S("g_ready"), 1)
            gvf = gv.rearrange("p c h -> p (c h)")
            mm(mb[1][:, 0:64], UT, gvf, start=True, stop=True, skip_group_check=True)
            mm(mb[1][:, 64:128], ones, gvf, start=True, stop=True, skip_group_check=True).then_inc(S("gsum"), 1)

            def mix1(g):
                g1 = g + 1
                for _ in range(7):
                    yield
                pe.wait_ge(S("sq"), g1)
                for c in range(TT):
                    for j in range(4):
                        last = mm(mb[0][:, 4 * c + j:4 * c + j + 1], E1[:, j, c * P:(c + 1) * P], ones[:, 0:1],
                                  start=c + j == 0, stop=True, skip_group_check=True)
                last.then_inc(S("ssq"), 1)
                for c in range(TT):
                    for j in range(2):
                        last = nc.tensor.transpose(mb[1][:, (2 * c + j) * P:(2 * c + j + 1) * P],
                                                   qkv[:, 2 + j, c * P:(c + 1) * P], ident)
                last.then_inc(S("kT"), 1)
                yield
                for c in range(TT):
                    for j in range(2):
                        last = mm(mb[2 + c][:, j * T:(j + 1) * T], qkv[:, 2 + j, c * P:(c + 1) * P],
                                  qkv[:, :, c * P:(c + 1) * P].rearrange("p (w j) t -> p j w t", j=2)[:, j, 0:2, :],
                                  start=j == 0, stop=True, skip_group_check=True)
                last.then_inc(S("kq"), 1)
                yield
                pe.wait_ge(S("ktok"), g1)
                pe.wait_ge(S("utg"), g1)
                for c in range(TT):
                    last = mm(mb[c][:, :], SL, UTg[:, c, :, :], start=True, stop=True, skip_group_check=True)
                last.then_inc(S("dlog"), 1)
                yield
                pe.wait_ge(S("KQm"), g1)
                pe.wait_ge(S("v_act"), g1)
                for c in range(TT):
                    for h in range(4):
                        last = nc.tensor.transpose(mb[2 + c][:, h * P:(h + 1) * P], qkv[:, 4 + h, c * P:(c + 1) * P], ident)
                last.then_inc(S("vT"), 1)
                yield
                pe.wait_ge(S("XT1_first"), g1)
                pe.wait_ge(S("vs"), g1)

                def transpose_x(src):
                    for p in range(8):
                        last = nc.tensor.transpose(mb[2 + p // 4][:, (p % 4) * P:(p % 4 + 1) * P], src[:, p, :], ident)
                    last.then_inc(S("X1new"), 1)

                def a_times_x(lv):
                    for p in range(8):
                        Xp = X1[:, p, :].rearrange("p (b w s) -> p b w s", w=2, s=1 << lv)
                        last = mm(mb[0][:, p * 64:(p + 1) * 64], At[:, p // 4, p % 4, :], Xp[:, :, 0, :],
                                  start=p == 0, stop=True, skip_group_check=True)
                    last.then_inc(S("AX1"), 1)

                transpose_x(XT1)
                yield
                pe.wait_ge(S("X1_ready"), 7 * g + 1)
                a_times_x(1)
                yield
                for lv in range(1, 7):
                    pe.wait_ge(S("Yn1"), 6 * g + lv)
                    if lv > 1:
                        pe.wait_ge(S("XT1_ready"), 6 * g + lv - 1)
                    for p in range(8):
                        last = mm(mb[1][:, p * 64:(p + 1) * 64], XT1[:, p, :], Yn1[:, p, :], start=p == 0, stop=True,
                                  skip_group_check=True)
                    last.then_inc(S("dX1"), 1)
                    yield
                    pe.wait_ge(S("X1_ready"), 7 * g + lv + 1)
                    transpose_x(X1)
                    if lv < 6:
                        a_times_x(lv + 1)
                    yield

                def heads(bank, lhs, rhs, name):
                    for h in range(4):
                        last = mm(bank[:, h * P:(h + 1) * P], lhs[:, h, :], rhs[:, h, :], start=h == 0, stop=True,
                                  skip_group_check=True)
                    last.then_inc(S(name), 1)

                def pairs(bank, lhs, rhs, name):
                    for j in range(2):
                        last = mm(bank[:, j * T:(j + 1) * T], lhs[:, j, :], rhs[:, 2 * j:2 * j + 2, :], start=j == 0,
                                  stop=True, skip_group_check=True)
                    last.then_inc(S(name), 1)

                pe.wait_ge(S("XT1_ready"), 6 * g1)
                heads(mb[0], XT1[:, 0:4, :], vs[:, 0, :, :], "z_psum")
                yield
                pe.wait_ge(S("vke"), g1)
                pairs(mb[3], ktok[:, 0, :, :], vke, "dS1")
                heads(mb[1], AT[:, 0, :, :], vk, "o_psum")
                yield
                pe.wait_ge(S("state1"), g1)
                pairs(mb[0], qkv[:, 2:4, P:T], S1, "kS")
                pairs(mb[2], qkv[:, 0:2, P:T], S1, "qS")
                yield
                pe.wait_ge(S("yp"), g1)
                heads(mb[3], XT1[:, 4:8, :], yp, "z_psum")
                yield
                pe.wait_ge(S("vk"), 2 * g + 2)
                pe.wait_ge(S("o0_read"), g1)
                heads(mb[1], AT[:, 1, :, :], vk, "o_psum")
                for c in range(TT):
                    pe.wait_ge(S("on"), 2 * g + c + 1)
                    if c == 0:
                        pe.wait_ge(S("t1"), g1)
                    bank = mb[2 if c == 0 else 0]
                    for h in range(4):
                        last = nc.tensor.transpose(bank[:, h * P:(h + 1) * P], on[:, h, :], ident)
                    last.then_inc(S("oT"), 1)
                    yield

            def group1(n, b):
                return blocks(n, b, "B", A, (0, 1, 0), WIDE, lag=1)

            drive(group1(P_L1, B_L1), 3 * UNITS)
            with pe.Fori(1, 5) as i:
                drive(group1(i * 3 + P_L1, i * 3 + B_L1), 3 * UNITS, 0, mix1(i - 1), Y1)
            pe.wait_ge(S("mix1_out"), 8)
            drive(blocks(P_OUT1A, B_OUT1A, "A", H, (1, 0, 1, 0), WIDE), 4 * UNITS, 0, mix1(4), Y1)
            drive(group1(P_L1B, B_L1B), 3 * UNITS)
            with pe.Fori(6, 8) as i:
                drive(group1(i * 3 + (P_L1B - 15), i * 3 + (B_L1B - 15)), 3 * UNITS, 0, mix1(i - 1), Y1)
            pe.wait_ge(S("mix1_out"), 14)
            drive(blocks(P_OUT1B, B_OUT1B, "A", H, (1, 0, 1, 0), WIDE, per=6), 24, 0, mix1(7), Y1)
            pe.wait_ge(S("mix1_out"), 16)
            drive(blocks(P_OUT1B, B_OUT1B + 4, "A", H, (1, 0, 1, 0), WIDE, per=2, u0=24, k0=12), 8, 24)
            transposes(3)
            mlp(P_MLP1, B_MLP1, 3, 1)

        @block.scalar
        def _(act):
            go = nc.scalar.activation
            st = Steps(act, S("act_steps"))

            def split(n, q, width):
                act.wait_ge(S(f"landed{q}"), n * 16 + 16)
                act.wait_ge(S("unit_used"), n * UNITS + (q + 1))
                nc.scalar.copy(wh[:, q % RING, :, 0:width], raw[:, q, :, 0:width]).then_inc(S("hi_ready"), 1)

            def x_high(k):
                for t in range(TT):
                    for c in range(4):
                        r = TT * 4 * k + 4 * t + c
                        if t == TT - 1 and c == 3:
                            act.wait_ge(S("x_transposed"), k + 1)
                        else:
                            act.wait_ge(S("xT"), 7 * k + 4 * t + c + 1)
                        nc.scalar.copy(aTh[:, 4 * c:4 * c + 4, t * P:(t + 1) * P],
                                       r2(mb[c][:, :], a=4)).then_inc(S("xhi"), 1)

            def used(n, u):
                act.wait_ge(S("unit_used"), n * UNITS + (u + 1 + RING))

            def layer_norm(k):
                for t in range(TT):
                    act.wait_ge(S("ln_var"), TT * k + t + 1)
                    st(go(rstd[:, t:t + 1], mv[:, t, 1:2], ACT.Ln, bias=eps_ln))
                    st.settle()
                    go(rstd[:, t:t + 1], rstd[:, t:t + 1], ACT.Exp, scale=-0.5).then_inc(S("ln_rstd"), 1)
                for t in range(TT):
                    act.wait_ge(S("ln_nmean"), TT * k + t + 1)
                    for h in range(2):
                        o = xres[:, t, h * 1024:(h + 1) * 1024]
                        go(o, o, ACT.Identity, scale=rstd[:, t:t + 1], bias=nmean[:, t:t + 1]).then_inc(S("xn"), 1)

            nc.scalar.preload_act_table_set("natural_log_exp_and_others")
            act.wait_ge(S("eps_ready"), 1)
            x_high(0)
            for q in range(UNITS):
                split(0, q, NARROW)
            used(0, UNITS - 1)
            act.wait_ge(S("zeroed"), 1)
            nc.scalar.copy(lobuf[:, :, 1:T + 1], r2(pp[1][:, 0:3 * T], a=3)).then_inc(S("evacuated"), 1)
            act.wait_ge(S("lo_shifted"), 1)
            st(go(loT[0:64, 0, :], loT[0:64, 0, :], ACT.Exp, scale=2.0))
            go(loT[:, 1:3, :], loT[:, 1:3, :], ACT.Exp, scale=-1.0).then_inc(S("lo_exp"), 1)

            def mix0(m):
                m1 = m + 1
                act.wait_ge(S("kk0"), m1)
                go(ksq, kk0, ACT.Square).then_inc(S("ksq"), 1)
                act.wait_ge(S("scores"), m1)
                st(go(ew[:, 0:T], mb[0][:, 0:T], ACT.Exp, scale=-1.0, bias=nprm[:, bass.ds(m, 1), 0]))
                go(ew[:, T:2 * T], mb[1][:, 0:T], ACT.Exp, scale=-1.0,
                   bias=nprm[:, bass.ds(m, 1), 1]).then_inc(S("gates_exp"), 1)
                st(go(sbb, mb[3][:, 0:384], ACT.Abs))
                st.settle()
                st(go(sbb, sbb, ACT.Exp, scale=-1.0))
                st.settle()
                go(sbb, sbb, ACT.Ln, bias=1.0).then_inc(S("softplus"), 1)
                st(nc.scalar.copy(gg, mb[0][:, T:2 * T]))
                nc.scalar.copy(vtk, r2(mb[1][:, T:2 * T], a=TT)).then_inc(S("vtk"), 1)
                yield
                act.wait_ge(S("kss"), m1)
                st(go(ksq, mb[1][:, 0:T], ACT.Ln, bias=eps_kk))
                st.settle()
                go(ksq, ksq, ACT.Exp, scale=-0.5).then_inc(S("rkk"), 1)
                act.wait_ge(S("cum"), m1)
                st(go(pinc, cum, ACT.Exp))
                st(go(pinv, cum, ACT.Exp, scale=-1.0))
                go(pexc, pexc, ACT.Exp).then_inc(S("powers"), 1)
                yield
                act.wait_ge(S("loga"), m1)
                go(sba, sba, ACT.Exp).then_inc(S("attn"), 1)
                yield
                act.wait_ge(S("sb_o"), m1)
                nc.scalar.copy(hTh[:, bass.ds(m * 2, 1), :], mb[3][:, 0:T].unsqueeze(1)).then_inc(S("sb_hi"), 1)
                yield
                yield
                act.wait_ge(S("tokT"), m1)
                st(nc.scalar.copy(tok[:, 0:2, :, :], mb[0][:, :].rearrange("p (w t c) -> p w t c", w=2, t=TT)))
                nc.scalar.copy(tok[:, 2:4, :, :], mb[1][:, :].rearrange("p (w t c) -> p w t c", w=2, t=TT)).then_inc(S("tok_ready"), 1)
                yield
                act.wait_ge(S("Xnew"), 6 * m + 1)
                nc.scalar.copy(X0, r2(mb[2][:, :], a=4)).then_inc(S("X_ready"), 1)
                act.wait_ge(S("AV"), m1)
                nc.scalar.copy(AVs, mb[1][:, 0:T]).then_inc(S("AVs"), 1)
                yield
                yield
                for lv in range(1, 6):
                    yield
                    act.wait_ge(S("Xnew"), 6 * m + lv + 1)
                    nc.scalar.copy(XT0, r2(mb[0][:, :], a=4)).then_inc(S("XT_ready"), 1)
                    yield
                act.wait_ge(S("WT"), m1)
                nc.scalar.copy(KR[:, :, 0, :], r2(mb[2][:, 0:T], a=TT)).then_inc(S("WT_ready"), 1)
                yield
                for c in range(4):
                    if c:
                        act.wait_ge(S("state0"), 3 * m + c)
                        if c < 3:
                            go(pcS, (Sb, Sa)[c % 2], ACT.Copy, scale=pinc[:, 64 * c + 63:64 * c + 64]).then_inc(S("pcS"), 1)
                        yield
                    if c == 3:
                        act.wait_ge(S("y_psum"), 4 * m1)
                        nc.scalar.copy(yT, mb[2][:, 0:T]).then_inc(S("yT"), 1)
                    yield
                act.wait_ge(S("yc"), m1)
                go(ksq, yc, ACT.Square).then_inc(S("ysq"), 1)
                yield
                act.wait_ge(S("yvar"), m1)
                st(go(ksq, mb[0][:, T:2 * T], ACT.Ln, bias=eps_lnx))
                st.settle()
                go(ksq, ksq, ACT.Exp, scale=-0.5).then_inc(S("yrstd"), 1)
                act.wait_ge(S("rw_o"), m1 + 1)
                nc.scalar.copy(hTh[:, bass.ds(m * 2 + 1, 1), :], yn.unsqueeze(1)).then_inc(S("rw_hi"), 1)
                yield

            def group0(i, first=False):
                n = i * 2 + P_GROUPS0

                def hook(j, after):
                    if after:
                        return
                    used(n, j * UNITS + UNITS - 1)
                    if j == 0:
                        if not first:
                            act.wait_ge(S("shifted"), i)
                        nc.scalar.copy(pb[:, :, 1:T + 1], r2(pp[0][:, 0:3 * T], a=3)).then_inc(S("evacuated"), 1)
                    else:
                        if not first:
                            act.wait_ge(S("scores"), i)
                        st(go(sbq[:, 0, :], pp[1][:, 0:T], ACT.Copy, scale=SB_SCALE))
                        nc.scalar.copy(sbq[:, 1:3, :], r2(pp[1][:, T:3 * T], a=2)).then_inc(S("evacuated"), 1)
                return 2 * UNITS, (lambda u: split(n + u // UNITS, u % UNITS, NARROW)), (7, 15), hook, False

            def wide(n):
                return lambda u: split(n + u // UNITS, u % UNITS, WIDE)

            def nothing(j, after):
                pass

            st.leave_straight()
            st.enter(0, 1)
            interleave(None, 0, *group0(0, True))
            st.leave(1)
            PER = 10
            with act.Fori(1, GROUPS) as i:
                st.enter(i - 1, PER)
                interleave(mix0(i - 1), Y0, *group0(i))
            st.leave(GROUPS - 1)
            st.enter(0, PER - 1)
            interleave(mix0(GROUPS - 1), Y0, 28, wide(P_OUT0), (), nothing, True)
            st.leave(1)
            interleave(None, 0, 4, wide(P_OUT0), (), nothing, stop != 1, begun=True, u0=28)
            layer_norm(0)
            x_high(1)
            if stop == 1:
                return

            def mlp(n0, b0, k, par):
                def body(f, ahead):
                    n = f * 8 + n0

                    def hook(j, after):
                        if j < 4 and after:
                            used(n, j * UNITS + UNITS - 1)
                            seen = f * 4 + (4 * FG * k + j + 1)
                            act.wait_ge(S("hid_ready"), seen)
                            go(hid, pp[(par + j) % 2][:, :], ACT.Relu).then_inc(S("evacuated"), 1)
                            act.wait_ge(S("evacuated"), f * 8 + (b0 + j + 3))
                            go(hTh[:, 4 * j:4 * j + 4, :], r2(hid, a=4), ACT.Square).then_inc(S("hid_hi"), 1)
                    interleave(None, 0, 8 * UNITS, wide(n), [UNITS * j + UNITS - 1 for j in range(8)], hook, ahead, begun=True)
                with act.Fori(0, FG - 1) as f:
                    body(f, True)
                body(FG - 1, k == 0)

            mlp(P_MLP0, B_MLP0, 0, 0)
            layer_norm(1)
            x_high(2)
            st.leave_straight()
            act.wait_ge(S("ba_out"), 1)
            act.wait_ge(S("c1_in"), 64)
            ba = mb[0][:, 0:128].rearrange("p (c h) -> p c h", c=TT)
            st(go(beta, ba[:, :, 0:32], ACT.Exp, scale=-1.0))
            go(r1[:, 0:32], r1[:, 0:32], ACT.Exp).then_inc(S("beta_exp"), 1)
            act.wait_ge(S("a_dt"), 1)
            st(go(gtmp, gv, ACT.Abs))
            st.settle()
            st(go(gtmp, gtmp, ACT.Exp, scale=-1.0))
            st.settle()
            go(gtmp, gtmp, ACT.Ln, bias=1.0).then_inc(S("g_ln"), 1)
            act.wait_ge(S("gsum"), 1)
            gc_ps = mb[1][:, 0:64].rearrange("p (c h) -> p c h", c=TT)
            gl_ps = mb[1][:, 64:128].rearrange("p (c h) -> p c h", c=TT)
            st(go(egc, gc_ps, ACT.Exp))
            go(egl, gl_ps, ACT.Exp).then_inc(S("gsum_read"), 1)
            act.wait_ge(S("kend_log"), 1)
            go(kend, kend, ACT.Exp).then_inc(S("gates1"), 1)

            def mix1(g, gl, free=None):
                g1 = g + 1
                head = lambda a, c, h: a[:, c, bass.ds(g * 4 + h, 1)]

                def conv_first(js):
                    for j in js:
                        last = go(qkv[:, j, :], cbuf[:, j, 3:T + 3], ACT.Copy, scale=cw[:, bass.ds(g, 1), 4 * j + 3])
                        if j != js[-1]:
                            st(last)
                    last.then_inc(S("conv_first"), 1)

                def softplus(dst, src, name):
                    st(go(dst, src, ACT.Abs))
                    st.settle()
                    st(go(dst, dst, ACT.Exp, scale=-1.0))
                    st.settle()
                    go(dst, dst, ACT.Ln, bias=1.0).then_inc(S(name), 1)

                def scaled(dst, bank, scale, name):
                    for h in range(4):
                        last = go(dst[:, h, :], bank[:, h * P:(h + 1) * P], ACT.Copy, scale=scale(h))
                        if h < 3:
                            st(last)
                    last.then_inc(S(name), 1)

                def mean_square(c):
                    if c:
                        act.wait_ge(S("o_sum"), g1)
                    for h in range(4):
                        go(sqj, os[c][:, h, :], ACT.Square, accum_out=oss[:, h:h + 1]).then_inc(S("oss"), 1)
                        act.wait_ge(S("oss"), 8 * g + (4 * c + h + 1))
                    act.wait_ge(S("o_ms"), 2 * g + c + 1)
                    st(go(osq, osc, ACT.Ln, bias=eps_l2))
                    st.settle()
                    go(osq, osq, ACT.Exp, scale=-0.5).then_inc(S("o_rstd"), 1)

                def out_high(c):
                    act.wait_ge(S("oTf"), 2 * g + c + 1)
                    if free is not None and c == 0:
                        used(P_OUT1A, free)
                    nc.scalar.copy(hTh[:, bass.ds(gl * 4, 4), c * P:(c + 1) * P], oT1).then_inc(S("mix1_hi"), 1)

                conv_first(range(0, 4))
                yield
                conv_first(range(4, 8))
                yield
                act.wait_ge(S("conv"), 2 * g + 1)
                softplus(E1[:, 0:4, :], qkv[:, 0:4, :], "sp_qk")
                yield
                softplus(SQ, zs, "sp_z")
                yield
                yield
                act.wait_ge(S("s_qk"), g1)
                go(E1[:, 0:4, :], E1[:, 0:4, :], ACT.Exp).then_inc(S("sig_qk"), 1)
                act.wait_ge(S("conv"), 2 * g + 2)
                softplus(E1[:, 4:8, :], qkv[:, 4:8, :], "sp_v")
                yield
                act.wait_ge(S("s_z"), g1)
                go(SQ, SQ, ACT.Exp).then_inc(S("sig_z"), 1)
                act.wait_ge(S("qk_act"), g1)
                go(E1[:, 0:4, :], qkv[:, 0:4, :], ACT.Square).then_inc(S("sq"), 1)
                yield
                act.wait_ge(S("s_v"), g1)
                go(E1[:, 4:8, :], E1[:, 4:8, :], ACT.Exp).then_inc(S("sig_v"), 1)
                act.wait_ge(S("ssq"), g1)
                st(go(lnss, r2(mb[0][:, 0:8], a=TT), ACT.Ln, bias=eps_l2))
                st.settle()
                st(go(qsc, lnss[:, :, 0:2], ACT.Exp, scale=-0.5, bias=ln_qs))
                st(go(skc, lnss[:, :, 2:4], ACT.Exp, scale=0.5))
                go(wkc, lnss[:, :, 2:4], ACT.Exp, scale=-1.0).then_inc(S("cols"), 1)
                act.wait_ge(S("kT"), g1)
                nc.scalar.copy(ktok, mb[1][:, :].rearrange("p (c j t) -> p c j t", c=TT, j=2)).then_inc(S("ktok"), 1)
                yield
                yield
                act.wait_ge(S("zs_ready"), g1)
                act.wait_ge(S("dlog"), g1)
                for c in range(TT):
                    last = go(Dm[:, c, :, :], r2(mb[c][:, :], a=4), ACT.Exp)
                    if c == 0:
                        st(last)
                last.then_inc(S("D"), 1)
                yield
                act.wait_ge(S("vT"), g1)
                act.wait_ge(S("cols"), g1)
                for c in range(TT):
                    for j in range(2):
                        last = go(vs[:, c, 2 * j:2 * j + 2, :], r2(mb[2 + c][:, j * T:(j + 1) * T], a=2), ACT.Copy,
                                  scale=skc[:, c, j:j + 1])
                        if c + j < 2:
                            st(last)
                last.then_inc(S("vs"), 1)
                yield

                def take_x(lv):
                    act.wait_ge(S("X1new"), 7 * g + lv + 1)
                    dst = XT1 if lv else X1
                    st(nc.scalar.copy(dst[:, 0:4, :], r2(mb[2][:, :], a=4)))
                    nc.scalar.copy(dst[:, 4:8, :], r2(mb[3][:, :], a=4)).then_inc(S("XT1_ready" if lv else "X1_ready"), 1)

                take_x(0)
                yield
                yield
                for lv in range(1, 7):
                    yield
                    take_x(lv)
                    yield
                act.wait_ge(S("z_psum"), 2 * g + 1)
                scaled(vk, mb[0], lambda h: wc[:, 0, h:h + 1], "vk")
                yield
                act.wait_ge(S("o_psum"), 2 * g + 1)
                nc.scalar.copy(os[0], r2(mb[1][:, :], a=4)).then_inc(S("o0_read"), 1)
                act.wait_ge(S("o0_read"), g1)
                yield
                act.wait_ge(S("qS"), g1)
                scaled(os[1], mb[2], lambda h: head(egc, 1, h), "t1")
                yield
                act.wait_ge(S("z_psum"), 2 * g + 2)
                scaled(vk, mb[3], lambda h: wc[:, 1, h:h + 1], "vk")
                mean_square(0)
                yield
                out_high(0)
                mean_square(1)
                yield
                out_high(1)
                yield

            def group1(n, before=None):
                def hook(j, after):
                    if after or j == 2:
                        return
                    used(n, j * UNITS + UNITS - 1)
                    if before is not None:
                        act.wait_ge(S("conv"), before * 2)
                    nc.scalar.copy(cbuf[:, 4 * j:4 * j + 4, 3:T + 3], r2(pp[j][:, :], a=4)).then_inc(S("evacuated"), 1)

                def z_out():
                    used(n, 3 * UNITS - 1)
                    nc.scalar.copy(zs, r2(pp[0][:, :], a=4)).then_inc(S("evacuated"), 1)
                return 3 * UNITS, wide(n), (7, 15, 23), hook, True, True, z_out

            PER1 = 37
            st.leave_straight()
            act.wait_ge(S("zeroed"), 2)
            interleave(None, 0, *group1(P_L1))
            with act.Fori(1, 5) as i:
                st.enter(i - 1, PER1)
                interleave(mix1(i - 1, i - 1), Y1, *group1(i * 3 + P_L1, i))
            st.leave(4)
            st.enter(0, PER1)
            interleave(mix1(4, 0, free=26), Y1, 4 * UNITS, wide(P_OUT1A), (), nothing, True, begun=True)
            st.leave(1)
            interleave(None, 0, *group1(P_L1B))
            with act.Fori(6, 8) as i:
                st.enter(i - 6, PER1)
                interleave(mix1(i - 1, i - 5), Y1, *group1(i * 3 + (P_L1B - 15), i))
            st.leave(2)
            st.enter(0, PER1)
            interleave(mix1(7, 3), Y1, 24, wide(P_OUT1B), (), nothing, True, begun=True)
            st.leave(1)
            interleave(None, 0, 8, wide(P_OUT1B), (), nothing, True, begun=True, u0=24)
            layer_norm(2)
            x_high(3)
            mlp(P_MLP1, B_MLP1, 1, 1)
            layer_norm(3)

        @block.vector
        def _(dve):
            tt, ts, stt = nc.vector.tensor_tensor, nc.vector.tensor_scalar, nc.vector.scalar_tensor_tensor
            st = Steps(dve, S("dve_steps"))

            def f(ap):
                return ap.bitcast(F32)

            def rep(ap, n):
                return ap.unsqueeze(1).to_broadcast([P, n, ap.shape[-1]])

            def split(n, q, width):
                dve.wait_ge(S("hi_ready"), n * UNITS + (q + 1))
                tt(wl[:, q % RING, :, 0:width], raw[:, q, :, 0:width], f(wh[:, q % RING, :, 0:width]),
                   ALU.subtract).then_inc(S("lo_ready"), 1)

            def x_low(k):
                for t in range(TT):
                    for c in range(4):
                        dve.wait_ge(S("xhi"), 8 * k + 4 * t + c + 1)
                        ks, ts_ = slice(4 * c, 4 * c + 4), slice(t * P, (t + 1) * P)
                        tt(aTl[:, ks, ts_], r2(mb[c][:, :], a=4), f(aTh[:, ks, ts_]), ALU.subtract).then_inc(S("xlo"), 1)

            def used(n, u):
                dve.wait_ge(S("unit_used"), n * UNITS + (u + 1 + RING))

            def add_residual(b, j, buf, stat):
                dve.wait_ge(S("evacuated"), b + 2)
                o = xres[:, :, j * WIDE:(j + 1) * WIDE]
                tt(o, o, r2(pp[buf][:, :], a=TT), ALU.add).then_inc(S("evacuated"), 1)
                if stat:
                    dve.wait_ge(S("evacuated"), b + 3)
                    for t in range(TT):
                        st(nc.vector.bn_stats(stats[:, t, j, :], xres[:, t, j * WIDE:(j + 1) * WIDE]))

            def sigmoid_tail(ap):
                st(ts(ap, ap, 1e30, 1.0, ALU.min, ALU.add))
                st.settle()
                st(nc.vector.reciprocal(ap, ap))
                st.settle()

            def layer_norm(k):
                st.settle()
                for t in range(TT):
                    nc.vector.bn_aggr(mv[:, t, :], stats[:, t, :, :].rearrange("p c s -> p (c s)")).then_inc(S("ln_var"), 1)
                for t in range(TT):
                    dve.wait_ge(S("ln_rstd"), TT * k + t + 1)
                    stt(nmean[:, t:t + 1], mv[:, t, 0:1], -1.0, rstd[:, t:t + 1], ALU.mult, ALU.mult).then_inc(S("ln_nmean"), 1)
                dve.wait_ge(S("ln_in"), 32 * (k + 1))
                for t in range(TT):
                    for h in range(2):
                        dve.wait_ge(S("xn"), 4 * k + 2 * t + h + 1)
                        c = slice(h * 1024, (h + 1) * 1024)
                        o = xres[:, t, c]
                        st(tt(o, o, lng[:, c], ALU.mult))
                        st.settle()
                        tt(o, o, lnb[:, c], ALU.add).then_inc(S("x_ready"), 1)
                if k in (0, 2):
                    dve.wait_ge(S("x_ready"), 4 * (k + 1))
                    dve.sem_inc(S("ws_free"), 1)

            dve.sem_inc(S("lo_ready"), UNITS)
            for ap, v in ((eps_ln, LN_EPS), (eps_lnx, LNX_EPS), (eps_kk, KK_EPS), (eps_l2, 1e-6)):
                st(nc.vector.memset(ap, v))
            nc.vector.memset(ln_qs, -3.5 * 0.6931471805599453).then_inc(S("eps_ready"), 1)
            st(nc.vector.memset(pb[:, :, 0:1], 0.0))
            nc.vector.memset(lobuf[:, :, 0:1], 0.0).then_inc(S("zeroed"), 1)
            dve.wait_ge(S("prm_in"), 16)
            st(ts(nprm, prm[:, :, 3:5], -1.0, None, ALU.mult))
            x_low(0)
            for q in range(UNITS):
                split(0, q, NARROW)
            dve.wait_ge(S("evacuated"), 3)
            st(tt(dsh, lobuf[:, :, 0:T], lobuf[:, :, 1:T + 1], ALU.subtract))
            st.settle()
            for j in range(3):
                last = stt(loT[:, j, :], dsh[:, j, :], mulo[:, j:j + 1], lobuf[:, j, 1:T + 1], ALU.mult, ALU.add)
                if j < 2:
                    st(last)
            last.then_inc(S("lo_shifted"), 1)
            dve.wait_ge(S("lo_exp"), 1)
            sigmoid_tail(loT[:, 1:3, :])
            sigmoid_tail(loT[0:64, 0, :])
            ts(loT[0:64, 0, :], loT[0:64, 0, :], -2.0, 1.0, ALU.mult, ALU.add).then_inc(S("lo_acts"), 1)
            dve.wait_ge(S("c0_in"), 16)

            def mix0(m):
                m1 = m + 1
                par = lambda j: prm[:, bass.ds(m, 1), j]
                dve.wait_ge(S("evacuated"), 2 * m + (P_GROUPS0 + 3))
                st(tt(dsh, pb[:, :, 0:T], pb[:, :, 1:T + 1], ALU.subtract))
                st.settle()
                for j in range(3):
                    last = stt(rkv[:, j, :], dsh[:, j, :], par(j), pb[:, j, 1:T + 1], ALU.mult, ALU.add)
                    if j < 2:
                        st(last)
                last.then_inc(S("shifted"), 1)
                dve.wait_ge(S("shifted"), m1)
                ts(kk0, rkv[:, 1, :], par(5), None, ALU.mult).then_inc(S("kk0"), 1)
                dve.wait_ge(S("gates_exp"), m1)
                sigmoid_tail(ew)
                st(ts(Lg, sigw, -0.6065306597126334, None, ALU.mult))
                st.settle()
                st(nc.vector.tensor_tensor_scan(cum, rst, Lg, 0.0, ALU.mult, ALU.add))
                st.settle()
                tt(pexc, cum, Lg, ALU.subtract).then_inc(S("cum"), 1)
                dve.wait_ge(S("softplus"), m1)
                st(stt(sbb, mb[3][:, 0:384], 0.0, sbb, ALU.max, ALU.add))
                st(tt(sbc, mb[3][:, 0:384], sbbig, ALU.add))
                st.settle()
                tt(sbb, sbb, sbneg, ALU.mult).then_inc(S("lkeep"), 1)
                yield
                st(ts(k2, av, 1.0, par(6), ALU.subtract, ALU.mult))
                st.settle()
                st(stt(k2, k2, 1.0, rkv[:, 1, :], ALU.add, ALU.mult))
                dve.wait_ge(S("rkk"), m1)
                st(tt(kkt, kk0, ksq, ALU.mult))
                st.settle()
                st(stt(rk, rkv[:, 0, :], par(7), k2, ALU.mult, ALU.mult))
                st(tt(bt, kkt, av, ALU.mult))
                dve.wait_ge(S("powers"), m1)
                st(tt(KR[:, :, 1, :], r2(rkv[:, 0, :], a=TT), r2(pinc, a=TT), ALU.mult))
                st(tt(KR[:, :, 0, :], r2(kkt, a=TT), r2(pexc, a=TT), ALU.mult))
                st(tt(kt_, k2, pinv, ALU.mult))
                st.settle()
                tt(bt, bt, pinv, ALU.mult).then_inc(S("operands"), 1)
                yield
                dve.wait_ge(S("lcum"), m1)
                tt(sba, sbc, mb[2][:, 0:384], ALU.add).then_inc(S("loga"), 1)
                yield
                dve.wait_ge(S("sb_hi"), m1)
                tt(hTl[:, bass.ds(m * 2, 1), :], mb[3][:, 0:T].unsqueeze(1), f(hTh[:, bass.ds(m * 2, 1), :]),
                   ALU.subtract).then_inc(S("sb_lo"), 1)
                yield
                for t in range(TT):
                    dve.wait_ge(S("gram"), 2 * m + t + 1)
                    for h in range(2):
                        last = tt(GM[:, t, h, :, :, :].rearrange("p w r c -> p w (r c)"), r2(mb[2 * t + h][:, :], a=2),
                                  rep(rwmask, 2), ALU.mult)
                        if h == 0:
                            st(last)
                    last.then_inc(S("masked"), 1)
                dve.wait_ge(S("masked"), 2 * m1)
                st(tt(XT0, GM.rearrange("p t h w r c -> p (t h) w r c")[:, :, 0, 0, :], rep(cc[:, C_M0:C_M0 + P], 4), ALU.mult))
                st.settle()
                tt(XT0, XT0, rep(ident, 4), ALU.add).then_inc(S("XT_first"), 1)
                yield
                yield
                yield
                for lv in range(1, 6):
                    s_ = 1 << lv
                    dve.wait_ge(S("AX"), 5 * m + lv)
                    tt(Yn0, r2(mb[3][:, 0:256], a=4), rep(cc[:, C_LV + 64 * (lv - 1):C_LV + 64 * lv], 4),
                       ALU.mult).then_inc(S("Yn"), 1)
                    yield
                    dve.wait_ge(S("dX"), 5 * m + lv)
                    left = X0.rearrange("p a (b w s) -> p a b w s", w=2, s=s_)[:, :, :, 0, :]
                    tt(left, left, mb[2][:, 0:256].rearrange("p (a b s) -> p a b s", a=4, s=s_), ALU.add).then_inc(S("X_ready"), 1)
                    yield
                yield
                dve.wait_ge(S("XAV"), m1)
                st(ts(U[0:64, :], mb[1][0:64, 0:P], -1.0, None, ALU.mult))
                ts(Un, mb[1][:, 0:T], -1.0, None, ALU.mult).then_inc(S("U"), 1)
                dve.wait_ge(S("U"), 4 * m + 1)
                yield
                for c in range(4):
                    t, hf = divmod(c, 2)
                    R = slice(64 * hf, 64 * hf + 64)
                    if c:
                        dve.wait_ge(S("u_psum"), 3 * m + c)
                        tt(U[R, :], Un[R, t * P:(t + 1) * P], mb[0][R, 0:P], ALU.subtract).then_inc(S("U"), 1)
                        yield
                    if c < 3:
                        new = (Sa, Sb)[c % 2]
                        pend = pinc[:, 64 * c + 63:64 * c + 64]
                        dve.wait_ge(S("dS"), 3 * m + c + 1)
                        if c == 0:
                            stt(new, mb[3][:, 0:P], pend, bo, ALU.mult, ALU.mult).then_inc(S("state0"), 1)
                        else:
                            st(stt(dS0, mb[3][:, 0:P], pend, bo, ALU.mult, ALU.mult))
                            st.settle()
                            dve.wait_ge(S("pcS"), 2 * m + c)
                            tt(new, dS0, pcS, ALU.add).then_inc(S("state0"), 1)
                    yield
                dve.wait_ge(S("ymean"), m1)
                tt(yc, yT, mb[0][:, 0:T], ALU.subtract).then_inc(S("yc"), 1)
                yield
                dve.wait_ge(S("yrstd"), m1)
                st(tt(yn, yc, ksq, ALU.mult))
                st.settle()
                st(ts(yn, yn, par(8), par(9), ALU.mult, ALU.add))
                st(tt(yc, mb[1][:, 0:T], rkv[:, 2, :], ALU.mult))
                st.settle()
                st(tt(yn, yn, yc, ALU.add))
                st.settle()
                tt(yn, yn, gg, ALU.mult).then_inc(S("rw_o"), 1)
                dve.wait_ge(S("rw_hi"), m1)
                tt(hTl[:, bass.ds(m * 2 + 1, 1), :], yn.unsqueeze(1), f(hTh[:, bass.ds(m * 2 + 1, 1), :]),
                   ALU.subtract).then_inc(S("mix0_out"), 1)
                dve.wait_ge(S("mix0_out"), m1)
                yield

            def nothing(j, after):
                pass

            def narrow(n):
                return lambda u: split(n + u // UNITS, u % UNITS, NARROW)

            def wide(n):
                return lambda u: split(n + u // UNITS, u % UNITS, WIDE)

            def out_hook(n, b, bufs, per, u0, stat):
                def hook(j, after):
                    if not after:
                        used(n, u0 + per * j + per - 1)
                        add_residual(b + j, j, bufs[j], stat)
                return [per * j + per - 1 for j in range(4)], hook

            st.leave_straight()
            interleave(None, 0, 2 * UNITS, narrow(P_GROUPS0), (), nothing, False)
            PER = 27
            with dve.Fori(1, GROUPS) as i:
                st.enter(i - 1, PER)
                interleave(mix0(i - 1), Y0, 2 * UNITS, narrow(i * 2 + P_GROUPS0), (), nothing, False)
            st.leave(GROUPS - 1)
            dve.wait_ge(S("x_scaled"), 1)
            interleave(mix0(GROUPS - 1), Y0, 28, wide(P_OUT0), *out_hook(P_OUT0, B_OUT0, (0, 1, 0, 1), 7, 0, False), True)
            dve.sem_inc(S("ws_free"), 1)
            st.leave_straight()
            interleave(None, 0, 4, wide(P_OUT0), *out_hook(P_OUT0, B_OUT0 + 4, (0, 1, 0, 1), 1, 28, True), stop != 1,
                       begun=True, u0=28)
            layer_norm(0)
            x_low(1)
            if stop == 1:
                return

            def mlp(n0, b0, k, par):
                def body(f_, ahead, last):
                    n = f_ * 8 + n0

                    def hook(j, after):
                        if j < 4 and after:
                            seen = f_ * 4 + (4 * FG * k + j + 1)
                            dve.wait_ge(S("hid_hi"), seen)
                            tt(hid, hid, hid, ALU.mult).then_inc(S("hid_sq"), 1)
                            dve.wait_ge(S("hid_sq"), seen)
                            tt(hTl[:, 4 * j:4 * j + 4, :], r2(hid, a=4), f(hTh[:, 4 * j:4 * j + 4, :]),
                               ALU.subtract).then_inc(S("hid_ready"), 1)
                        elif j >= 4 and not after:
                            used(n, j * UNITS + UNITS - 1)
                            add_residual(f_ * 8 + (b0 + j), j - 4, (par + j) % 2, last)
                    interleave(None, 0, 8 * UNITS, wide(n), [UNITS * j + UNITS - 1 for j in range(8)], hook, ahead, begun=True)
                with dve.Fori(0, FG - 1) as f_:
                    body(f_, True, False)
                st.leave_straight()
                body(FG - 1, k == 0, True)

            dve.wait_ge(S("x_scaled"), 2)
            mlp(P_MLP0, B_MLP0, 0, 0)
            layer_norm(1)
            x_low(2)
            st.leave_straight()
            dve.wait_ge(S("beta_exp"), 1)
            tt(gv, mb[0][:, 0:128].rearrange("p (c h) -> p c h", c=TT)[:, :, 32:64], rep(r1[:, 32:64], TT),
               ALU.add).then_inc(S("a_dt"), 1)
            sigmoid_tail(beta)
            dve.wait_ge(S("g_ln"), 1)
            st(stt(gv, gv, 0.0, gtmp, ALU.max, ALU.add))
            st.settle()
            stt(gv, gv, -1.0, rep(r1[:, 0:32], TT), ALU.mult, ALU.mult).then_inc(S("g_ready"), 1)
            nc.vector.memset(cbuf[:, :, 0:3], 0.0).then_inc(S("zeroed"), 1)
            dve.wait_ge(S("gsum_read"), 1)
            st(nc.vector.tensor_copy(gtmp, mb[1][:, 0:64].rearrange("p (c h) -> p c h", c=TT)))
            st.settle()
            tt(kend, mb[1][:, 64:128].rearrange("p (c h) -> p c h", c=TT), gtmp, ALU.subtract).then_inc(S("kend_log"), 1)
            dve.wait_ge(S("gates1"), 1)
            st(ts(negc, egc, -1.0, None, ALU.mult))

            def mix1(g, b, gl):
                g1 = g + 1
                head = lambda a, c, h: a[:, c, bass.ds(g * 4 + h, 1)]
                heads = lambda a: a[:, :, bass.ds(g * 4, 4)].rearrange("p c (j r) -> p c j r", r=2)
                two = lambda a: a.unsqueeze(3).to_broadcast([P, TT, 2, 2])

                def tap(js, k):
                    for j in js:
                        last = stt(qkv[:, j, :], cbuf[:, j, k:T + k], cw[:, bass.ds(g, 1), 4 * j + k], qkv[:, j, :],
                                   ALU.mult, ALU.add)
                        if j != js[-1] or k < 2:
                            st(last)
                    if k == 2:
                        last.then_inc(S("conv"), 1)
                    else:
                        st.settle()

                def log_sigmoid(dst, src, sp, name):
                    dve.wait_ge(S(sp), g1)
                    stt(dst, src, 0.0, dst, ALU.min, ALU.subtract).then_inc(S(name), 1)

                def o_scale(c):
                    dve.wait_ge(S("oss"), 8 * g + (4 * c + 4))
                    q2 = qsc[:, c, :].unsqueeze(2).to_broadcast([P, 2, 2])
                    o4 = lambda a: a.rearrange("p (j r) -> p j r", r=2)
                    st(stt(o4(osc), o4(oss), 1.0 / P, q2, ALU.mult, ALU.mult))
                    st.settle()
                    tt(o4(osc), o4(osc), q2, ALU.mult).then_inc(S("o_ms"), 1)
                    dve.wait_ge(S("o_rstd"), 2 * g + c + 1)
                    st(tt(o4(osq), o4(osq), q2, ALU.mult))
                    st.settle()
                    for h in range(4):
                        last = ts(on[:, h, :], os[c][:, h, :], osq[:, h:h + 1], None, ALU.mult)
                        if h < 3:
                            st(last)
                    last.then_inc(S("on"), 1)

                def out_low(c):
                    dve.wait_ge(S("oT"), 2 * g + c + 1)
                    stt(oT1, r2(mb[2 if c == 0 else 0][:, :], a=4), nw, zs[:, :, c * P:(c + 1) * P], ALU.mult,
                        ALU.mult).then_inc(S("oTf"), 1)
                    dve.wait_ge(S("mix1_hi"), 2 * g + c + 1)
                    hs = (slice(None), bass.ds(gl * 4, 4), slice(c * P, (c + 1) * P))
                    tt(hTl[hs], oT1, f(hTh[hs]), ALU.subtract).then_inc(S("mix1_out"), 1)
                    dve.wait_ge(S("mix1_out"), 2 * g + c + 1)

                dve.wait_ge(S("evacuated"), b + 5)
                dve.wait_ge(S("conv_first"), 2 * g + 1)
                tap(range(0, 4), 0)
                yield
                tap(range(0, 4), 1)
                yield
                tap(range(0, 4), 2)
                yield
                dve.wait_ge(S("conv_first"), 2 * g + 2)
                tap(range(4, 8), 0)
                yield
                tap(range(4, 8), 1)
                log_sigmoid(E1[:, 0:4, :], qkv[:, 0:4, :], "sp_qk", "s_qk")
                yield
                tap(range(4, 8), 2)
                log_sigmoid(SQ, zs, "sp_z", "s_z")
                yield
                dve.wait_ge(S("sig_qk"), g1)
                tt(qkv[:, 0:4, :], qkv[:, 0:4, :], E1[:, 0:4, :], ALU.mult).then_inc(S("qk_act"), 1)
                log_sigmoid(E1[:, 4:8, :], qkv[:, 4:8, :], "sp_v", "s_v")
                yield
                for c in range(TT):
                    for h in range(4):
                        last = ts(UTg[:, c, h, :], UT, head(gv, c, h), None, ALU.mult)
                        if c * 4 + h < 7:
                            st(last)
                last.then_inc(S("utg"), 1)
                dve.wait_ge(S("sig_z"), g1)
                tt(zs, zs, SQ, ALU.mult).then_inc(S("zs_ready"), 1)
                yield
                dve.wait_ge(S("sig_v"), g1)
                tt(qkv[:, 4:8, :], qkv[:, 4:8, :], E1[:, 4:8, :], ALU.mult).then_inc(S("v_act"), 1)
                dve.wait_ge(S("cols"), g1)
                w4 = wc.rearrange("p c (j r) -> p c j r", r=2)
                st(tt(w4, heads(beta), two(wkc), ALU.mult))
                st.settle()
                st(tt(wke.rearrange("p c (j r) -> p c j r", r=2), w4, heads(kend), ALU.mult))
                yield
                dve.wait_ge(S("kq"), g1)
                for c in range(TT):
                    last = tt(KQ[:, c, :, :, :].rearrange("p j w t -> p j (w t)"), r2(mb[2 + c][:, :], a=2), rep(gmask, 2),
                              ALU.mult)
                    if c == 0:
                        st(last)
                last.then_inc(S("KQm"), 1)
                dve.wait_ge(S("v_act"), g1)
                yield
                dve.wait_ge(S("KQm"), g1)
                dve.wait_ge(S("D"), g1)
                st.settle()
                for c in range(TT):
                    for h in range(4):
                        st(stt(At[:, c, h, :], Dm[:, c, h, :], wc[:, c, h:h + 1], KQ[:, c, h // 2, 1, :], ALU.mult, ALU.mult))
                st.settle()
                st(tt(XT1, At.rearrange("p c h t -> p (c h) t"), rep(cc[:, C_M0:C_M0 + P], 8), ALU.mult))
                st.settle()
                tt(XT1, XT1, rep(ident, 8), ALU.add).then_inc(S("XT1_first"), 1)
                yield
                for c in range(TT):
                    st(tt(AT[:, c, :, :].rearrange("p (j r) t -> p j r t", r=2), Dm[:, c, :, :].rearrange("p (j r) t -> p j r t", r=2),
                          KQ[:, c, :, 0:1, :].to_broadcast([P, 2, 2, P]), ALU.mult))
                yield
                for lv in range(1, 7):
                    s_ = 1 << lv
                    dve.wait_ge(S("AX1"), 6 * g + lv)
                    tt(Yn1, r2(mb[0][:, :], a=8), rep(cc[:, C_LV + 64 * (lv - 1):C_LV + 64 * lv], 8),
                       ALU.mult).then_inc(S("Yn1"), 1)
                    yield
                    dve.wait_ge(S("dX1"), 6 * g + lv)
                    left = X1.rearrange("p a (b w s) -> p a b w s", w=2, s=s_)[:, :, :, 0, :]
                    tt(left, left, mb[1][:, :].rearrange("p (a b s) -> p a b s", a=8, s=s_), ALU.add).then_inc(S("X1_ready"), 1)
                    yield
                yield

                def take_z(c, bank):
                    dve.wait_ge(S("vk"), 2 * g + c + 1)
                    for h in range(4):
                        last = ts(vke[:, h, :], bank[:, h * P:(h + 1) * P], wke[:, c, h:h + 1], None, ALU.mult)
                        if h < 3:
                            st(last)
                    last.then_inc(S("vke"), 1)

                take_z(0, mb[0])
                yield
                dve.wait_ge(S("dS1"), g1)
                nc.vector.tensor_copy(S1, r2(mb[3][:, :], a=4)).then_inc(S("state1"), 1)
                dve.wait_ge(S("o0_read"), g1)
                yield
                dve.wait_ge(S("kS"), g1)
                for h in range(4):
                    last = stt(yp[:, h, :], mb[0][:, h * P:(h + 1) * P], head(negc, 1, h), vs[:, 1, h, :], ALU.mult, ALU.add)
                    if h < 3:
                        st(last)
                last.then_inc(S("yp"), 1)
                yield
                o_scale(0)
                yield
                dve.wait_ge(S("o_psum"), 2 * g + 2)
                dve.wait_ge(S("t1"), g1)
                tt(os[1], r2(mb[1][:, :], a=4), os[1], ALU.add).then_inc(S("o_sum"), 1)
                out_low(0)
                o_scale(1)
                yield
                out_low(1)
                yield

            def group1(n):
                return 3 * UNITS, wide(n), (), nothing, True, True

            PER1 = 59
            st.leave_straight()
            interleave(None, 0, *group1(P_L1))
            with dve.Fori(1, 5) as i:
                st.enter(i - 1, PER1)
                interleave(mix1(i - 1, i * 3 + (B_L1 - 3), i - 1), Y1, *group1(i * 3 + P_L1))
            st.leave(4)
            dve.wait_ge(S("x_scaled"), 3)
            interleave(mix1(4, B_L1 + 12, 0), Y1, 4 * UNITS, wide(P_OUT1A),
                       *out_hook(P_OUT1A, B_OUT1A, (1, 0, 1, 0), UNITS, 0, False), True, begun=True)
            st.leave_straight()
            interleave(None, 0, *group1(P_L1B))
            with dve.Fori(6, 8) as i:
                st.enter(i - 6, PER1)
                interleave(mix1(i - 1, i * 3 + (B_L1B - 18), i - 5), Y1, *group1(i * 3 + (P_L1B - 15)))
            st.leave(2)
            interleave(mix1(7, B_L1B + 6, 3), Y1, 24, wide(P_OUT1B),
                       *out_hook(P_OUT1B, B_OUT1B, (1, 0, 1, 0), 6, 0, False), True, begun=True)
            dve.sem_inc(S("ws_free"), 1)
            interleave(None, 0, 8, wide(P_OUT1B), *out_hook(P_OUT1B, B_OUT1B + 4, (1, 0, 1, 0), 2, 24, True), True, begun=True, u0=24)
            layer_norm(2)
            x_low(3)
            dve.wait_ge(S("x_scaled"), 4)
            mlp(P_MLP1, B_MLP1, 1, 1)
            layer_norm(3)


def constants():
    import numpy as np

    a = np.arange(P)
    s, t = a[:, None], a[None, :]
    cc = np.zeros((P, C_SHARED), np.float32)
    cc[:, C_ID:C_ID + P] = s == t
    cc[:, C_ONES:C_ONES + P] = 1
    for lv in range(1, 7):
        w = 1 << lv
        cols = a.reshape(-1, 2, w)[:, 0, :].reshape(-1)[None, :]
        same = (s // (2 * w) == cols // (2 * w)) & (s // w % 2 == 1)
        cc[:, C_LV + 64 * (lv - 1):C_LV + 64 * lv] = -1.0 * same
    cc[:, C_M0:C_M0 + P] = -1.0 * ((s // 2 == t // 2) & (s < t))
    c0 = np.zeros((P, C0_N), np.float32)
    q = np.arange(T)[None, :]
    keep = np.concatenate([s < q, s < t], axis=1)
    c0[:, C0_SB:C0_SB + 384] = -1.0 * keep
    c0[:, C0_BIG:C0_BIG + 384] = np.where(keep, 0.0, -1e30)
    c0[:, C0_TRI:C0_TRI + P] = s >= t
    block = s // 64 == t // 64
    c0[:, C0_BO:C0_BO + P] = block
    c0[:, C0_BO64:C0_BO64 + P] = block / 64.0
    c0[:, C0_RW:C0_RW + P] = block & (s < t)
    c0[:, C0_RW + P:C0_RW + 2 * P] = block & (s <= t)
    c0[:, C0_RST:C0_RST + T] = q % 64 != 0
    c1 = np.zeros((P, C1_N), np.float32)
    c1[:, C1_GM:C1_GM + P] = s <= t
    c1[:, C1_GM + P:C1_GM + 2 * P] = s < t
    c1[:, C1_SL:C1_SL + P] = s > t
    return cc, c0, c1


def layout(x, ev_w_in, ev_shift, ev_w0, ev_w_up, ev_a0, ev_a_up, ev_g_up, ev_k_k, ev_k_a, ev_r_k, ev_lnx_g, ev_lnx_b,
           vres_w_down, vres_shift, vres_v0, vres_v_up, ev_w_out, od_w_in, od_conv, od_a_log, od_dt_bias, od_norm_w,
           od_w_out, ln1_g, ln1_b, mlp_w1, mlp_w2, ln2_g, ln2_b):
    import numpy as np

    def fill(dst, w):
        dst[:, :, :w.shape[1]] = w.reshape(KT, P, w.shape[1]).transpose(1, 0, 2)

    def unit(w, rows):
        return np.stack([w[r:r + P] for r in rows], axis=1)

    w384 = np.zeros((P_OUT0, P, KT, NARROW), np.float32)
    w = ev_w_in[0]
    fill(w384[0], w[:, 6144:])
    for i in range(GROUPS):
        for b in range(3):
            for n, base in ((1 + 2 * i, 3072), (2 + 2 * i, 0)):
                c = base + 1024 * b + P * i
                fill(w384[n][:, :, b * P:(b + 1) * P], w[:, c:c + P])
    w384 = w384.reshape(P_OUT0, P, UNITS, UK, NARROW).transpose(0, 2, 1, 3, 4).reshape(-1, P, UK, NARROW)
    w512 = np.empty(((PANELS - P_OUT0) * UNITS, P, UK, WIDE), np.float32)
    at = 0

    def put(w, first=0, last=UNITS, rows=lambda q: (2 * P * q, 2 * P * q + P)):
        nonlocal at
        for q in range(first, last):
            w512[at] = unit(w, rows(q))
            at += 1

    def put_mlp(k):
        for f in range(FG):
            for j in range(4):
                put(mlp_w1[k][:, f * D + j * WIDE:f * D + (j + 1) * WIDE])
            for j in range(4):
                put(mlp_w2[k][f * D:(f + 1) * D, j * WIDE:(j + 1) * WIDE])

    def put_group(g):
        w = od_w_in[0]
        put(np.concatenate([w[:, 256 * g:256 * g + 256], w[:, 2048 + 256 * g:2048 + 256 * g + 256]], axis=1))
        put(w[:, 4096 + 512 * g:4096 + 512 * g + 512])
        put(w[:, 8192 + 512 * g:8192 + 512 * g + 512])

    for first, last in ((0, 7), (7, 8)):
        for j in range(4):
            put(ev_w_out[0][:, j * WIDE:(j + 1) * WIDE], first, last, lambda q: (P * q, 1024 + P * q))
    put_mlp(0)
    for g in range(5):
        put_group(g)
    for j in range(4):
        put(od_w_out[0][0:D, j * WIDE:(j + 1) * WIDE])
    for g in range(5, GROUPS):
        put_group(g)
    for first, last in ((0, 6), (6, 8)):
        for j in range(4):
            put(od_w_out[0][D:2 * D, j * WIDE:(j + 1) * WIDE], first, last)
    put_mlp(1)
    assert at == len(w512)
    w = od_w_in[0]
    wba = np.ascontiguousarray(w[:, 12288:].reshape(KT, P, 64).transpose(1, 0, 2))

    prm0 = np.zeros((P, GROUPS * 10 + 3), np.float32)
    vecs = [ev_shift[0][0:1024], ev_shift[0][1024:2048], ev_shift[0][2048:3072], ev_w0[0], ev_a0[0], ev_k_k[0], ev_k_a[0],
            ev_r_k[0].reshape(-1), ev_lnx_g[0], ev_lnx_b[0]]
    for j, v in enumerate(vecs):
        prm0[:, j:GROUPS * 10:10] = v.reshape(GROUPS, P).T
    lo = np.zeros(384, np.float32)
    lo[:288] = ev_shift[0][3072:]
    prm0[:, GROUPS * 10:] = lo.reshape(3, P).T
    lora = np.zeros((GROUPS, P, 3, P), np.float32)
    for m in range(GROUPS):
        c = slice(m * P, (m + 1) * P)
        lora[m, 0:64, 0], lora[m, 64:, 0] = ev_w_up[0][:, c], ev_a_up[0][:, c]
        lora[m, :, 1], lora[m, 0:32, 2] = ev_g_up[0][0:P, c], ev_g_up[0][P:, c]
    conv = np.zeros((P, GROUPS, 8, 4), np.float32)
    for g in range(GROUPS):
        for j in range(8):
            c = (256 * g + P * j, 2048 + 256 * g + P * (j - 2), 4096 + 512 * g + P * (j - 4))[(j >= 2) + (j >= 4)]
            conv[:, g, j] = od_conv[0][:, c:c + P].T
    rows1 = np.concatenate([od_a_log, od_dt_bias], axis=1)
    ln = np.stack([ln1_g[0], ln1_b[0], ln2_g[0], ln2_b[0], ln1_g[1], ln1_b[1], ln2_g[1], ln2_b[1]])
    cc, c0, c1 = constants()
    return {"x": x[0], "w384": w384, "w512": w512, "wba": wba, "consts": cc, "c0": c0, "c1": c1, "prm0": prm0,
            "lora": lora.reshape(GROUPS, P, 3 * P), "conv": conv.reshape(P, GROUPS * 32), "rows1": rows1,
            "normw": np.ascontiguousarray(od_norm_w[0].reshape(P, 1)), "ln": ln}


STOP = 0


def kernel(**inputs):
    import numpy as _np
    import concourse.bacc as _bacc
    from concourse import mybir as _mybir
    from concourse.bass_utils import run_bass_kernel_spmd as _run

    nc = _bacc.Bacc("TRN2", target_bir_lowering=False, num_devices=1)
    laid = layout(**{k: _np.asarray(v) for k, v in inputs.items()})
    arrays, args = {}, {}
    for name, a in laid.items():
        a = _np.ascontiguousarray(a)
        arrays[f"in_{name}_dram"] = a
        args[name] = nc.dram_tensor(f"in_{name}_dram", a.shape, _mybir.dt.from_np(a.dtype), kind="ExternalInput").ap()
    args["out"] = nc.dram_tensor("out_0_dram", (T, D), _mybir.dt.float32, kind="ExternalOutput").ap()
    trunk(nc, STOP, **args)
    r = _run(nc, [arrays], core_ids=[0])
    return r.results[0]["out_0_dram"].reshape(1, T, D)
```

```python
from contextlib import ExitStack

import concourse.bass as bass
from concourse import mybir

F32 = mybir.dt.float32
F32R = mybir.dt.float32r
ALU = mybir.AluOpType
ACT = mybir.ActivationFunctionType

P = 128
D = 2048
T = 256
KT = D // P
TT = T // P
UK = 2
UNITS = KT // UK
RING = 4
WIDE = 512
NARROW = 384
GROUPS = 8
FF = 4 * D
FG = FF // D
ALPHA = 4.0 ** 0.25
LN_EPS = 1e-5
LNX_EPS = 64e-5
KK_EPS = 1e-12
SB_SCALE = 128.0 ** -0.5
LEAD = 2

P_GROUPS0 = 1
P_OUT0 = P_GROUPS0 + 2 * GROUPS
P_MLP0 = P_OUT0 + 4
P_L1 = P_MLP0 + 8 * FG
P_OUT1A = P_L1 + 3 * 5
P_L1B = P_OUT1A + 4
P_OUT1B = P_L1B + 3 * 3
P_MLP1 = P_OUT1B + 4
PANELS = P_MLP1 + 8 * FG
B_OUT0 = P_OUT0
B_MLP0 = B_OUT0 + 8
B_L1 = B_MLP0 + 8 * FG
B_OUT1A = B_L1 + 3 * 5
B_L1B = B_OUT1A + 4
B_OUT1B = B_L1B + 3 * 3
B_MLP1 = B_OUT1B + 8
HOPS0 = (3, 4, 3, 3, 3) + 24 * (1,)
HOPS_LORA = 16 * (1,)
HOPS1 = (2, 3, 3, 3, 3, 2) + (1, 1, 2, 3) + 14 * (1,) + (2, 1, 2, 2, 3, 1)
HOPS_GATES = 4 * (4,) + (5,) + 9 * (3,)
HOPS_X = 4 * (1,)
HOPS_MLP = 4 * (2,) + 56 * (1,)

C_ID, C_ONES, C_LV, C_M0 = 0, 128, 256, 640
C_SHARED = 768
C0_SB, C0_BIG, C0_TRI, C0_BO, C0_BO64, C0_RW, C0_RST = 0, 384, 768, 896, 1024, 1152, 1408
C0_N = 1664
C1_GM, C1_SL = 0, 256
C1_N = 384
WS = 53215 - 36864 - C_SHARED - 32


class Steps:

    def __init__(self, eng, sem):
        self.eng, self.sem, self.total, self.n, self.base, self.per = eng, sem, 0, 0, 0, None

    def enter(self, i, per):
        self.base, self.per, self.n = i * per + self.total, per, 0

    def __call__(self, ins):
        self.n += 1
        return ins.then_inc(self.sem, 1)

    def settle(self):
        self.eng.wait_ge(self.sem, self.base + self.n)

    def leave(self, times):
        assert self.n == self.per, f"the body has {self.n} steps, {self.per} declared"
        self.total += times * self.per
        self.base, self.n, self.per = self.total, 0, None

    def leave_straight(self):
        self.total += self.n
        self.base, self.n = self.total, 0


def hop_of(half, halves, hops):
    share = 0
    for y, h in enumerate(hops):
        share += h
        if share * halves > half * sum(hops):
            return y


def interleave(mixer, hops, units, one, ends, hook, ahead, begun=False, late=None, u0=0,
               wait=None):
    if not begun:
        for u in range(LEAD):
            one(u0 + u)
    wait = wait or (1 if mixer else 2)
    hops = hops if mixer else units * (1,)
    for y in range(len(hops) + wait + 1):
        if mixer and y < len(hops):
            next(mixer)
        for u in range(units):
            if hop_of(2 * u, 2 * units, hops) == y and (ahead or u + LEAD < units):
                one(u0 + u + LEAD)
        for j, e in enumerate(ends):
            after = y - hop_of(2 * e + 1, 2 * units, hops) - wait
            if after in (0, 1):
                hook(j, after)
    if mixer:
        assert next(mixer, "over") == "over"
    if late:
        late()


def then(*parts):
    for part in parts:
        yield from (None for _ in range(part)) if isinstance(part, int) else part


class Lay:

    def __init__(self, ws, at=0):
        self.ws, self.at = ws, at

    def __call__(self, n):
        self.at += n
        assert self.at <= WS, self.at
        return self.ws[:, self.at - n:self.at]


def trunk(nc, stop, x, w384, w512, wba, consts, c0, c1, prm0, lora, conv, rows1, normw, ln, out):
    ctx = ExitStack()
    with ctx:
        def sb(name, shape, dt=F32):
            return ctx.enter_context(nc.sbuf_tensor(name, shape, dt))

        sems = {}

        def S(name):
            if name not in sems:
                sems[name] = ctx.enter_context(nc.semaphore(name))
            return sems[name]

        raw = sb("raw", [P, UNITS, UK, WIDE])
        wh = sb("wh", [P, RING, UK, WIDE], F32R)
        wl = sb("wl", [P, RING, UK, WIDE], F32R)
        xres = sb("xres", [P, TT, D])
        aTh = sb("aTh", [P, KT, T], F32R)
        aTl = sb("aTl", [P, KT, T], F32R)
        hTh = sb("hTh", [P, KT, T], F32R)
        hTl = sb("hTl", [P, KT, T], F32R)
        cc = sb("cc", [P, C_SHARED])
        ws = sb("ws", [P, WS])
        small = sb("small", [P, 16])
        pp = [ctx.enter_context(nc.psum_tensor(f"pp{b}", [P, 2 * WIDE], F32)) for b in range(2)]
        mb = [ctx.enter_context(nc.psum_tensor(f"mb{b}", [P, WIDE], F32)) for b in range(4)]

        ident = cc[:, C_ID:C_ID + P]
        ones = cc[:, C_ONES:C_ONES + P]
        eps_ln, eps_lnx, eps_kk, eps_l2, ln_qs = (small[:, j:j + 1] for j in range(5))
        mv = small[:, 8:12].rearrange("p (t s) -> p t s", t=TT)
        rstd = small[:, 12:14]

        def r2(ap, **kw):
            return ap.rearrange("p (a b) -> p a b", **kw)

        lay = Lay(ws)
        lng = lay(D)
        lnb = lay(D)
        stats = lay(TT * 4 * 6).rearrange("p (t c s) -> p t c s", t=TT, c=4)
        hid = lay(2 * WIDE)

        lay = Lay(ws)
        k0 = lay(C0_N)
        sbneg, sbbig = k0[:, C0_SB:C0_SB + 384], k0[:, C0_BIG:C0_BIG + 384]
        tri, bo, bo64 = (k0[:, c:c + P] for c in (C0_TRI, C0_BO, C0_BO64))
        rwmask, rst = k0[:, C0_RW:C0_RW + 256], k0[:, C0_RST:C0_RST + 256]
        pb = r2(lay(3 * (T + 1)), a=3)
        sbq = r2(lay(3 * T), a=3)
        rkv = r2(lay(3 * T), a=3)
        loT = r2(lay(3 * T), a=3)
        lw = r2(lay(3 * P), a=3)
        prmf = lay(GROUPS * 10 + 3)
        prm = r2(prmf[:, 0:GROUPS * 10], a=GROUPS)
        mulo = prmf[:, GROUPS * 10:GROUPS * 10 + 3]
        nprm = r2(lay(GROUPS * 2), a=GROUPS)
        ew = lay(2 * T)
        sigw, av = ew[:, 0:T], ew[:, T:2 * T]
        Lg, cum = lay(T), lay(T)
        p3 = lay(3 * T)
        pinc, pinv, pexc = (p3[:, j * T:(j + 1) * T] for j in range(3))
        yT, yc, yn = pinv, pexc, Lg
        kk0, k2 = lay(T), lay(T)
        KR = lay(2 * T).rearrange("p (t w c) -> p t w c", t=TT, w=2)
        bt, kt_, gg, rk = lay(T), lay(T), lay(T), lay(T)
        tok = lay(4 * T).rearrange("p (w t c) -> p w t c", w=4, t=TT)
        GMf = lay(2048)
        GM = GMf.rearrange("p (t h w r c) -> p t h w r c", t=TT, h=2, w=2, r=2)
        dsh = r2(GMf[:, 0:3 * T], a=3)
        lobuf = r2(GMf[:, 3 * T:3 * T + 3 * (T + 1)], a=3)
        ksq = GMf[:, 3 * T:4 * T]
        kkt = GMf[:, 4 * T:5 * T]
        X0 = r2(lay(4 * P), a=4)
        XT0 = r2(lay(4 * P), a=4)
        Yn0 = r2(lay(4 * 64), a=4)
        Sa, Sb, U = (lay(P) for _ in range(3))
        vtk = r2(lay(T), a=TT)
        sba, sbb, sbc = (lay(384) for _ in range(3))
        AVs, Un = sba[:, 0:T], sbb[:, 0:T]
        dS0, pcS = sbc[:, 0:P], sbc[:, P:2 * P]

        lay = Lay(ws)
        k1 = lay(C1_N)
        gmask, SL = k1[:, C1_GM:C1_GM + 256], k1[:, C1_SL:C1_SL + P]
        UT = gmask[:, 0:P]
        cbuf = r2(lay(8 * (T + 3)), a=8)
        zs = r2(lay(4 * T), a=4)
        qkv = r2(lay(8 * T), a=8)
        Ef = lay(2048)
        E1 = r2(Ef, a=8)
        AT = Ef[:, 0:1024].rearrange("p (c h t) -> p c h t", c=TT, h=4)
        At = Ef[:, 1024:2048].rearrange("p (c h t) -> p c h t", c=TT, h=4)
        Df = lay(1024)
        SQ = r2(Df, a=4)
        Dm = Df.rearrange("p (c h t) -> p c h t", c=TT, h=4)
        KQf = lay(1024)
        KQ = KQf.rearrange("p (c j w t) -> p c j w t", c=TT, j=2, w=2)
        Xf = lay(1024)
        X1 = r2(Xf, a=8)
        UTg = Xf.rearrange("p (c h t) -> p c h t", c=TT, h=4)
        XT1 = r2(lay(1024), a=8)
        ktok = lay(512).rearrange("p (c j t) -> p c j t", c=TT, j=2)
        vs = lay(1024).rearrange("p (c h t) -> p c h t", c=TT, h=4)
        Yn1 = r2(lay(512), a=8)
        oT1 = r2(Yn1.rearrange("p a b -> p (a b)"), a=4)
        S1 = r2(lay(512), a=4)
        yp = r2(Df[:, 0:512], a=4)
        vk = r2(Df[:, 512:1024], a=4)
        vke = r2(KQf[:, 0:512], a=4)
        os = (r2(KQf[:, 512:1024], a=4), r2(Ef[:, 1024:1536], a=4))
        on = r2(Ef[:, 1536:2048], a=4)
        wba_sb, wbh, wbl = r2(Ef[:, 0:1024], a=KT), hTh[:, :, 0:64], hTl[:, :, 0:64]
        gates = lay(7 * 64).rearrange("p (s c h) -> p s c h", s=7, c=TT)
        beta, gv, negc, egc, kend, egl, gtmp = (gates[:, s] for s in range(7))
        colk = lay(48)
        ssc = colk[:, 0:8].rearrange("p (c j) -> p c j", c=TT)
        lnss = colk[:, 8:16].rearrange("p (c j) -> p c j", c=TT)
        qsc = colk[:, 16:20].rearrange("p (c j) -> p c j", c=TT)
        skc = colk[:, 20:24].rearrange("p (c j) -> p c j", c=TT)
        wkc = colk[:, 24:28].rearrange("p (c j) -> p c j", c=TT)
        wc = colk[:, 28:36].rearrange("p (c h) -> p c h", c=TT)
        wke = lay(8).rearrange("p (c h) -> p c h", c=TT)
        oss = colk[:, 36:40]
        egq = colk[:, 40:44]
        osq = lay(4)
        cw = r2(lay(GROUPS * 32), a=GROUPS)
        r1 = lay(64)
        nw = lay(1)
        sqj = lay(P)

        block = ctx.enter_context(nc.Block())

        @block.sync
        def _(sp):
            sp.dma_start(ident, consts[:, C_ID:C_ID + P]).then_inc(S("ident_in"), 16)
            for c in range(2):
                sp.dma_start(xres[:, :, c * WIDE:(c + 1) * WIDE],
                             x[:, c * WIDE:(c + 1) * WIDE].rearrange("(t p) d -> p t d", p=P)).then_inc(S(f"x_in{c}"), 16)

            def load(n, src, width):
                for q in range(UNITS):
                    sp.wait_ge(S("lo_ready"), n * UNITS + (q + 1))
                    sp.dma_start(raw[:, q, :, 0:width], src[:, q, :, :]).then_inc(S(f"landed{q}"), 16)

            with sp.Fori(0, P_OUT0) as i:
                load(i, w384[bass.ds(i * UNITS, UNITS)].rearrange("q p k c -> p q k c"), NARROW)
            with sp.Fori(0, 4 if stop == 1 else PANELS - P_OUT0) as i:
                load(i + P_OUT0, w512[bass.ds(i * UNITS, UNITS)].rearrange("q p k c -> p q k c"), WIDE)
            o = out.rearrange("(t p) d -> p t d", p=P)
            for r in range(8):
                c, t = divmod(r, TT)
                sp.wait_ge(S("x_ready"), (0 if stop == 1 else 24) + r + 1)
                sp.dma_start(o[:, t, c * WIDE:(c + 1) * WIDE], xres[:, t, c * WIDE:(c + 1) * WIDE]).then_inc(S("stored"), 16)
            sp.wait_ge(S("stored"), 16 * 8)

        @block.gpsimd
        def _(pool):
            def scale_residual(k):
                pool.wait_ge(S("x_transposed"), k)
                nc.gpsimd.tensor_scalar(xres[:, :, :], xres[:, :, :], ALPHA, None, ALU.mult).then_inc(S("x_scaled"), 1)

            def load_ln(k):
                pool.wait_ge(S("ws_free"), k + 1)
                pool.dma_start(lng, ln[2 * k:2 * k + 1, :].partition_broadcast(P)).then_inc(S("ln_in"), 16)
                pool.dma_start(lnb, ln[2 * k + 1:2 * k + 2, :].partition_broadcast(P)).then_inc(S("ln_in"), 16)

            pool.wait_ge(S("x_in3"), 16)
            pool.dma_start(prmf, prm0).then_inc(S("prm_in"), 16)
            pool.dma_start(cc[:, P:C_SHARED], consts[:, P:C_SHARED]).then_inc(S("masks_in"), 16)
            pool.dma_start(k0, c0).then_inc(S("c0_in"), 16)
            scale_residual(1)
            with pool.Fori(0, GROUPS) as i:
                pool.wait_ge(S("lora_used"), i + 1)
                pool.dma_start(lw, lora[bass.ds(i, 1)].rearrange("a p (w c) -> p (a w) c", w=3)).then_inc(S("lora_in"), 16)
            load_ln(0)
            if stop == 1:
                return
            scale_residual(2)
            load_ln(1)
            pool.dma_start(wba_sb, wba).then_inc(S("wba_in"), 16)
            scale_residual(3)
            pool.dma_start(k1, c1).then_inc(S("c1_in"), 16)
            pool.dma_start(cw, conv).then_inc(S("c1_in"), 16)
            pool.dma_start(r1, rows1.partition_broadcast(P)).then_inc(S("c1_in"), 16)
            pool.dma_start(nw, normw).then_inc(S("c1_in"), 16)
            load_ln(2)
            scale_residual(4)
            load_ln(3)

        @block.tensor
        def _(pe):
            mm = nc.tensor.matmul

            def unit(n, u, mode, act, buf, width, ks, first=None, end=False, half=None, ready=None):
                ah, al = act
                if first is not None and half != 1:
                    pe.wait_ge(S("evacuated"), first)
                if half != 1:
                    pe.wait_ge(S("lo_ready"), n * UNITS + (u + 1 + UNITS))
                if ready is not None and half != 1:
                    pe.wait_ge(S("hid_ready"), ready)
                slot = u % RING
                halves = (0, 1) if half is None else (half,)
                for j in range(width // P if mode == "B" else TT):
                    for kk in halves:
                        k = ks[kk]
                        c = slice(j * P, (j + 1) * P)
                        if mode == "B":
                            o = pp[buf][:, j * T:(j + 1) * T]
                            pairs = [(wh[:, slot, kk, c], ah[:, k, :]), (wh[:, slot, kk, c], al[:, k, :]),
                                     (wl[:, slot, kk, c], ah[:, k, :])]
                            opens = first is not None and kk == 0 and j % 2 == 0
                        else:
                            o = pp[buf][:, j * WIDE:(j + 1) * WIDE]
                            pairs = [(ah[:, k, c], wh[:, slot, kk, :]), (ah[:, k, c], wl[:, slot, kk, :]),
                                     (al[:, k, c], wh[:, slot, kk, :])]
                            opens = first is not None and kk == 0
                        for m, (lhs, rhs) in enumerate(pairs):
                            last = mm(o, lhs, rhs, start=opens and m == 0, stop=end and kk == 1 and m == 2,
                                      skip_group_check=True)
                if half != 0:
                    last.then_inc(S("unit_used"), 1)

            def blocks(n, b, mode, act, bufs, width, per=UNITS, u0=0, k0=0, lag=2):
                def one(u, half=None):
                    j, q = divmod(u - u0, per)
                    unit(n, u, mode, act, bufs[j], width, (k0 + 2 * q, k0 + 2 * q + 1),
                         first=b + (j + 3 - (lag if j == 0 else 2)) if q == 0 else None, end=q == per - 1, half=half)
                return one

            def drive(one, units, u0=0, mixer=None, hops=()):
                if mixer is None:
                    for u in range(units):
                        one(u0 + u)
                    return
                for y in range(len(hops)):
                    next(mixer)
                    for h in range(2 * units):
                        if hop_of(h, 2 * units, hops) == y:
                            one(u0 + h // 2, h % 2)
                assert next(mixer, "over") == "over"

            A, H = (aTh, aTl), (hTh, hTl)

            def new_x(k):
                def turn(r):
                    c, t = divmod(r, TT)
                    if k:
                        pe.wait_ge(S("x_ready"), 8 * (k - 1) + r + 1)
                    elif t == 0:
                        pe.wait_ge(S(f"x_in{c}"), 16)
                    if 8 * k + r >= 4:
                        pe.wait_ge(S("xlo"), 8 * k + r - 3)
                    for e in range(4):
                        last = nc.tensor.transpose(mb[r % 4][:, e * P:(e + 1) * P],
                                                   xres[:, t, (4 * c + e) * P:(4 * c + e + 1) * P], ident)
                    last.then_inc(S("xT" if r < 7 else "x_transposed"), 1)

                for y, tiles in enumerate((range(0, 4), range(4, 6), range(6, 8), ())):
                    for r in tiles:
                        turn(r)
                    pe.wait_ge(S("xlo"), 8 * k + 2 * y + 2)
                    yield

            pe.sem_inc(S("unit_used"), RING)
            pe.sem_inc(S("evacuated"), 2)
            pe.sem_inc(S("lora_used"), 1)
            pe.sem_inc(S("rw_o"), 1)
            pe.sem_inc(S("hid_ready"), 1)
            pe.wait_ge(S("ident_in"), 16)
            drive(blocks(0, 0, "B", A, (1,), NARROW), UNITS, 0, new_x(0), HOPS_X)

            def mix0(m):
                m1 = m + 1
                yield
                pe.wait_ge(S("lora_in"), 16 * m1)
                pe.wait_ge(S("rw_o"), m1)
                pe.wait_ge(S("lo_acts"), 1)
                mm(mb[0][:, 0:T], lw[0:64, 0, :], loT[0:64, 0, :], start=True, stop=True)
                mm(mb[1][:, 0:T], lw[64:P, 0, :], loT[64:P, 0, :], start=True, stop=True)
                mm(mb[0][:, T:2 * T], lw[:, 1, :], loT[:, 1, :], start=True, stop=False, skip_group_check=True)
                mm(mb[0][:, T:2 * T], lw[0:32, 2, :], loT[0:32, 2, :], start=False, stop=True,
                   skip_group_check=True).then_inc(S("lora_used"), 1)
                pe.wait_ge(S("evacuated"), 2 * m + (2 + P_GROUPS0 + 2))
                nc.tensor.transpose(mb[1][:, T:T + P], sbq[:, 2, 0:P], ident)
                nc.tensor.transpose(mb[1][:, T + P:2 * T], sbq[:, 2, P:T], ident)
                mm(mb[3][:, 0:T], sbq[:, 1, 0:P], sbq[:, 0, :], start=True, stop=True, skip_group_check=True)
                mm(mb[3][:, T:T + P], sbq[:, 1, P:T], sbq[:, 0, P:T], start=True, stop=True,
                   skip_group_check=True).then_inc(S("scores"), 1)
                yield
                pe.wait_ge(S("ksq"), m1)
                pe.wait_ge(S("vtk"), m1)
                mm(mb[1][:, 0:T], bo, ksq, start=True, stop=True, skip_group_check=True).then_inc(S("kss"), 1)
                yield
                pe.wait_ge(S("lkeep"), m1)
                mm(mb[2][:, 0:384], tri, sbb, start=True, stop=False, skip_group_check=True)
                mm(mb[2][:, P:T], ones, sbb[:, T:384], start=False, stop=True, skip_group_check=True).then_inc(S("lcum"), 1)
                yield
                pe.wait_ge(S("attn"), m1)
                mm(mb[3][:, 0:T], vtk[:, 0, :], sba[:, 0:T], start=True, stop=False, skip_group_check=True)
                mm(mb[3][:, P:T], vtk[:, 1, :], sba[:, T:384], start=False, stop=True,
                   skip_group_check=True).then_inc(S("sb_o"), 1)
                yield
                pe.wait_ge(S("operands"), m1)
                for t in range(TT):
                    for h in range(2):
                        hr = slice(64 * h, 64 * h + 64)
                        for w, src in enumerate((bt, kt_)):
                            if t == 1 and h == 0 and w == 0:
                                pe.wait_ge(S("sb_lo"), m1)
                            last = mm(mb[2 * t + h][:, w * T:(w + 1) * T], src[hr, t * P:(t + 1) * P],
                                      KR[hr, t, :, :], start=w == 0, stop=True, skip_group_check=True)
                    last.then_inc(S("gram"), 1)
                yield
                pe.wait_ge(S("masked"), 2 * m + 1)
                for w, src in enumerate((bt, kt_, rkv[:, 2, :], None)):
                    for t in range(TT):
                        e = 2 * w + t
                        src_t = KR[:, t, 0, :] if src is None else src[:, t * P:(t + 1) * P]
                        last = nc.tensor.transpose(mb[e // 4][:, (e % 4) * P:(e % 4 + 1) * P], src_t, ident)
                last.then_inc(S("tokT"), 1)
                yield
                pe.wait_ge(S("XT_first"), m1)
                for p in range(4):
                    last = nc.tensor.transpose(mb[2][:, p * P:(p + 1) * P], XT0[:, p, :], ident)
                last.then_inc(S("Xnew"), 1)
                pe.wait_ge(S("tok_ready"), m1)
                for p in range(4):
                    last = mm(mb[1][:, p * 64:(p + 1) * 64], GM[:, p // 2, p % 2, 1, 0, :],
                              tok[:, 2, p // 2, 64 * (p % 2):64 * (p % 2) + 64], start=p == 0, stop=True,
                              skip_group_check=True)
                last.then_inc(S("AV"), 1)
                yield

                def a_times_x(lv):
                    s = 1 << lv
                    for p in range(4):
                        Xp = X0[:, p, :].rearrange("p (b w s) -> p b w s", w=2, s=s)
                        last = mm(mb[3][:, p * 64:(p + 1) * 64], GM[:, p // 2, p % 2, 0, 0, :], Xp[:, :, 0, :],
                                  start=p == 0, stop=True, skip_group_check=True)
                    last.then_inc(S("AX"), 1)

                pe.wait_ge(S("X_ready"), 6 * m + 1)
                a_times_x(1)
                yield
                for lv in range(1, 6):
                    pe.wait_ge(S("Yn"), 5 * m + lv)
                    if lv > 1:
                        pe.wait_ge(S("XT_ready"), 5 * m + lv - 1)
                    for p in range(4):
                        last = mm(mb[2][:, p * 64:(p + 1) * 64], XT0[:, p, :], Yn0[:, p, :], start=p == 0, stop=True,
                                  skip_group_check=True)
                    last.then_inc(S("dX"), 1)
                    yield
                    pe.wait_ge(S("X_ready"), 6 * m + lv + 1)
                    for p in range(4):
                        last = nc.tensor.transpose(mb[0][:, p * P:(p + 1) * P], X0[:, p, :], ident)
                    last.then_inc(S("Xnew"), 1)
                    if lv < 5:
                        a_times_x(lv + 1)
                    yield
                pe.wait_ge(S("XT_ready"), 5 * m1)
                pe.wait_ge(S("AVs"), m1)
                for p in range(4):
                    last = mm(mb[1][:, p * 64:(p + 1) * 64], XT0[:, p, :], AVs[:, p * 64:(p + 1) * 64], start=p == 0,
                              stop=True, skip_group_check=True)
                last.then_inc(S("XAV"), 1)
                for p in range(4):
                    t, h = divmod(p, 2)
                    last = mm(mb[2][64 * h:64 * h + 64, t * P:(t + 1) * P], tok[:, 3, t, 64 * h:64 * h + 64], XT0[:, p, :],
                              start=t == 0, stop=True, skip_group_check=True)
                last.then_inc(S("WT"), 1)
                yield
                for c in range(4):
                    t, hf = divmod(c, 2)
                    R = slice(64 * hf, 64 * hf + 64)
                    st_in, yc_ = (Sb, Sa)[c % 2], slice(64 * c, 64 * c + 64)
                    if c:
                        pe.wait_ge(S("state0"), 3 * m + c)
                        mm(mb[0][R, 0:P], KR[:, t, 0, R], st_in, start=True, stop=True,
                           skip_group_check=True).then_inc(S("u_psum"), 1)
                        yield
                    if c == 0:
                        pe.wait_ge(S("WT_ready"), m1)
                    pe.wait_ge(S("U"), 4 * m + c + 1)
                    if c < 3:
                        mm(mb[3][:, 0:P], tok[R, 0, t, :], U[R, :], start=True, stop=False, skip_group_check=True)
                        mm(mb[3][:, 0:P], tok[R, 1, t, :], tok[R, 2, t, :], start=False, stop=True,
                           skip_group_check=True).then_inc(S("dS"), 1)
                    if c:
                        mm(mb[2][:, yc_], st_in, KR[:, t, 1, R], start=True, stop=False, skip_group_check=True)
                    for h in range(2):
                        hs = slice(64 * h, 64 * h + 64)
                        mm(mb[2][hs, yc_], U[R, hs], GM[R, t, h, 0, 1, R], start=c == 0, stop=False, skip_group_check=True)
                        last = mm(mb[2][hs, yc_], tok[R, 2, t, hs], GM[R, t, h, 1, 1, R], start=False, stop=True,
                                  skip_group_check=True)
                    last.then_inc(S("y_psum"), 1)
                    yield
                pe.wait_ge(S("yT"), m1)
                mm(mb[0][:, 0:T], bo64, yT, start=True, stop=True, skip_group_check=True)
                mm(mb[1][:, 0:T], bo, rk, start=True, stop=True, skip_group_check=True).then_inc(S("ymean"), 1)
                yield
                pe.wait_ge(S("ysq"), m1)
                mm(mb[0][:, T:2 * T], bo64, ksq, start=True, stop=True, skip_group_check=True).then_inc(S("yvar"), 1)
                yield

            def group0(i):
                return blocks(i * 2 + P_GROUPS0, i * 2 + P_GROUPS0, "B", A, (0, 1), NARROW)

            pe.wait_ge(S("masks_in"), 16)
            pe.wait_ge(S("c0_in"), 16)
            drive(group0(0), 2 * UNITS)
            with pe.Fori(1, GROUPS - 1) as i:
                drive(group0(i), 2 * UNITS, 0, mix0(i - 1), HOPS0)
            drive(group0(GROUPS - 1), 2 * UNITS, 0, mix0(GROUPS - 2), HOPS0)
            pe.wait_ge(S("mix0_out"), GROUPS - 1)
            drive(blocks(P_OUT0, B_OUT0, "A", H, (0, 1, 0, 1), WIDE, per=7), 28, 0, mix0(GROUPS - 1), HOPS0)
            pe.wait_ge(S("mix0_out"), GROUPS)
            drive(blocks(P_OUT0, B_OUT0 + 4, "A", H, (0, 1, 0, 1), WIDE, per=1, u0=28, k0=14), 4, 28)
            if stop == 1:
                return

            def mlp(n0, b0, k, par):
                def body(f, mixer=None):
                    n, b = f * 8 + n0, f * 8 + b0
                    bufs = tuple((par + j) % 2 for j in range(4))
                    drive(blocks(n, b, "B", A, bufs, WIDE), 4 * UNITS, 0, mixer, HOPS_MLP[:28])
                    for u in range(4 * UNITS):
                        j, q = divmod(u, UNITS)
                        ready = f * 4 + (4 * FG * (k - 1) // 2 + (UK * q + 1) // 4 + 2) if j == 0 and q % 2 == 0 else None
                        unit(n, u + 4 * UNITS, "A", H, bufs[j], WIDE, (2 * q, 2 * q + 1),
                             first=b + (4 + j + 1) if q == 0 else None, end=q == UNITS - 1, ready=ready)

                body(0, then(new_x(k), 24))
                with pe.Fori(1, FG) as f:
                    body(f)

            mlp(P_MLP0, B_MLP0, 1, 0)

            def gates():
                yield
                pe.wait_ge(S("wba_split"), 1)
                for k in range(KT):
                    for t in range(TT):
                        for a, w in ((aTh, wbh), (aTh, wbl), (aTl, wbh)):
                            last = mm(mb[0][:, t * 64:(t + 1) * 64], a[:, k, t * P:(t + 1) * P], w[:, k, :],
                                      start=k == 0 and a is aTh and w is wbh and t == 0, stop=k == KT - 1 and a is aTl,
                                      skip_group_check=True)
                    if k == KT - 1:
                        last.then_inc(S("ba_out"), 1)
                    if k % 2:
                        yield
                pe.wait_ge(S("g_ready"), 1)
                gvf = gv.rearrange("p c h -> p (c h)")
                mm(mb[1][:, 0:64], UT, gvf, start=True, stop=True, skip_group_check=True)
                mm(mb[1][:, 64:128], ones, gvf, start=True, stop=True, skip_group_check=True).then_inc(S("gsum"), 1)
                yield

            def mix1(g):
                g1 = g + 1
                for _ in range(6):
                    yield
                pe.wait_ge(S("qk_act"), g1)
                for w in range(2):
                    for c in range(TT):
                        for j in range(2):
                            last = nc.tensor.transpose(mb[w][:, (2 * c + j) * P:(2 * c + j + 1) * P],
                                                       qkv[:, 2 * w + j, c * P:(c + 1) * P], ident)
                last.then_inc(S("kT"), 1)
                yield
                for c in range(TT):
                    for j in range(2):
                        last = mm(mb[2 + c][:, j * T:(j + 1) * T], qkv[:, 2 + j, c * P:(c + 1) * P],
                                  qkv[:, :, c * P:(c + 1) * P].rearrange("p (w j) t -> p j w t", j=2)[:, j, 0:2, :],
                                  start=j == 0, stop=True, skip_group_check=True)
                last.then_inc(S("kq"), 1)
                yield
                pe.wait_ge(S("ktok"), g1)
                pe.wait_ge(S("utg"), g1)
                for c in range(TT):
                    last = mm(mb[c][:, :], SL, UTg[:, c, :, :], start=True, stop=True, skip_group_check=True)
                last.then_inc(S("dlog"), 1)
                yield
                pe.wait_ge(S("KQm"), g1)
                pe.wait_ge(S("v_act"), g1)
                for c in range(TT):
                    for h in range(4):
                        last = nc.tensor.transpose(mb[2 + c][:, h * P:(h + 1) * P], qkv[:, 4 + h, c * P:(c + 1) * P], ident)
                last.then_inc(S("vT"), 1)
                yield
                pe.wait_ge(S("XT1_first"), g1)
                pe.wait_ge(S("vs"), g1)

                def transpose_x(src):
                    for p in range(8):
                        last = nc.tensor.transpose(mb[2 + p // 4][:, (p % 4) * P:(p % 4 + 1) * P], src[:, p, :], ident)
                    last.then_inc(S("X1new"), 1)

                def a_times_x(lv):
                    for p in range(8):
                        Xp = X1[:, p, :].rearrange("p (b w s) -> p b w s", w=2, s=1 << lv)
                        last = mm(mb[0][:, p * 64:(p + 1) * 64], At[:, p // 4, p % 4, :], Xp[:, :, 0, :],
                                  start=p == 0, stop=True, skip_group_check=True)
                    last.then_inc(S("AX1"), 1)

                transpose_x(XT1)
                yield
                pe.wait_ge(S("X1_ready"), 7 * g + 1)
                a_times_x(1)
                yield
                for lv in range(1, 7):
                    pe.wait_ge(S("Yn1"), 6 * g + lv)
                    if lv > 1:
                        pe.wait_ge(S("XT1_ready"), 6 * g + lv - 1)
                    for p in range(8):
                        last = mm(mb[1][:, p * 64:(p + 1) * 64], XT1[:, p, :], Yn1[:, p, :], start=p == 0, stop=True,
                                  skip_group_check=True)
                    last.then_inc(S("dX1"), 1)
                    yield
                    pe.wait_ge(S("X1_ready"), 7 * g + lv + 1)
                    transpose_x(X1)
                    if lv < 6:
                        a_times_x(lv + 1)
                    yield

                def heads(bank, lhs, rhs, name):
                    for h in range(4):
                        last = mm(bank[:, h * P:(h + 1) * P], lhs[:, h, :], rhs[:, h, :], start=h == 0, stop=True,
                                  skip_group_check=True)
                    last.then_inc(S(name), 1)

                def pairs(bank, lhs, rhs, name):
                    for j in range(2):
                        last = mm(bank[:, j * T:(j + 1) * T], lhs[:, j, :], rhs[:, 2 * j:2 * j + 2, :], start=j == 0,
                                  stop=True, skip_group_check=True)
                    last.then_inc(S(name), 1)

                pe.wait_ge(S("XT1_ready"), 6 * g1)
                heads(mb[0], XT1[:, 0:4, :], vs[:, 0, :, :], "z_psum")
                yield
                pe.wait_ge(S("vke"), g1)
                pairs(mb[3], ktok[:, 0, :, :], vke, "dS1")
                heads(mb[1], AT[:, 0, :, :], vk, "o_psum")
                yield
                pe.wait_ge(S("state1"), g1)
                pairs(mb[0], qkv[:, 2:4, P:T], S1, "kS")
                pairs(mb[2], qkv[:, 0:2, P:T], S1, "qS")
                yield
                pe.wait_ge(S("yp"), g1)
                heads(mb[3], XT1[:, 4:8, :], yp, "z_psum")

                def transpose_o(c, bank):
                    pe.wait_ge(S("on"), 2 * g + c + 1)
                    for h in range(4):
                        last = nc.tensor.transpose(bank[:, h * P:(h + 1) * P], on[:, h, :], ident)
                    last.then_inc(S("oT"), 1)

                pe.wait_ge(S("t1"), g1)
                transpose_o(0, mb[2])
                yield
                pe.wait_ge(S("vk"), 2 * g + 2)
                heads(mb[1], AT[:, 1, :, :], vk, "o_psum")
                yield
                transpose_o(1, mb[0])
                yield

            def group1(n, b):
                return blocks(n, b, "B", A, (0, 1, 0), WIDE, lag=1)

            drive(group1(P_L1, B_L1), 3 * UNITS, 0, then(new_x(2), gates()), HOPS_GATES)
            with pe.Fori(1, 5) as i:
                drive(group1(i * 3 + P_L1, i * 3 + B_L1), 3 * UNITS, 0, mix1(i - 1), HOPS1)
            pe.wait_ge(S("mix1_out"), 8)
            drive(blocks(P_OUT1A, B_OUT1A, "A", H, (1, 0, 1, 0), WIDE), 4 * UNITS, 0, mix1(4), HOPS1)
            drive(group1(P_L1B, B_L1B), 3 * UNITS)
            with pe.Fori(6, 8) as i:
                drive(group1(i * 3 + (P_L1B - 15), i * 3 + (B_L1B - 15)), 3 * UNITS, 0, mix1(i - 1), HOPS1)
            pe.wait_ge(S("mix1_out"), 14)
            drive(blocks(P_OUT1B, B_OUT1B, "A", H, (1, 0, 1, 0), WIDE, per=6), 24, 0, mix1(7), HOPS1)
            pe.wait_ge(S("mix1_out"), 16)
            drive(blocks(P_OUT1B, B_OUT1B + 4, "A", H, (1, 0, 1, 0), WIDE, per=2, u0=24, k0=12), 8, 24)
            mlp(P_MLP1, B_MLP1, 3, 1)

        @block.scalar
        def _(act):
            go = nc.scalar.activation
            st = Steps(act, S("act_steps"))

            def split(n, q, width):
                act.wait_ge(S(f"landed{q}"), n * 16 + 16)
                act.wait_ge(S("unit_used"), n * UNITS + (q + 1))
                nc.scalar.copy(wh[:, q % RING, :, 0:width], raw[:, q, :, 0:width]).then_inc(S("hi_ready"), 1)

            def new_x(k):
                for tiles in (range(0, 4), range(4, 6), range(6, 8), ()):
                    for r in tiles:
                        c, t = divmod(r, TT)
                        if r < 7:
                            act.wait_ge(S("xT"), 7 * k + r + 1)
                        else:
                            act.wait_ge(S("x_transposed"), k + 1)
                        nc.scalar.copy(aTh[:, 4 * c:4 * c + 4, t * P:(t + 1) * P],
                                       r2(mb[r % 4][:, :], a=4)).then_inc(S("xhi"), 1)
                    if k == 0 and tiles == range(0, 4):
                        for q in range(LEAD):
                            split(0, q, NARROW)
                    yield

            def used(n, u):
                act.wait_ge(S("unit_used"), n * UNITS + (u + 1 + RING))

            def layer_norm(k):
                for t in range(TT):
                    act.wait_ge(S("ln_var"), TT * k + t + 1)
                    st(go(rstd[:, t:t + 1], mv[:, t, 1:2], ACT.Ln, bias=eps_ln))
                    st.settle()
                    go(rstd[:, t:t + 1], rstd[:, t:t + 1], ACT.Exp, scale=-0.5).then_inc(S("ln_rstd"), 1)

            for c in range(2, 4):
                act.dma_start(xres[:, :, c * WIDE:(c + 1) * WIDE],
                              x[:, c * WIDE:(c + 1) * WIDE].rearrange("(t p) d -> p t d", p=P)).then_inc(S(f"x_in{c}"), 16)
            nc.scalar.preload_act_table_set("natural_log_exp_and_others")
            act.wait_ge(S("eps_ready"), 1)
            interleave(new_x(0), HOPS_X, UNITS, (lambda u: split(u // UNITS, u % UNITS, NARROW)), (), (lambda j, after: None),
                       True, True)

            def lora_acts():
                used(0, UNITS - 1)
                act.wait_ge(S("zeroed"), 1)
                nc.scalar.copy(lobuf[:, :, 1:T + 1], r2(pp[1][:, 0:3 * T], a=3)).then_inc(S("evacuated"), 1)
                yield
                yield
                act.wait_ge(S("lo_shifted"), 1)
                st(go(loT[0:64, 0, :], loT[0:64, 0, :], ACT.Exp, scale=2.0))
                go(loT[:, 1:3, :], loT[:, 1:3, :], ACT.Exp, scale=-1.0).then_inc(S("lo_exp"), 1)
                yield
                yield
                act.wait_ge(S("lo_bounded"), 1)
                for r, c in ((slice(0, 64), slice(0, 1)), (slice(0, P), slice(1, 3))):
                    st(go(loT[r, c, :], loT[r, c, :], ACT.Ln, bias=1.0))
                st.settle()
                st(go(loT[0:64, 0, :], loT[0:64, 0, :], ACT.Exp, scale=-1.0))
                go(loT[:, 1:3, :], loT[:, 1:3, :], ACT.Exp, scale=-1.0).then_inc(S("lo_sig"), 1)
                for _ in range(12):
                    yield

            def mix0(m):
                m1 = m + 1
                yield
                act.wait_ge(S("scores"), m1)
                st(go(ew[:, 0:T], mb[0][:, 0:T], ACT.Exp, scale=-1.0, bias=nprm[:, bass.ds(m, 1), 0]))
                go(ew[:, T:2 * T], mb[1][:, 0:T], ACT.Exp, scale=-1.0,
                   bias=nprm[:, bass.ds(m, 1), 1]).then_inc(S("gates_exp"), 1)
                nc.scalar.copy(vtk, r2(mb[1][:, T:2 * T], a=TT)).then_inc(S("vtk"), 1)
                st(go(sbb, mb[3][:, 0:384], ACT.Abs))
                act.wait_ge(S("kk0"), m1)
                go(ksq, kk0, ACT.Square).then_inc(S("ksq"), 1)
                st.settle()
                st(go(sbb, sbb, ACT.Exp, scale=-1.0))
                st.settle()
                go(sbb, sbb, ACT.Ln, bias=1.0).then_inc(S("softplus"), 1)
                yield
                act.wait_ge(S("gates_bounded"), m1)
                st(go(ew, ew, ACT.Ln, bias=1.0))
                st.settle()
                go(ew, ew, ACT.Exp, scale=-1.0).then_inc(S("gates0"), 1)
                st(nc.scalar.copy(gg, mb[0][:, T:2 * T]))
                act.wait_ge(S("kss"), m1)
                st(go(ksq, mb[1][:, 0:T], ACT.Ln, bias=eps_kk))
                st.settle()
                go(ksq, ksq, ACT.Exp, scale=-0.5).then_inc(S("rkk"), 1)
                act.wait_ge(S("cum"), m1)
                st(go(pinc, cum, ACT.Exp))
                st(go(pinv, cum, ACT.Exp, scale=-1.0))
                go(pexc, pexc, ACT.Exp).then_inc(S("powers"), 1)
                yield
                act.wait_ge(S("loga"), m1)
                go(sba, sba, ACT.Exp).then_inc(S("attn"), 1)
                yield
                act.wait_ge(S("sb_o"), m1)
                nc.scalar.copy(hTh[:, bass.ds(m * 2, 1), :], mb[3][:, 0:T].unsqueeze(1)).then_inc(S("sb_hi"), 1)
                yield
                yield
                act.wait_ge(S("tokT"), m1)
                st(nc.scalar.copy(tok[:, 0:2, :, :], mb[0][:, :].rearrange("p (w t c) -> p w t c", w=2, t=TT)))
                nc.scalar.copy(tok[:, 2:4, :, :], mb[1][:, :].rearrange("p (w t c) -> p w t c", w=2, t=TT)).then_inc(S("tok_ready"), 1)
                yield
                act.wait_ge(S("Xnew"), 6 * m + 1)
                nc.scalar.copy(X0, r2(mb[2][:, :], a=4)).then_inc(S("X_ready"), 1)
                act.wait_ge(S("AV"), m1)
                nc.scalar.copy(AVs, mb[1][:, 0:T]).then_inc(S("AVs"), 1)
                yield
                yield
                for lv in range(1, 6):
                    yield
                    act.wait_ge(S("Xnew"), 6 * m + lv + 1)
                    nc.scalar.copy(XT0, r2(mb[0][:, :], a=4)).then_inc(S("XT_ready"), 1)
                    yield
                act.wait_ge(S("WT"), m1)
                nc.scalar.copy(KR[:, :, 0, :], r2(mb[2][:, 0:T], a=TT)).then_inc(S("WT_ready"), 1)
                yield
                for c in range(4):
                    if c:
                        act.wait_ge(S("state0"), 3 * m + c)
                        if c < 3:
                            go(pcS, (Sb, Sa)[c % 2], ACT.Copy, scale=pinc[:, 64 * c + 63:64 * c + 64]).then_inc(S("pcS"), 1)
                        yield
                    if c == 3:
                        act.wait_ge(S("y_psum"), 4 * m1)
                        nc.scalar.copy(yT, mb[2][:, 0:T]).then_inc(S("yT"), 1)
                    yield
                act.wait_ge(S("yc"), m1)
                go(ksq, yc, ACT.Square).then_inc(S("ysq"), 1)
                yield
                act.wait_ge(S("yvar"), m1)
                st(go(ksq, mb[0][:, T:2 * T], ACT.Ln, bias=eps_lnx))
                st.settle()
                go(ksq, ksq, ACT.Exp, scale=-0.5).then_inc(S("yrstd"), 1)
                act.wait_ge(S("rw_o"), m1 + 1)
                nc.scalar.copy(hTh[:, bass.ds(m * 2 + 1, 1), :], yn.unsqueeze(1)).then_inc(S("rw_hi"), 1)
                yield

            def group0(i, first=False, last=False):
                n = i * 2 + P_GROUPS0

                def one(u):
                    if last and u >= 2 * UNITS:
                        split(P_OUT0, u - 2 * UNITS, WIDE)
                    else:
                        split(n + u // UNITS, u % UNITS, NARROW)

                def hook(j, after):
                    if after:
                        return
                    used(n, j * UNITS + UNITS - 1)
                    if j == 0:
                        if not first:
                            act.wait_ge(S("shifted"), i)
                        nc.scalar.copy(pb[:, :, 1:T + 1], r2(pp[0][:, 0:3 * T], a=3)).then_inc(S("evacuated"), 1)
                    else:
                        if not first:
                            act.wait_ge(S("scores"), i)
                        st(go(sbq[:, 0, :], pp[1][:, 0:T], ACT.Copy, scale=SB_SCALE))
                        nc.scalar.copy(sbq[:, 1:3, :], r2(pp[1][:, T:3 * T], a=2)).then_inc(S("evacuated"), 1)
                return 2 * UNITS, one, (7, 15), hook, True, True

            def wide(n):
                return lambda u: split(n + u // UNITS, u % UNITS, WIDE)

            def nothing(j, after):
                pass

            interleave(lora_acts(), HOPS_LORA, *group0(0, True))
            st.leave_straight()
            PER = 11
            with act.Fori(1, GROUPS - 1) as i:
                st.enter(i - 1, PER)
                interleave(mix0(i - 1), HOPS0, *group0(i))
            st.leave(GROUPS - 2)
            interleave(mix0(GROUPS - 2), HOPS0, *group0(GROUPS - 1, last=True))
            interleave(mix0(GROUPS - 1), HOPS0, 28, wide(P_OUT0), (), nothing, True, begun=True)
            st.leave_straight()
            interleave(None, (), 4, wide(P_OUT0), (), nothing, stop != 1, begun=True, u0=28)
            layer_norm(0)
            if stop == 1:
                return

            def mlp(n0, b0, k, par):
                def body(f, ahead, mixer=None):
                    n = f * 8 + n0

                    def hook(j, after):
                        if j < 4 and after:
                            used(n, j * UNITS + UNITS - 1)
                            seen = f * 4 + (4 * FG * k + j + 1)
                            act.wait_ge(S("hid_ready"), seen)
                            go(hid, pp[(par + j) % 2][:, :], ACT.Relu).then_inc(S("evacuated"), 1)
                            act.wait_ge(S("evacuated"), f * 8 + (b0 + j + 3))
                            go(hTh[:, 4 * j:4 * j + 4, :], r2(hid, a=4), ACT.Square).then_inc(S("hid_hi"), 1)
                    interleave(mixer, HOPS_MLP, 8 * UNITS, wide(n), [UNITS * j + UNITS - 1 for j in range(8)], hook, ahead,
                               begun=True, wait=2)
                body(0, True, then(new_x(2 * k + 1), 56))
                with act.Fori(1, FG - 1) as f:
                    body(f, True)
                body(FG - 1, k == 0)

            mlp(P_MLP0, B_MLP0, 0, 0)
            layer_norm(1)
            st.leave_straight()

            def gates():
                act.wait_ge(S("wba_in"), 16)
                nc.scalar.copy(wbh, wba_sb).then_inc(S("wba_hi"), 1)
                for _ in range(2):
                    yield
                act.wait_ge(S("zeroed"), 2)
                for _ in range(6):
                    yield
                act.wait_ge(S("ba_out"), 1)
                act.wait_ge(S("c1_in"), 64)
                ba = mb[0][:, 0:128].rearrange("p (c h) -> p c h", c=TT)
                st(go(beta, ba[:, :, 0:32], ACT.Exp, scale=-1.0))
                go(r1[:, 0:32], r1[:, 0:32], ACT.Exp).then_inc(S("beta_exp"), 1)
                act.wait_ge(S("a_dt"), 1)
                st(go(gtmp, gv, ACT.Abs))
                st.settle()
                st(go(gtmp, gtmp, ACT.Exp, scale=-1.0))
                st.settle()
                go(gtmp, gtmp, ACT.Ln, bias=1.0).then_inc(S("g_ln"), 1)
                yield
                act.wait_ge(S("gsum"), 1)
                gc_ps = mb[1][:, 0:64].rearrange("p (c h) -> p c h", c=TT)
                gl_ps = mb[1][:, 64:128].rearrange("p (c h) -> p c h", c=TT)
                st(go(egc, gc_ps, ACT.Exp))
                go(egl, gl_ps, ACT.Exp).then_inc(S("gsum_read"), 1)
                act.wait_ge(S("kend_log"), 1)
                go(kend, kend, ACT.Exp).then_inc(S("gates1"), 1)
                yield

            def mix1(g, gl, free=None):
                g1 = g + 1
                head = lambda a, c, h: a[:, c, bass.ds(g * 4 + h, 1)]

                def conv_first(js):
                    for j in js:
                        last = go(qkv[:, j, :], cbuf[:, j, 3:T + 3], ACT.Copy, scale=cw[:, bass.ds(g, 1), 4 * j + 3])
                        if j != js[-1]:
                            st(last)
                    last.then_inc(S("conv_first"), 1)

                def sigmoid(e, name):
                    act.wait_ge(S("bounded"), 3 * g + ("qk", "v").index(name) + 1)
                    st(go(e, e, ACT.Exp, scale=-1.0))
                    st.settle()
                    st(go(e, e, ACT.Ln, bias=1.0))
                    st.settle()
                    go(e, e, ACT.Exp, scale=-1.0).then_inc(S("sig_" + name), 1)

                def scaled(dst, bank, scale, name):
                    for h in range(4):
                        last = go(dst[:, h, :], bank[:, h * P:(h + 1) * P], ACT.Copy, scale=scale(h))
                        if h < 3:
                            st(last)
                    last.then_inc(S(name), 1)

                def mean_square(c):
                    for h in range(4):
                        go(sqj, os[c][:, h, :], ACT.Square, accum_out=oss[:, h:h + 1]).then_inc(S("oss"), 1)
                        act.wait_ge(S("oss"), 8 * g + (4 * c + h + 1))
                    st(go(osq, oss, ACT.Ln, scale=1.0 / P, bias=eps_l2))
                    st.settle()
                    go(osq, osq, ACT.Exp, scale=-0.5).then_inc(S("o_rstd"), 1)

                def out_high(c):
                    act.wait_ge(S("oTf"), 2 * g + c + 1)
                    if free is not None and c == 0:
                        used(P_OUT1A, free)
                    nc.scalar.copy(hTh[:, bass.ds(gl * 4, 4), c * P:(c + 1) * P], oT1).then_inc(S("mix1_hi"), 1)

                yield
                conv_first(range(0, 4))
                yield
                conv_first(range(4, 8))
                yield
                sigmoid(E1[:, 0:4, :], "qk")
                yield
                yield
                yield
                act.wait_ge(S("kT"), g1)
                for c in range(TT):
                    for j in range(4):
                        e = 4 * c + j
                        st(go(Ef[:, e * P:(e + 1) * P], mb[j // 2][:, (2 * c + j % 2) * P:(2 * c + j % 2 + 1) * P], ACT.Square,
                              accum_out=ssc[:, c, j:j + 1]))
                nc.scalar.copy(ktok, mb[1][:, :].rearrange("p (c j t) -> p c j t", c=TT, j=2)).then_inc(S("ktok"), 1)
                st.settle()
                st(go(lnss, ssc, ACT.Ln, bias=eps_l2))
                st.settle()
                st(go(qsc, lnss[:, :, 0:2], ACT.Exp, scale=-0.5, bias=ln_qs))
                st(go(skc, lnss[:, :, 2:4], ACT.Exp, scale=0.5))
                go(wkc, lnss[:, :, 2:4], ACT.Exp, scale=-1.0).then_inc(S("cols"), 1)
                yield
                sigmoid(E1[:, 4:8, :], "v")
                yield
                act.wait_ge(S("dlog"), g1)
                for c in range(TT):
                    last = go(Dm[:, c, :, :], r2(mb[c][:, :], a=4), ACT.Exp)
                    if c == 0:
                        st(last)
                last.then_inc(S("D"), 1)
                yield
                act.wait_ge(S("vT"), g1)
                act.wait_ge(S("cols"), g1)
                for c in range(TT):
                    for j in range(2):
                        last = go(vs[:, c, 2 * j:2 * j + 2, :], r2(mb[2 + c][:, j * T:(j + 1) * T], a=2), ACT.Copy,
                                  scale=skc[:, c, j:j + 1])
                        if c + j < 2:
                            st(last)
                last.then_inc(S("vs"), 1)
                yield

                def take_x(lv):
                    act.wait_ge(S("X1new"), 7 * g + lv + 1)
                    dst = XT1 if lv else X1
                    st(nc.scalar.copy(dst[:, 0:4, :], r2(mb[2][:, :], a=4)))
                    nc.scalar.copy(dst[:, 4:8, :], r2(mb[3][:, :], a=4)).then_inc(S("XT1_ready" if lv else "X1_ready"), 1)

                take_x(0)
                yield
                yield
                for lv in range(1, 7):
                    yield
                    take_x(lv)
                    if lv == 2:
                        act.wait_ge(S("bounded"), 3 * g + 3)
                        st(go(SQ, SQ, ACT.Exp, scale=-1.0))
                    elif lv == 3:
                        st.settle()
                        st(go(SQ, SQ, ACT.Ln, bias=1.0))
                    elif lv == 4:
                        st.settle()
                        go(SQ, SQ, ACT.Exp, scale=-1.0).then_inc(S("sig_z"), 1)
                    yield
                act.wait_ge(S("zs_ready"), g1)
                act.wait_ge(S("z_psum"), 2 * g + 1)
                scaled(vk, mb[0], lambda h: wc[:, 0, h:h + 1], "vk")
                yield
                act.wait_ge(S("o_psum"), 2 * g + 1)
                scaled(os[0], mb[1], lambda h: qsc[:, 0, h // 2:h // 2 + 1], "o0_read")
                act.wait_ge(S("o0_read"), g1)
                st.settle()
                mean_square(0)
                yield
                act.wait_ge(S("qS"), g1)
                scaled(os[1], mb[2], lambda h: egq[:, h:h + 1], "t1")
                yield
                act.wait_ge(S("z_psum"), 2 * g + 2)
                scaled(vk, mb[3], lambda h: wc[:, 1, h:h + 1], "vk")
                out_high(0)
                yield
                act.wait_ge(S("o_sum"), g1)
                mean_square(1)
                yield
                out_high(1)
                yield

            def group1(n, before=None):
                def hook(j, after):
                    if after or j == 2:
                        return
                    used(n, j * UNITS + UNITS - 1)
                    if before is not None:
                        act.wait_ge(S("conv"), before * 2)
                    nc.scalar.copy(cbuf[:, 4 * j:4 * j + 4, 3:T + 3], r2(pp[j][:, :], a=4)).then_inc(S("evacuated"), 1)

                def z_out():
                    used(n, 3 * UNITS - 1)
                    nc.scalar.copy(zs, r2(pp[0][:, :], a=4)).then_inc(S("evacuated"), 1)
                return 3 * UNITS, wide(n), (7, 15, 23), hook, True, True, z_out

            PER1 = 48
            interleave(then(new_x(2), gates()), HOPS_GATES, *group1(P_L1))
            st.leave_straight()
            with act.Fori(1, 5) as i:
                st.enter(i - 1, PER1)
                interleave(mix1(i - 1, i - 1), HOPS1, *group1(i * 3 + P_L1, i))
            st.leave(4)
            st.enter(0, PER1)
            interleave(mix1(4, 0, free=26), HOPS1, 4 * UNITS, wide(P_OUT1A), (), nothing, True, begun=True)
            st.leave(1)
            interleave(None, (), *group1(P_L1B))
            with act.Fori(6, 8) as i:
                st.enter(i - 6, PER1)
                interleave(mix1(i - 1, i - 5), HOPS1, *group1(i * 3 + (P_L1B - 15), i))
            st.leave(2)
            st.enter(0, PER1)
            interleave(mix1(7, 3), HOPS1, 24, wide(P_OUT1B), (), nothing, True, begun=True)
            st.leave(1)
            interleave(None, (), 8, wide(P_OUT1B), (), nothing, True, begun=True, u0=24)
            layer_norm(2)
            mlp(P_MLP1, B_MLP1, 1, 1)
            layer_norm(3)

        @block.vector
        def _(dve):
            tt, ts, stt = nc.vector.tensor_tensor, nc.vector.tensor_scalar, nc.vector.scalar_tensor_tensor
            st = Steps(dve, S("dve_steps"))

            def f(ap):
                return ap.bitcast(F32)

            def rep(ap, n):
                return ap.unsqueeze(1).to_broadcast([P, n, ap.shape[-1]])

            def split(n, q, width):
                dve.wait_ge(S("hi_ready"), n * UNITS + (q + 1))
                tt(wl[:, q % RING, :, 0:width], raw[:, q, :, 0:width], f(wh[:, q % RING, :, 0:width]),
                   ALU.subtract).then_inc(S("lo_ready"), 1)

            def new_x(k):
                def norm(r):
                    if k:
                        ln_tile(k - 1, r)

                def low(r):
                    c, t = divmod(r, TT)
                    dve.wait_ge(S("xhi"), 8 * k + r + 1)
                    ks, ts_ = slice(4 * c, 4 * c + 4), slice(t * P, (t + 1) * P)
                    tt(aTl[:, ks, ts_], r2(mb[r % 4][:, :], a=4), f(aTh[:, ks, ts_]), ALU.subtract).then_inc(S("xlo"), 1)

                norm(0)
                norm(1)
                for r in range(4):
                    norm(r + 2)
                    low(r)
                if k == 0:
                    for q in range(LEAD):
                        split(0, q, NARROW)
                yield
                for r in range(4, 6):
                    norm(r + 2)
                    low(r)
                if k in (1, 3):
                    dve.wait_ge(S("x_ready"), 8 * k)
                    dve.sem_inc(S("ws_free"), 1)
                yield
                low(6)
                low(7)
                yield
                yield

            def used(n, u):
                dve.wait_ge(S("unit_used"), n * UNITS + (u + 1 + RING))

            def add_residual(b, j, buf, stat):
                dve.wait_ge(S("evacuated"), b + 2)
                o = xres[:, :, j * WIDE:(j + 1) * WIDE]
                tt(o, o, r2(pp[buf][:, :], a=TT), ALU.add).then_inc(S("evacuated"), 1)
                if stat:
                    dve.wait_ge(S("evacuated"), b + 3)
                    for t in range(TT):
                        st(nc.vector.bn_stats(stats[:, t, j, :], xres[:, t, j * WIDE:(j + 1) * WIDE]))

            def sigmoid_tail(ap):
                st(ts(ap, ap, 1e30, 1.0, ALU.min, ALU.add))
                st.settle()
                st(nc.vector.reciprocal(ap, ap))
                st.settle()

            def layer_norm(k):
                st.settle()
                for t in range(TT):
                    nc.vector.bn_aggr(mv[:, t, :], stats[:, t, :, :].rearrange("p c s -> p (c s)")).then_inc(S("ln_var"), 1)
                dve.wait_ge(S("ln_in"), 32 * (k + 1))
                dve.wait_ge(S("ln_var"), TT * (k + 1))

            def ln_tile(k, r):
                c, t = divmod(r, TT)
                cols = slice(c * WIDE, (c + 1) * WIDE)
                o = xres[:, t, cols]
                st(stt(o, o, mv[:, t, 0:1], lng[:, cols], ALU.subtract, ALU.mult))
                st.settle()
                if c == 0:
                    dve.wait_ge(S("ln_rstd"), TT * k + t + 1)
                stt(o, o, rstd[:, t:t + 1], lnb[:, cols], ALU.mult, ALU.add).then_inc(S("x_ready"), 1)

            dve.sem_inc(S("lo_ready"), UNITS)
            for ap, v in ((eps_ln, LN_EPS), (eps_lnx, LNX_EPS), (eps_kk, KK_EPS), (eps_l2, 1e-6)):
                st(nc.vector.memset(ap, v))
            nc.vector.memset(ln_qs, -3.5 * 0.6931471805599453).then_inc(S("eps_ready"), 1)
            st(nc.vector.memset(pb[:, :, 0:1], 0.0))
            nc.vector.memset(lobuf[:, :, 0:1], 0.0).then_inc(S("zeroed"), 1)
            interleave(new_x(0), HOPS_X, UNITS, (lambda u: split(u // UNITS, u % UNITS, NARROW)), (), (lambda j, after: None),
                       True, True)

            def lora_acts():
                dve.wait_ge(S("prm_in"), 16)
                st(ts(nprm, prm[:, :, 3:5], -1.0, None, ALU.mult))
                yield
                dve.wait_ge(S("evacuated"), 3)
                st(tt(dsh, lobuf[:, :, 0:T], lobuf[:, :, 1:T + 1], ALU.subtract))
                st.settle()
                for j in range(3):
                    last = stt(loT[:, j, :], dsh[:, j, :], mulo[:, j:j + 1], lobuf[:, j, 1:T + 1], ALU.mult, ALU.add)
                    if j < 2:
                        st(last)
                last.then_inc(S("lo_shifted"), 1)
                yield
                yield
                dve.wait_ge(S("lo_exp"), 1)
                st(ts(loT[0:64, 0, :], loT[0:64, 0, :], 1e18, None, ALU.min))
                ts(loT[:, 1:3, :], loT[:, 1:3, :], 1e18, None, ALU.min).then_inc(S("lo_bounded"), 1)
                yield
                yield
                dve.wait_ge(S("lo_sig"), 1)
                ts(loT[0:64, 0, :], loT[0:64, 0, :], -2.0, 1.0, ALU.mult, ALU.add).then_inc(S("lo_acts"), 1)
                for _ in range(11):
                    yield

            dve.wait_ge(S("c0_in"), 16)

            def mix0(m):
                m1 = m + 1
                par = lambda j: prm[:, bass.ds(m, 1), j]
                dve.wait_ge(S("evacuated"), 2 * m + (P_GROUPS0 + 3))
                st(tt(dsh, pb[:, :, 0:T], pb[:, :, 1:T + 1], ALU.subtract))
                st.settle()
                for j in range(3):
                    last = stt(rkv[:, j, :], dsh[:, j, :], par(j), pb[:, j, 1:T + 1], ALU.mult, ALU.add)
                    if j < 2:
                        st(last)
                last.then_inc(S("shifted"), 1)
                dve.wait_ge(S("shifted"), m1)
                ts(kk0, rkv[:, 1, :], par(5), None, ALU.mult).then_inc(S("kk0"), 1)
                yield
                dve.wait_ge(S("gates_exp"), m1)
                ts(ew, ew, 1e18, None, ALU.min).then_inc(S("gates_bounded"), 1)
                dve.wait_ge(S("softplus"), m1)
                st(stt(sbb, mb[3][:, 0:384], 0.0, sbb, ALU.max, ALU.add))
                st.settle()
                tt(sbb, sbb, sbneg, ALU.mult).then_inc(S("lkeep"), 1)
                st(tt(sbc, mb[3][:, 0:384], sbbig, ALU.add))
                yield
                dve.wait_ge(S("gates0"), m1)
                st(ts(Lg, sigw, -0.6065306597126334, None, ALU.mult))
                st.settle()
                st(nc.vector.tensor_tensor_scan(cum, rst, Lg, 0.0, ALU.mult, ALU.add))
                st.settle()
                tt(pexc, cum, Lg, ALU.subtract).then_inc(S("cum"), 1)
                st(ts(k2, av, 1.0, par(6), ALU.subtract, ALU.mult))
                st.settle()
                st(stt(k2, k2, 1.0, rkv[:, 1, :], ALU.add, ALU.mult))
                dve.wait_ge(S("rkk"), m1)
                st(tt(kkt, kk0, ksq, ALU.mult))
                st.settle()
                st(stt(rk, rkv[:, 0, :], par(7), k2, ALU.mult, ALU.mult))
                st(tt(bt, kkt, av, ALU.mult))
                dve.wait_ge(S("powers"), m1)
                st(tt(KR[:, :, 1, :], r2(rkv[:, 0, :], a=TT), r2(pinc, a=TT), ALU.mult))
                st(tt(KR[:, :, 0, :], r2(kkt, a=TT), r2(pexc, a=TT), ALU.mult))
                st(tt(kt_, k2, pinv, ALU.mult))
                st.settle()
                tt(bt, bt, pinv, ALU.mult).then_inc(S("operands"), 1)
                yield
                dve.wait_ge(S("lcum"), m1)
                tt(sba, sbc, mb[2][:, 0:384], ALU.add).then_inc(S("loga"), 1)
                yield
                dve.wait_ge(S("sb_hi"), m1)
                tt(hTl[:, bass.ds(m * 2, 1), :], mb[3][:, 0:T].unsqueeze(1), f(hTh[:, bass.ds(m * 2, 1), :]),
                   ALU.subtract).then_inc(S("sb_lo"), 1)
                yield
                for t in range(TT):
                    dve.wait_ge(S("gram"), 2 * m + t + 1)
                    for h in range(2):
                        last = tt(GM[:, t, h, :, :, :].rearrange("p w r c -> p w (r c)"), r2(mb[2 * t + h][:, :], a=2),
                                  rep(rwmask, 2), ALU.mult)
                        if h == 0:
                            st(last)
                    last.then_inc(S("masked"), 1)
                dve.wait_ge(S("masked"), 2 * m1)
                st(tt(XT0, GM.rearrange("p t h w r c -> p (t h) w r c")[:, :, 0, 0, :], rep(cc[:, C_M0:C_M0 + P], 4), ALU.mult))
                st.settle()
                tt(XT0, XT0, rep(ident, 4), ALU.add).then_inc(S("XT_first"), 1)
                yield
                yield
                yield
                for lv in range(1, 6):
                    s_ = 1 << lv
                    dve.wait_ge(S("AX"), 5 * m + lv)
                    tt(Yn0, r2(mb[3][:, 0:256], a=4), rep(cc[:, C_LV + 64 * (lv - 1):C_LV + 64 * lv], 4),
                       ALU.mult).then_inc(S("Yn"), 1)
                    yield
                    dve.wait_ge(S("dX"), 5 * m + lv)
                    left = X0.rearrange("p a (b w s) -> p a b w s", w=2, s=s_)[:, :, :, 0, :]
                    tt(left, left, mb[2][:, 0:256].rearrange("p (a b s) -> p a b s", a=4, s=s_), ALU.add).then_inc(S("X_ready"), 1)
                    yield
                yield
                dve.wait_ge(S("XAV"), m1)
                st(ts(U[0:64, :], mb[1][0:64, 0:P], -1.0, None, ALU.mult))
                ts(Un, mb[1][:, 0:T], -1.0, None, ALU.mult).then_inc(S("U"), 1)
                dve.wait_ge(S("U"), 4 * m + 1)
                yield
                for c in range(4):
                    t, hf = divmod(c, 2)
                    R = slice(64 * hf, 64 * hf + 64)
                    if c:
                        dve.wait_ge(S("u_psum"), 3 * m + c)
                        tt(U[R, :], Un[R, t * P:(t + 1) * P], mb[0][R, 0:P], ALU.subtract).then_inc(S("U"), 1)
                        yield
                    if c < 3:
                        new = (Sa, Sb)[c % 2]
                        pend = pinc[:, 64 * c + 63:64 * c + 64]
                        dve.wait_ge(S("dS"), 3 * m + c + 1)
                        if c == 0:
                            stt(new, mb[3][:, 0:P], pend, bo, ALU.mult, ALU.mult).then_inc(S("state0"), 1)
                        else:
                            st(stt(dS0, mb[3][:, 0:P], pend, bo, ALU.mult, ALU.mult))
                            st.settle()
                            dve.wait_ge(S("pcS"), 2 * m + c)
                            tt(new, dS0, pcS, ALU.add).then_inc(S("state0"), 1)
                    yield
                dve.wait_ge(S("ymean"), m1)
                tt(yc, yT, mb[0][:, 0:T], ALU.subtract).then_inc(S("yc"), 1)
                yield
                dve.wait_ge(S("yrstd"), m1)
                st(tt(yn, yc, ksq, ALU.mult))
                st.settle()
                st(ts(yn, yn, par(8), par(9), ALU.mult, ALU.add))
                st(tt(yc, mb[1][:, 0:T], rkv[:, 2, :], ALU.mult))
                st.settle()
                st(tt(yn, yn, yc, ALU.add))
                st.settle()
                tt(yn, yn, gg, ALU.mult).then_inc(S("rw_o"), 1)
                dve.wait_ge(S("rw_hi"), m1)
                tt(hTl[:, bass.ds(m * 2 + 1, 1), :], yn.unsqueeze(1), f(hTh[:, bass.ds(m * 2 + 1, 1), :]),
                   ALU.subtract).then_inc(S("mix0_out"), 1)
                dve.wait_ge(S("mix0_out"), m1)
                yield

            def nothing(j, after):
                pass

            def narrow(n, last=False):
                def one(u):
                    if last and u >= 2 * UNITS:
                        split(P_OUT0, u - 2 * UNITS, WIDE)
                    else:
                        split(n + u // UNITS, u % UNITS, NARROW)
                return one

            def wide(n):
                return lambda u: split(n + u // UNITS, u % UNITS, WIDE)

            def out_hook(n, b, bufs, per, u0, stat):
                def hook(j, after):
                    if not after:
                        used(n, u0 + per * j + per - 1)
                        add_residual(b + j, j, bufs[j], stat)
                return [per * j + per - 1 for j in range(4)], hook

            interleave(lora_acts(), HOPS_LORA, 2 * UNITS, narrow(P_GROUPS0), (), nothing, True, True)
            st.leave_straight()
            PER = 25
            with dve.Fori(1, GROUPS - 1) as i:
                st.enter(i - 1, PER)
                interleave(mix0(i - 1), HOPS0, 2 * UNITS, narrow(i * 2 + P_GROUPS0), (), nothing, True, True)
            st.leave(GROUPS - 2)
            interleave(mix0(GROUPS - 2), HOPS0, 2 * UNITS, narrow(2 * GROUPS - 1, True), (), nothing, True, True)
            dve.wait_ge(S("x_scaled"), 1)
            interleave(mix0(GROUPS - 1), HOPS0, 28, wide(P_OUT0), *out_hook(P_OUT0, B_OUT0, (0, 1, 0, 1), 7, 0, False), True,
                       begun=True)
            dve.sem_inc(S("ws_free"), 1)
            st.leave_straight()
            interleave(None, (), 4, wide(P_OUT0), *out_hook(P_OUT0, B_OUT0 + 4, (0, 1, 0, 1), 1, 28, True), stop != 1,
                       begun=True, u0=28)
            layer_norm(0)
            if stop == 1:
                for r in range(8):
                    ln_tile(0, r)
                return

            def mlp(n0, b0, k, par):
                def body(f_, ahead, last, mixer=None):
                    n = f_ * 8 + n0

                    def hook(j, after):
                        if j < 4 and after:
                            seen = f_ * 4 + (4 * FG * k + j + 1)
                            dve.wait_ge(S("hid_hi"), seen)
                            tt(hid, hid, hid, ALU.mult).then_inc(S("hid_sq"), 1)
                            dve.wait_ge(S("hid_sq"), seen)
                            tt(hTl[:, 4 * j:4 * j + 4, :], r2(hid, a=4), f(hTh[:, 4 * j:4 * j + 4, :]),
                               ALU.subtract).then_inc(S("hid_ready"), 1)
                        elif j >= 4 and not after:
                            if mixer and j == 4:
                                dve.wait_ge(S("x_scaled"), 2 * k + 2)
                            used(n, j * UNITS + UNITS - 1)
                            add_residual(f_ * 8 + (b0 + j), j - 4, (par + j) % 2, last)
                    interleave(mixer, HOPS_MLP, 8 * UNITS, wide(n), [UNITS * j + UNITS - 1 for j in range(8)], hook, ahead,
                               begun=True, wait=2)
                body(0, True, False, then(new_x(2 * k + 1), 56))
                with dve.Fori(1, FG - 1) as f_:
                    body(f_, True, False)
                st.leave_straight()
                body(FG - 1, k == 0, True)

            mlp(P_MLP0, B_MLP0, 0, 0)
            layer_norm(1)
            st.leave_straight()

            def gates():
                nc.vector.memset(cbuf[:, :, 0:3], 0.0).then_inc(S("zeroed"), 1)
                dve.wait_ge(S("wba_hi"), 1)
                tt(wbl, wba_sb, f(wbh), ALU.subtract).then_inc(S("wba_split"), 1)
                for _ in range(8):
                    yield
                dve.wait_ge(S("beta_exp"), 1)
                tt(gv, mb[0][:, 0:128].rearrange("p (c h) -> p c h", c=TT)[:, :, 32:64], rep(r1[:, 32:64], TT),
                   ALU.add).then_inc(S("a_dt"), 1)
                sigmoid_tail(beta)
                dve.wait_ge(S("g_ln"), 1)
                st(stt(gv, gv, 0.0, gtmp, ALU.max, ALU.add))
                st.settle()
                stt(gv, gv, -1.0, rep(r1[:, 0:32], TT), ALU.mult, ALU.mult).then_inc(S("g_ready"), 1)
                yield
                dve.wait_ge(S("gsum_read"), 1)
                st(nc.vector.tensor_copy(gtmp, mb[1][:, 0:64].rearrange("p (c h) -> p c h", c=TT)))
                st.settle()
                tt(kend, mb[1][:, 64:128].rearrange("p (c h) -> p c h", c=TT), gtmp, ALU.subtract).then_inc(S("kend_log"), 1)
                dve.wait_ge(S("gates1"), 1)
                st(ts(negc, egc, -1.0, None, ALU.mult))
                yield

            def mix1(g, b, gl):
                g1 = g + 1
                head = lambda a, c, h: a[:, c, bass.ds(g * 4 + h, 1)]
                heads = lambda a: a[:, :, bass.ds(g * 4, 4)].rearrange("p c (j r) -> p c j r", r=2)
                two = lambda a: a.unsqueeze(3).to_broadcast([P, TT, 2, 2])

                def tap(js, k):
                    for j in js:
                        last = stt(qkv[:, j, :], cbuf[:, j, k:T + k], cw[:, bass.ds(g, 1), 4 * j + k], qkv[:, j, :],
                                   ALU.mult, ALU.add)
                        if j != js[-1] or k < 2:
                            st(last)
                    if k == 2:
                        last.then_inc(S("conv"), 1)
                    else:
                        st.settle()

                def bounded(dst, src):
                    ts(dst, src, -40.0, None, ALU.max).then_inc(S("bounded"), 1)

                def o_scale(c):
                    dve.wait_ge(S("o_rstd"), 2 * g + c + 1)
                    for h in range(4):
                        last = ts(on[:, h, :], os[c][:, h, :], osq[:, h:h + 1], None, ALU.mult)
                        if h < 3:
                            st(last)
                    last.then_inc(S("on"), 1)

                def out_low(c):
                    dve.wait_ge(S("oT"), 2 * g + c + 1)
                    if c == 0:
                        dve.wait_ge(S("zs_ready"), g1)
                    stt(oT1, r2(mb[2 if c == 0 else 0][:, :], a=4), nw, zs[:, :, c * P:(c + 1) * P], ALU.mult,
                        ALU.mult).then_inc(S("oTf"), 1)
                    dve.wait_ge(S("mix1_hi"), 2 * g + c + 1)
                    hs = (slice(None), bass.ds(gl * 4, 4), slice(c * P, (c + 1) * P))
                    tt(hTl[hs], oT1, f(hTh[hs]), ALU.subtract).then_inc(S("mix1_out"), 1)
                    dve.wait_ge(S("mix1_out"), 2 * g + c + 1)

                for c in range(TT):
                    for h in range(4):
                        last = ts(UTg[:, c, h, :], UT, head(gv, c, h), None, ALU.mult)
                        if c * 4 + h < 7:
                            st(last)
                last.then_inc(S("utg"), 1)
                yield
                dve.wait_ge(S("evacuated"), b + 5)
                dve.wait_ge(S("conv_first"), 2 * g + 1)
                tap(range(0, 4), 0)
                yield
                tap(range(0, 4), 1)
                yield
                tap(range(0, 4), 2)
                dve.wait_ge(S("conv"), 2 * g + 1)
                bounded(E1[:, 0:4, :], qkv[:, 0:4, :])
                yield
                dve.wait_ge(S("conv_first"), 2 * g + 2)
                tap(range(4, 8), 0)
                yield
                tap(range(4, 8), 1)
                dve.wait_ge(S("sig_qk"), g1)
                tt(qkv[:, 0:4, :], qkv[:, 0:4, :], E1[:, 0:4, :], ALU.mult).then_inc(S("qk_act"), 1)
                yield
                tap(range(4, 8), 2)
                dve.wait_ge(S("conv"), 2 * g + 2)
                bounded(E1[:, 4:8, :], qkv[:, 4:8, :])
                yield
                yield
                dve.wait_ge(S("kq"), g1)
                for c in range(TT):
                    last = tt(KQ[:, c, :, :, :].rearrange("p j w t -> p j (w t)"), r2(mb[2 + c][:, :], a=2), rep(gmask, 2),
                              ALU.mult)
                    if c == 0:
                        st(last)
                last.then_inc(S("KQm"), 1)
                dve.wait_ge(S("sig_v"), g1)
                tt(qkv[:, 4:8, :], qkv[:, 4:8, :], E1[:, 4:8, :], ALU.mult).then_inc(S("v_act"), 1)
                dve.wait_ge(S("cols"), g1)
                w4 = wc.rearrange("p c (j r) -> p c j r", r=2)
                st(tt(w4, heads(beta), two(wkc), ALU.mult))
                st(tt(egq.rearrange("p (j r) -> p j r", r=2), heads(egc)[:, 1], two(qsc)[:, 1], ALU.mult))
                st.settle()
                st(tt(wke.rearrange("p c (j r) -> p c j r", r=2), w4, heads(kend), ALU.mult))
                dve.wait_ge(S("v_act"), g1)
                yield
                dve.wait_ge(S("KQm"), g1)
                dve.wait_ge(S("D"), g1)
                st.settle()
                for c in range(TT):
                    for h in range(4):
                        st(stt(At[:, c, h, :], Dm[:, c, h, :], wc[:, c, h:h + 1], KQ[:, c, h // 2, 1, :], ALU.mult, ALU.mult))
                st.settle()
                st(tt(XT1, At.rearrange("p c h t -> p (c h) t"), rep(cc[:, C_M0:C_M0 + P], 8), ALU.mult))
                st.settle()
                tt(XT1, XT1, rep(ident, 8), ALU.add).then_inc(S("XT1_first"), 1)
                yield
                for c in range(TT):
                    st(tt(AT[:, c, :, :].rearrange("p (j r) t -> p j r t", r=2), Dm[:, c, :, :].rearrange("p (j r) t -> p j r t", r=2),
                          KQ[:, c, :, 0:1, :].to_broadcast([P, 2, 2, P]), ALU.mult))
                st.settle()
                bounded(SQ, zs)
                yield
                for lv in range(1, 7):
                    s_ = 1 << lv
                    dve.wait_ge(S("AX1"), 6 * g + lv)
                    tt(Yn1, r2(mb[0][:, :], a=8), rep(cc[:, C_LV + 64 * (lv - 1):C_LV + 64 * lv], 8),
                       ALU.mult).then_inc(S("Yn1"), 1)
                    yield
                    dve.wait_ge(S("dX1"), 6 * g + lv)
                    left = X1.rearrange("p a (b w s) -> p a b w s", w=2, s=s_)[:, :, :, 0, :]
                    tt(left, left, mb[1][:, :].rearrange("p (a b s) -> p a b s", a=8, s=s_), ALU.add).then_inc(S("X1_ready"), 1)
                    if lv == 6:
                        dve.wait_ge(S("sig_z"), g1)
                        tt(zs, zs, SQ, ALU.mult).then_inc(S("zs_ready"), 1)
                    yield
                yield

                def take_z(c, bank):
                    dve.wait_ge(S("vk"), 2 * g + c + 1)
                    for h in range(4):
                        last = ts(vke[:, h, :], bank[:, h * P:(h + 1) * P], wke[:, c, h:h + 1], None, ALU.mult)
                        if h < 3:
                            st(last)
                    last.then_inc(S("vke"), 1)

                take_z(0, mb[0])
                yield
                dve.wait_ge(S("dS1"), g1)
                nc.vector.tensor_copy(S1, r2(mb[3][:, :], a=4)).then_inc(S("state1"), 1)
                yield
                dve.wait_ge(S("kS"), g1)
                for h in range(4):
                    last = stt(yp[:, h, :], mb[0][:, h * P:(h + 1) * P], head(negc, 1, h), vs[:, 1, h, :], ALU.mult, ALU.add)
                    if h < 3:
                        st(last)
                last.then_inc(S("yp"), 1)
                o_scale(0)
                yield
                out_low(0)
                yield
                dve.wait_ge(S("o_psum"), 2 * g + 2)
                dve.wait_ge(S("t1"), g1)
                for h in range(4):
                    last = stt(os[1][:, h, :], mb[1][:, h * P:(h + 1) * P], qsc[:, 1, h // 2:h // 2 + 1], os[1][:, h, :],
                               ALU.mult, ALU.add)
                    if h < 3:
                        st(last)
                last.then_inc(S("o_sum"), 1)
                o_scale(1)
                yield
                out_low(1)
                yield

            def group1(n):
                return 3 * UNITS, wide(n), (), nothing, True, True

            PER1 = 59
            interleave(then(new_x(2), gates()), HOPS_GATES, *group1(P_L1))
            st.leave_straight()
            with dve.Fori(1, 5) as i:
                st.enter(i - 1, PER1)
                interleave(mix1(i - 1, i * 3 + (B_L1 - 3), i - 1), HOPS1, *group1(i * 3 + P_L1))
            st.leave(4)
            dve.wait_ge(S("x_scaled"), 3)
            interleave(mix1(4, B_L1 + 12, 0), HOPS1, 4 * UNITS, wide(P_OUT1A),
                       *out_hook(P_OUT1A, B_OUT1A, (1, 0, 1, 0), UNITS, 0, False), True, begun=True)
            st.leave_straight()
            interleave(None, (), *group1(P_L1B))
            with dve.Fori(6, 8) as i:
                st.enter(i - 6, PER1)
                interleave(mix1(i - 1, i * 3 + (B_L1B - 18), i - 5), HOPS1, *group1(i * 3 + (P_L1B - 15)))
            st.leave(2)
            interleave(mix1(7, B_L1B + 6, 3), HOPS1, 24, wide(P_OUT1B),
                       *out_hook(P_OUT1B, B_OUT1B, (1, 0, 1, 0), 6, 0, False), True, begun=True)
            dve.sem_inc(S("ws_free"), 1)
            interleave(None, (), 8, wide(P_OUT1B), *out_hook(P_OUT1B, B_OUT1B + 4, (1, 0, 1, 0), 2, 24, True), True, begun=True, u0=24)
            layer_norm(2)
            mlp(P_MLP1, B_MLP1, 1, 1)
            layer_norm(3)
            for r in range(8):
                ln_tile(3, r)


def constants():
    import numpy as np

    a = np.arange(P)
    s, t = a[:, None], a[None, :]
    cc = np.zeros((P, C_SHARED), np.float32)
    cc[:, C_ID:C_ID + P] = s == t
    cc[:, C_ONES:C_ONES + P] = 1
    for lv in range(1, 7):
        w = 1 << lv
        cols = a.reshape(-1, 2, w)[:, 0, :].reshape(-1)[None, :]
        same = (s // (2 * w) == cols // (2 * w)) & (s // w % 2 == 1)
        cc[:, C_LV + 64 * (lv - 1):C_LV + 64 * lv] = -1.0 * same
    cc[:, C_M0:C_M0 + P] = -1.0 * ((s // 2 == t // 2) & (s < t))
    c0 = np.zeros((P, C0_N), np.float32)
    q = np.arange(T)[None, :]
    keep = np.concatenate([s < q, s < t], axis=1)
    c0[:, C0_SB:C0_SB + 384] = -1.0 * keep
    c0[:, C0_BIG:C0_BIG + 384] = np.where(keep, 0.0, -1e30)
    c0[:, C0_TRI:C0_TRI + P] = s >= t
    block = s // 64 == t // 64
    c0[:, C0_BO:C0_BO + P] = block
    c0[:, C0_BO64:C0_BO64 + P] = block / 64.0
    c0[:, C0_RW:C0_RW + P] = block & (s < t)
    c0[:, C0_RW + P:C0_RW + 2 * P] = block & (s <= t)
    c0[:, C0_RST:C0_RST + T] = q % 64 != 0
    c1 = np.zeros((P, C1_N), np.float32)
    c1[:, C1_GM:C1_GM + P] = s <= t
    c1[:, C1_GM + P:C1_GM + 2 * P] = s < t
    c1[:, C1_SL:C1_SL + P] = s > t
    return cc, c0, c1


def layout(x, ev_w_in, ev_shift, ev_w0, ev_w_up, ev_a0, ev_a_up, ev_g_up, ev_k_k, ev_k_a, ev_r_k, ev_lnx_g, ev_lnx_b,
           vres_w_down, vres_shift, vres_v0, vres_v_up, ev_w_out, od_w_in, od_conv, od_a_log, od_dt_bias, od_norm_w,
           od_w_out, ln1_g, ln1_b, mlp_w1, mlp_w2, ln2_g, ln2_b):
    import numpy as np

    def fill(dst, w):
        dst[:, :, :w.shape[1]] = w.reshape(KT, P, w.shape[1]).transpose(1, 0, 2)

    def unit(w, rows):
        return np.stack([w[r:r + P] for r in rows], axis=1)

    w384 = np.zeros((P_OUT0, P, KT, NARROW), np.float32)
    w = ev_w_in[0]
    fill(w384[0], w[:, 6144:])
    for i in range(GROUPS):
        for b in range(3):
            for n, base in ((1 + 2 * i, 3072), (2 + 2 * i, 0)):
                c = base + 1024 * b + P * i
                fill(w384[n][:, :, b * P:(b + 1) * P], w[:, c:c + P])
    w384 = w384.reshape(P_OUT0, P, UNITS, UK, NARROW).transpose(0, 2, 1, 3, 4).reshape(-1, P, UK, NARROW)
    w512 = np.empty(((PANELS - P_OUT0) * UNITS, P, UK, WIDE), np.float32)
    at = 0

    def put(w, first=0, last=UNITS, rows=lambda q: (2 * P * q, 2 * P * q + P)):
        nonlocal at
        for q in range(first, last):
            w512[at] = unit(w, rows(q))
            at += 1

    def put_mlp(k):
        for f in range(FG):
            for j in range(4):
                put(mlp_w1[k][:, f * D + j * WIDE:f * D + (j + 1) * WIDE])
            for j in range(4):
                put(mlp_w2[k][f * D:(f + 1) * D, j * WIDE:(j + 1) * WIDE])

    def put_group(g):
        w = od_w_in[0]
        put(np.concatenate([w[:, 256 * g:256 * g + 256], w[:, 2048 + 256 * g:2048 + 256 * g + 256]], axis=1))
        put(w[:, 4096 + 512 * g:4096 + 512 * g + 512])
        put(w[:, 8192 + 512 * g:8192 + 512 * g + 512])

    for first, last in ((0, 7), (7, 8)):
        for j in range(4):
            put(ev_w_out[0][:, j * WIDE:(j + 1) * WIDE], first, last, lambda q: (P * q, 1024 + P * q))
    put_mlp(0)
    for g in range(5):
        put_group(g)
    for j in range(4):
        put(od_w_out[0][0:D, j * WIDE:(j + 1) * WIDE])
    for g in range(5, GROUPS):
        put_group(g)
    for first, last in ((0, 6), (6, 8)):
        for j in range(4):
            put(od_w_out[0][D:2 * D, j * WIDE:(j + 1) * WIDE], first, last)
    put_mlp(1)
    assert at == len(w512)
    w = od_w_in[0]
    wba = np.ascontiguousarray(w[:, 12288:].reshape(KT, P, 64).transpose(1, 0, 2))

    prm0 = np.zeros((P, GROUPS * 10 + 3), np.float32)
    vecs = [ev_shift[0][0:1024], ev_shift[0][1024:2048], ev_shift[0][2048:3072], ev_w0[0], ev_a0[0], ev_k_k[0], ev_k_a[0],
            ev_r_k[0].reshape(-1), ev_lnx_g[0], ev_lnx_b[0]]
    for j, v in enumerate(vecs):
        prm0[:, j:GROUPS * 10:10] = v.reshape(GROUPS, P).T
    lo = np.zeros(384, np.float32)
    lo[:288] = ev_shift[0][3072:]
    prm0[:, GROUPS * 10:] = lo.reshape(3, P).T
    lora = np.zeros((GROUPS, P, 3, P), np.float32)
    for m in range(GROUPS):
        c = slice(m * P, (m + 1) * P)
        lora[m, 0:64, 0], lora[m, 64:, 0] = ev_w_up[0][:, c], ev_a_up[0][:, c]
        lora[m, :, 1], lora[m, 0:32, 2] = ev_g_up[0][0:P, c], ev_g_up[0][P:, c]
    conv = np.zeros((P, GROUPS, 8, 4), np.float32)
    for g in range(GROUPS):
        for j in range(8):
            c = (256 * g + P * j, 2048 + 256 * g + P * (j - 2), 4096 + 512 * g + P * (j - 4))[(j >= 2) + (j >= 4)]
            conv[:, g, j] = od_conv[0][:, c:c + P].T
    rows1 = np.concatenate([od_a_log, od_dt_bias], axis=1)
    ln = np.stack([ln1_g[0], ln1_b[0], ln2_g[0], ln2_b[0], ln1_g[1], ln1_b[1], ln2_g[1], ln2_b[1]])
    cc, c0, c1 = constants()
    return {"x": x[0], "w384": w384, "w512": w512, "wba": wba, "consts": cc, "c0": c0, "c1": c1, "prm0": prm0,
            "lora": lora.reshape(GROUPS, P, 3 * P), "conv": conv.reshape(P, GROUPS * 32), "rows1": rows1,
            "normw": np.ascontiguousarray(od_norm_w[0].reshape(P, 1)), "ln": ln}


STOP = 0


def kernel(**inputs):
    import numpy as _np
    import concourse.bacc as _bacc
    from concourse import mybir as _mybir
    from concourse.bass_utils import run_bass_kernel_spmd as _run

    nc = _bacc.Bacc("TRN2", target_bir_lowering=False, num_devices=1)
    laid = layout(**{k: _np.asarray(v) for k, v in inputs.items()})
    arrays, args = {}, {}
    for name, a in laid.items():
        a = _np.ascontiguousarray(a)
        arrays[f"in_{name}_dram"] = a
        args[name] = nc.dram_tensor(f"in_{name}_dram", a.shape, _mybir.dt.from_np(a.dtype), kind="ExternalInput").ap()
    args["out"] = nc.dram_tensor("out_0_dram", (T, D), _mybir.dt.float32, kind="ExternalOutput").ap()
    trunk(nc, STOP, **args)
    r = _run(nc, [arrays], core_ids=[0])
    return r.results[0]["out_0_dram"].reshape(1, T, D)
```
